# Optimizing a Trainium2 kernel written in Bass

```python
import math
import jax, jax.numpy as jnp
from jax import lax
import numpy as np

D_MODEL = 1024
BATCH = 1
SEQ = 256
DEPTH = 1

MEM_LEN = 256
MEM_HEADS = 4
MEM_HEAD_DIM = D_MODEL // MEM_HEADS
A_HEADS = 8
A_HEAD_DIM = 64
A_WIDTH = A_HEADS * A_HEAD_DIM
MOBA_BLOCK = 256
MOBA_TOPK = 3
B_HEADS = 4
B_QK_DIM = 64
B_V_DIM = 2 * B_QK_DIM
B_QK_WIDTH = B_HEADS * 2 * B_QK_DIM
B_WIDTH = B_HEADS * B_V_DIM
MIX_WIDTH = A_WIDTH + B_WIDTH
IN_WIDTH = 3 * A_WIDTH + 2 * B_QK_WIDTH + B_WIDTH
IN_SPLITS = [A_WIDTH, 2 * A_WIDTH, 3 * A_WIDTH, 3 * A_WIDTH + B_QK_WIDTH, 3 * A_WIDTH + 2 * B_QK_WIDTH]
N_ATT_HEADS = A_HEADS + B_HEADS
REL_BUCKETS = 32
REL_MAX_DIST = 128
D_FF = -(-8 * D_MODEL // (3 * 256)) * 256
Q_BLOCK = 128
EPS = 1e-6
NEG_INF = -1e30


def rms_norm(x, g):
    xf = x.astype(jnp.float32)
    y = xf * lax.rsqrt(jnp.mean(xf * xf, axis=-1, keepdims=True) + EPS)
    return (y * g.astype(jnp.float32)).astype(x.dtype)

def rel_bucket(dist):
    n = jnp.maximum(dist, 0)
    max_exact = REL_BUCKETS // 2
    log_ratio = jnp.log(jnp.maximum(n, max_exact).astype(jnp.float32) / max_exact) / math.log(REL_MAX_DIST / max_exact)
    large = max_exact + (log_ratio * (REL_BUCKETS - max_exact)).astype(jnp.int32)
    large = jnp.minimum(large, REL_BUCKETS - 1)
    return jnp.where(n < max_exact, n, large)

def moba_attention(q, k, v, table_a):
    B_, S, H, dh = q.shape
    nb = -(-S // MOBA_BLOCK)
    pad = nb * MOBA_BLOCK - S
    topk = min(MOBA_TOPK, nb)
    n_chunks = S // Q_BLOCK
    scale = dh ** -0.5
    bias_ht = table_a.T.astype(jnp.float32)
    h_i = jnp.arange(H)[:, None, None]
    blk_ids = jnp.arange(nb)
    key_off = jnp.arange(MOBA_BLOCK)

    def per_batch(args):
        q1, k1, v1 = args
        kp = jnp.pad(k1, ((0, pad), (0, 0), (0, 0))).reshape(nb, MOBA_BLOCK, H, dh).transpose(2, 0, 1, 3)
        vp = jnp.pad(v1, ((0, pad), (0, 0), (0, 0))).reshape(nb, MOBA_BLOCK, H, dh).transpose(2, 0, 1, 3)
        kmean = jnp.mean(kp.astype(jnp.float32), axis=2)
        qc = q1.reshape(n_chunks, Q_BLOCK, H, dh).transpose(0, 2, 1, 3)

        def per_chunk(args2):
            qblk, c = args2
            t = c * Q_BLOCK + jnp.arange(Q_BLOCK)
            own = t // MOBA_BLOCK
            gate = jnp.einsum('hqd,hnd->hqn', qblk.astype(jnp.float32), kmean)
            gate = jnp.where(blk_ids[None, None, :] < own[None, :, None], gate, NEG_INF)
            _, sel = lax.top_k(gate, topk)
            idx = jnp.concatenate([sel, jnp.broadcast_to(own[None, :, None], (H, Q_BLOCK, 1))], axis=-1)
            k_sel = kp[h_i, idx]
            v_sel = vp[h_i, idx]
            logits = jnp.einsum('hqd,hqtld->hqtl', qblk, k_sel, preferred_element_type=jnp.float32) * scale
            kpos = idx[..., None] * MOBA_BLOCK + key_off
            dist = t[None, :, None, None] - kpos
            logits = logits + bias_ht[h_i[..., None], rel_bucket(dist)]
            slot_ok = jnp.concatenate([jnp.arange(topk)[None, :] < own[:, None],
                                       jnp.ones((Q_BLOCK, 1), dtype=bool)], axis=1)
            mask = slot_ok[None, :, :, None] & (dist >= 0)
            logits = jnp.where(mask, logits, NEG_INF)
            p = jax.nn.softmax(logits.reshape(H, Q_BLOCK, -1), axis=-1).reshape(logits.shape)
            out = jnp.einsum('hqtl,hqtld->hqd', p.astype(v_sel.dtype), v_sel, preferred_element_type=jnp.float32)
            return out.astype(q.dtype)

        outs = lax.map(per_chunk, (qc, jnp.arange(n_chunks)))
        return outs.transpose(0, 2, 1, 3).reshape(S, H, dh)

    return lax.map(per_batch, (q, k, v))

def diff_attention(q, k, v, table_b, lam, subln_g, lambda_init):
    B_, S, H, _, dq = q.shape
    n_chunks = S // Q_BLOCK
    scale = dq ** -0.5
    kt = k.transpose(0, 2, 3, 1, 4)
    vt = v.transpose(0, 2, 1, 3)
    qc = q.reshape(B_, n_chunks, Q_BLOCK, H, 2, dq).transpose(1, 0, 3, 4, 2, 5)
    bias_ht = table_b.T.astype(jnp.float32)
    s_pos = jnp.arange(S)

    def per_chunk(args):
        qblk, c = args
        t = c * Q_BLOCK + jnp.arange(Q_BLOCK)
        dist = t[:, None] - s_pos[None, :]
        bias = bias_ht[:, rel_bucket(dist)]
        logits = jnp.einsum('bhmqd,bhmsd->bhmqs', qblk, kt, preferred_element_type=jnp.float32) * scale
        logits = jnp.where(dist >= 0, logits + bias[None, :, None], NEG_INF)
        p = jax.nn.softmax(logits, axis=-1)
        attn = p[:, :, 0] - lam * p[:, :, 1]
        return jnp.einsum('bhqs,bhsd->bhqd', attn.astype(v.dtype), vt, preferred_element_type=jnp.float32)

    outs = lax.map(per_chunk, (qc, jnp.arange(n_chunks)))
    o = outs.transpose(1, 0, 3, 2, 4).reshape(B_, S, H, -1)
    o = rms_norm(o, subln_g) * (1.0 - lambda_init)
    return o.astype(v.dtype)

def memory_cross_attention(x, mem, norm_g, mem_g, wq, wk, wv, wo):
    B_, S, _ = x.shape
    M = mem.shape[1]
    h = rms_norm(x, norm_g)
    m = rms_norm(mem, mem_g)
    q = (h @ wq).reshape(B_, S, MEM_HEADS, MEM_HEAD_DIM)
    k = (m @ wk).reshape(B_, M, MEM_HEADS, MEM_HEAD_DIM)
    v = (m @ wv).reshape(B_, M, MEM_HEADS, MEM_HEAD_DIM)
    logits = jnp.einsum('bshd,bmhd->bhsm', q, k, preferred_element_type=jnp.float32) * (MEM_HEAD_DIM ** -0.5)
    p = jax.nn.softmax(logits, axis=-1)
    o = jnp.einsum('bhsm,bmhd->bshd', p.astype(v.dtype), v, preferred_element_type=jnp.float32).astype(x.dtype)
    return o.reshape(B_, S, MEM_HEADS * MEM_HEAD_DIM) @ wo

def swiglu(x, norm_g, w_gate, w_up, w_down):
    h = rms_norm(x, norm_g)
    return (jax.nn.silu(h @ w_gate) * (h @ w_up)) @ w_down

def first_inputs(seed: int = 0) -> dict:
    key = jax.random.key(seed)
    ks = jax.random.split(key, 24)
    f32 = jnp.float32

    def w(k, shape, fan_in):
        return jax.random.normal(k, shape, f32) * (fan_in ** -0.5)

    def gain(k, shape):
        return 1.0 + 0.02 * jax.random.normal(k, shape, f32)

    return {
        "x": jax.random.normal(ks[0], (BATCH, SEQ, D_MODEL), f32),
        "mem": jax.random.normal(ks[1], (BATCH, MEM_LEN, D_MODEL), f32),
        "mix_norm_g": gain(ks[2], (DEPTH, D_MODEL)),
        "w_in": w(ks[3], (DEPTH, D_MODEL, IN_WIDTH), D_MODEL),
        "moba_out_g": gain(ks[4], (DEPTH, A_WIDTH)),
        "diff_lambda": 0.1 * jax.random.normal(ks[5], (DEPTH, 4, B_QK_DIM), f32),
        "diff_subln_g": gain(ks[6], (DEPTH, B_V_DIM)),
        "w_out": w(ks[7], (DEPTH, MIX_WIDTH, D_MODEL), MIX_WIDTH),
        "rel_bias_table": 0.5 * jax.random.normal(ks[8], (REL_BUCKETS, N_ATT_HEADS), f32),
        "cross_norm_g": gain(ks[9], (DEPTH, D_MODEL)),
        "mem_norm_g": gain(ks[10], (DEPTH, D_MODEL)),
        "w_cq": w(ks[11], (DEPTH, D_MODEL, MEM_HEADS * MEM_HEAD_DIM), D_MODEL),
        "w_ck": w(ks[12], (DEPTH, D_MODEL, MEM_HEADS * MEM_HEAD_DIM), D_MODEL),
        "w_cv": w(ks[13], (DEPTH, D_MODEL, MEM_HEADS * MEM_HEAD_DIM), D_MODEL),
        "w_co": w(ks[14], (DEPTH, MEM_HEADS * MEM_HEAD_DIM, D_MODEL), MEM_HEADS * MEM_HEAD_DIM),
        "ffn_norm_g": gain(ks[15], (DEPTH, D_MODEL)),
        "w_gate": w(ks[16], (DEPTH, D_MODEL, D_FF), D_MODEL),
        "w_up": w(ks[17], (DEPTH, D_MODEL, D_FF), D_MODEL),
        "w_down": w(ks[18], (DEPTH, D_FF, D_MODEL), D_FF),
        "final_norm_g": gain(ks[19], (D_MODEL,)),
    }

def first_block(x, mem, mix_norm_g, w_in, moba_out_g, diff_lambda, diff_subln_g, w_out, rel_bias_table,
              cross_norm_g, mem_norm_g, w_cq, w_ck, w_cv, w_co, ffn_norm_g, w_gate, w_up, w_down,
              final_norm_g):
    B_, S, _ = x.shape
    table_a = rel_bias_table[:, :A_HEADS]
    table_b = rel_bias_table[:, A_HEADS:]
    for l in range(DEPTH):
        h = rms_norm(x, mix_norm_g[l])
        proj = jnp.einsum('bsd,de->bse', h, w_in[l])
        qa, ka, va, qb, kb, vb = jnp.split(proj, IN_SPLITS, axis=-1)
        oa = moba_attention(qa.reshape(B_, S, A_HEADS, A_HEAD_DIM),
                            ka.reshape(B_, S, A_HEADS, A_HEAD_DIM),
                            va.reshape(B_, S, A_HEADS, A_HEAD_DIM), table_a)
        oa = rms_norm(oa.reshape(B_, S, A_WIDTH), moba_out_g[l])
        lambda_init = 0.8 - 0.6 * math.exp(-0.3 * l)
        lp = diff_lambda[l].astype(jnp.float32)
        lam = jnp.exp(jnp.sum(lp[0] * lp[1])) - jnp.exp(jnp.sum(lp[2] * lp[3])) + lambda_init
        ob = diff_attention(qb.reshape(B_, S, B_HEADS, 2, B_QK_DIM),
                            kb.reshape(B_, S, B_HEADS, 2, B_QK_DIM),
                            vb.reshape(B_, S, B_HEADS, B_V_DIM),
                            table_b, lam, diff_subln_g[l], lambda_init)
        ob = ob.reshape(B_, S, B_WIDTH)
        mixed = jnp.concatenate([oa, ob], axis=-1)
        x = x + jnp.einsum('bse,ed->bsd', mixed, w_out[l])
        x = x + memory_cross_attention(x, mem, cross_norm_g[l], mem_norm_g[l], w_cq[l], w_ck[l], w_cv[l], w_co[l])
        x = x + swiglu(x, ffn_norm_g[l], w_gate[l], w_up[l], w_down[l])
    return rms_norm(x, final_norm_g)


DEPTH_2 = 2

HEAD_DIM = 64
ATTN_Q_HEADS = 8
ATTN_KV_HEADS = 2
ATTN_GROUP = ATTN_Q_HEADS // ATTN_KV_HEADS
WINDOW = 128
ATTN_BLOCK = 128
ROPE_THETA = 10000.0
ATTN_WIDTH = ATTN_Q_HEADS * HEAD_DIM
KV_WIDTH = ATTN_KV_HEADS * HEAD_DIM
CONV_WIDTH = D_MODEL // 2
SHORT_CONV_K = 3
HY_SPLITS = (ATTN_WIDTH, KV_WIDTH, KV_WIDTH, CONV_WIDTH, CONV_WIDTH, CONV_WIDTH)
HY_IN_WIDTH = sum(HY_SPLITS)
HY_OUT_WIDTH = ATTN_WIDTH + CONV_WIDTH
GLA_HEADS = 4
GLA_KEY_DIM = D_MODEL // 2
GLA_VAL_DIM = D_MODEL
GLA_DK = GLA_KEY_DIM // GLA_HEADS
GLA_DV = GLA_VAL_DIM // GLA_HEADS
GLA_GATE_RANK = 16
GLA_GATE_NORMALIZER = 16.0
GLA_CHUNK = 64
GLA_SPLITS = (GLA_KEY_DIM, GLA_KEY_DIM, GLA_VAL_DIM, GLA_GATE_RANK, GLA_VAL_DIM)
GLA_IN_WIDTH = sum(GLA_SPLITS)
D_FF_2 = 2816
FFN_CONV_K = 3
PLE_DIM = 256
MAX_POS_OFFSET = 1024
N_EVEN = (DEPTH_2 + 1) // 2
N_ODD = DEPTH_2 // 2
RMS_EPS = 1e-6


def _split(z, widths):
    idx, acc = [], 0
    for w in widths[:-1]:
        acc += w
        idx.append(acc)
    return jnp.split(z, idx, axis=-1)

def _rms_norm(x, gain):
    xf = x.astype(jnp.float32)
    y = xf * lax.rsqrt(jnp.mean(xf * xf, axis=-1, keepdims=True) + RMS_EPS)
    return (y * gain.astype(jnp.float32)).astype(x.dtype)

def _causal_depthwise_conv(x, w):
    k = w.shape[0]
    return lax.conv_general_dilated(
        x, w[:, None, :].astype(x.dtype), window_strides=(1,), padding=[(k - 1, 0)],
        dimension_numbers=('NWC', 'WIO', 'NWC'), feature_group_count=x.shape[-1])

def _rope_tables(positions):
    inv_freq = ROPE_THETA ** (-jnp.arange(0, HEAD_DIM, 2, dtype=jnp.float32) / HEAD_DIM)
    ang = positions.astype(jnp.float32)[..., None] * inv_freq
    return jnp.cos(ang)[:, :, None, :], jnp.sin(ang)[:, :, None, :]

def _apply_rope(x, cos, sin):
    x1, x2 = jnp.split(x.astype(jnp.float32), 2, axis=-1)
    return jnp.concatenate([x1 * cos - x2 * sin, x2 * cos + x1 * sin], axis=-1).astype(x.dtype)

def _sliding_window_sink_attention(q, k, v, sinks):
    b, s = q.shape[0], q.shape[1]
    nb = s // ATTN_BLOCK
    qb = q.reshape(b, nb, ATTN_BLOCK, ATTN_KV_HEADS, ATTN_GROUP, HEAD_DIM)

    def band(t):
        tb = t.reshape(b, nb, ATTN_BLOCK, ATTN_KV_HEADS, HEAD_DIM)
        prev = jnp.pad(tb[:, :-1], ((0, 0), (1, 0), (0, 0), (0, 0), (0, 0)))
        return jnp.concatenate([prev, tb], axis=2)

    kband, vband = band(k), band(v)
    scores = jnp.einsum('bnqhgd,bnkhd->bnhgqk', qb, kband).astype(jnp.float32) * (HEAD_DIM ** -0.5)
    blk = jnp.arange(nb)[:, None] * ATTN_BLOCK
    q_pos = blk + jnp.arange(ATTN_BLOCK)[None, :]
    k_pos = blk - ATTN_BLOCK + jnp.arange(2 * ATTN_BLOCK)[None, :]
    dist = q_pos[:, :, None] - k_pos[:, None, :]
    allowed = (dist >= 0) & (dist < WINDOW) & (k_pos[:, None, :] >= 0)
    scores = jnp.where(allowed[None, :, None, None], scores, -jnp.inf)
    sink = jnp.broadcast_to(
        sinks.astype(jnp.float32).reshape(1, 1, ATTN_KV_HEADS, ATTN_GROUP, 1, 1), scores.shape[:-1] + (1,))
    probs = jax.nn.softmax(jnp.concatenate([scores, sink], axis=-1), axis=-1)[..., :-1]
    out = jnp.einsum('bnhgqk,bnkhd->bnqhgd', probs.astype(v.dtype), vband)
    return out.reshape(b, s, ATTN_WIDTH)

def _attn_conv_mixer(h, cos, sin, w_in, q_norm, k_norm, sinks, conv_w, w_out):
    b, s, _ = h.shape
    q, k, v, cb, cc, cx = _split(h @ w_in, HY_SPLITS)
    q = _apply_rope(_rms_norm(q.reshape(b, s, ATTN_Q_HEADS, HEAD_DIM), q_norm), cos, sin)
    k = _apply_rope(_rms_norm(k.reshape(b, s, ATTN_KV_HEADS, HEAD_DIM), k_norm), cos, sin)
    v = v.reshape(b, s, ATTN_KV_HEADS, HEAD_DIM)
    attn = _sliding_window_sink_attention(q, k, v, sinks)
    conv = cb * _causal_depthwise_conv(cc * cx, conv_w)
    return jnp.concatenate([attn, conv], axis=-1) @ w_out

def _gla_chunked(q, k, v, log_a):
    b, s, nh, dk = q.shape
    dv = v.shape[-1]
    nc = s // GLA_CHUNK

    def chunks(t):
        return t.astype(jnp.float32).reshape(b, nc, GLA_CHUNK, nh, t.shape[-1]).transpose(1, 0, 3, 2, 4)

    qc, kc, vc = chunks(q), chunks(k), chunks(v)
    gc = jnp.cumsum(chunks(log_a), axis=3)
    causal = jnp.tril(jnp.ones((GLA_CHUNK, GLA_CHUNK), dtype=bool))

    def step(state, inp):
        qi, ki, vi, gi = inp
        g_end = gi[:, :, -1, :]
        o_inter = jnp.einsum('bhtd,bhdv->bhtv', qi * jnp.exp(gi), state)
        rel = gi[:, :, :, None, :] - gi[:, :, None, :, :]
        decay = jnp.exp(jnp.where(causal[:, :, None], rel, -jnp.inf))
        scores = jnp.einsum('bhtd,bhsd,bhtsd->bhts', qi, ki, decay)
        o_intra = jnp.einsum('bhts,bhsv->bhtv', scores, vi)
        state = jnp.exp(g_end)[..., None] * state + jnp.einsum(
            'bhsd,bhsv->bhdv', ki * jnp.exp(g_end[:, :, None, :] - gi), vi)
        return state, o_inter + o_intra

    state0 = jnp.zeros((b, nh, dk, dv), jnp.float32)
    _, o = lax.scan(step, state0, (qc, kc, vc, gc))
    return o.transpose(1, 0, 3, 2, 4).reshape(b, s, nh, dv)

def _gla_mixer(h, w_in, w_gate_up, gate_bias, o_norm, w_out):
    b, s, _ = h.shape
    q, k, v, g_lr, og = _split(h @ w_in, GLA_SPLITS)
    log_a = jax.nn.log_sigmoid((g_lr @ w_gate_up + gate_bias).astype(jnp.float32)) / GLA_GATE_NORMALIZER

    def heads(t, d):
        return t.reshape(b, s, GLA_HEADS, d)

    o = _gla_chunked(heads(q, GLA_DK) * (GLA_DK ** -0.5), heads(k, GLA_DK), heads(v, GLA_DV), heads(log_a, GLA_DK))
    o = _rms_norm(o.astype(h.dtype), o_norm) * jax.nn.silu(heads(og, GLA_DV))
    return o.reshape(b, s, GLA_VAL_DIM) @ w_out

def _conv_ffn(h, w_up, conv_w, conv_b, w_down):
    u = _causal_depthwise_conv(h @ w_up, conv_w) + conv_b
    gate, up = jnp.split(u, 2, axis=-1)
    return (jax.nn.gelu(gate, approximate=False) * up) @ w_down

def _per_layer_embedding(x, p_i, norm, w_gate, w_proj):
    gate = jax.nn.sigmoid(_rms_norm(x, norm) @ w_gate)
    return gate * (p_i @ w_proj)

def second_inputs(seed: int = 0) -> dict:
    key = jax.random.key(seed)
    ks = jax.random.split(key, 24)
    f32 = jnp.float32

    def normal(k, shape, fan_in):
        return jax.random.normal(k, shape, f32) * (fan_in ** -0.5)

    def gain(k, shape):
        return 1.0 + 0.05 * jax.random.normal(k, shape, f32)

    x = jax.random.normal(ks[0], (BATCH, SEQ, D_MODEL), f32)
    p = jax.random.normal(ks[1], (DEPTH_2, BATCH, SEQ, PLE_DIM), f32)
    offset = jax.random.randint(ks[2], (BATCH, 1), 0, MAX_POS_OFFSET, dtype=jnp.int32)
    positions = offset + jnp.arange(SEQ, dtype=jnp.int32)[None, :]
    return {
        'x': x,
        'p': p,
        'positions': positions,
        'mix_norm': gain(ks[3], (DEPTH_2, D_MODEL)),
        'ffn_norm': gain(ks[4], (DEPTH_2, D_MODEL)),
        'ffn_w_up': normal(ks[5], (DEPTH_2, D_MODEL, 2 * D_FF_2), D_MODEL),
        'ffn_conv_w': normal(ks[6], (DEPTH_2, FFN_CONV_K, 2 * D_FF_2), FFN_CONV_K),
        'ffn_conv_b': 0.02 * jax.random.normal(ks[7], (DEPTH_2, 2 * D_FF_2), f32),
        'ffn_w_down': normal(ks[8], (DEPTH_2, D_FF_2, D_MODEL), D_FF_2),
        'ple_norm': gain(ks[9], (DEPTH_2, D_MODEL)),
        'ple_w_gate': normal(ks[10], (DEPTH_2, D_MODEL, D_MODEL), D_MODEL),
        'ple_w_proj': normal(ks[11], (DEPTH_2, PLE_DIM, D_MODEL), PLE_DIM),
        'hy_w_in': normal(ks[12], (N_EVEN, D_MODEL, HY_IN_WIDTH), D_MODEL),
        'hy_q_norm': gain(ks[13], (N_EVEN, HEAD_DIM)),
        'hy_k_norm': gain(ks[14], (N_EVEN, HEAD_DIM)),
        'hy_sinks': jax.random.normal(ks[15], (N_EVEN, ATTN_Q_HEADS), f32),
        'hy_conv_w': normal(ks[16], (N_EVEN, SHORT_CONV_K, CONV_WIDTH), SHORT_CONV_K),
        'hy_w_out': normal(ks[17], (N_EVEN, HY_OUT_WIDTH, D_MODEL), HY_OUT_WIDTH),
        'gla_w_in': normal(ks[18], (N_ODD, D_MODEL, GLA_IN_WIDTH), D_MODEL),
        'gla_w_gate_up': normal(ks[19], (N_ODD, GLA_GATE_RANK, GLA_KEY_DIM), GLA_GATE_RANK),
        'gla_gate_bias': 0.1 * jax.random.normal(ks[20], (N_ODD, GLA_KEY_DIM), f32),
        'gla_o_norm': gain(ks[21], (N_ODD, GLA_DV)),
        'gla_w_out': normal(ks[22], (N_ODD, GLA_VAL_DIM, D_MODEL), GLA_VAL_DIM),
    }

def second_block(x, p, positions, mix_norm, ffn_norm, ffn_w_up, ffn_conv_w, ffn_conv_b, ffn_w_down,
              ple_norm, ple_w_gate, ple_w_proj, hy_w_in, hy_q_norm, hy_k_norm, hy_sinks, hy_conv_w,
              hy_w_out, gla_w_in, gla_w_gate_up, gla_gate_bias, gla_o_norm, gla_w_out):
    cos, sin = _rope_tables(positions)
    for i in range(DEPTH_2):
        j = i // 2
        h = _rms_norm(x, mix_norm[i])
        if i % 2 == 0:
            x = x + _attn_conv_mixer(h, cos, sin, hy_w_in[j], hy_q_norm[j], hy_k_norm[j], hy_sinks[j],
                                     hy_conv_w[j], hy_w_out[j])
        else:
            x = x + _gla_mixer(h, gla_w_in[j], gla_w_gate_up[j], gla_gate_bias[j], gla_o_norm[j], gla_w_out[j])
        x = x + _conv_ffn(_rms_norm(x, ffn_norm[i]), ffn_w_up[i], ffn_conv_w[i], ffn_conv_b[i], ffn_w_down[i])
        x = x + _per_layer_embedding(x, p[i], ple_norm[i], ple_w_gate[i], ple_w_proj[i])
    return x


def setup_inputs(seed=0):
    out = dict(first_inputs(seed))
    for name, value in second_inputs(seed + 1).items():
        if name != "x":
            out[name + "_2"] = value
    return out


def reference(
    x, mem, mix_norm_g, w_in, moba_out_g, diff_lambda, diff_subln_g, w_out, rel_bias_table,
    cross_norm_g, mem_norm_g, w_cq, w_ck, w_cv, w_co, ffn_norm_g, w_gate, w_up, w_down,
    final_norm_g, p_2, positions_2, mix_norm_2, ffn_norm_2, ffn_w_up_2, ffn_conv_w_2,
    ffn_conv_b_2, ffn_w_down_2, ple_norm_2, ple_w_gate_2, ple_w_proj_2, hy_w_in_2, hy_q_norm_2,
    hy_k_norm_2, hy_sinks_2, hy_conv_w_2, hy_w_out_2, gla_w_in_2, gla_w_gate_up_2,
    gla_gate_bias_2, gla_o_norm_2, gla_w_out_2,
):
    x = first_block(
        x, mem, mix_norm_g, w_in, moba_out_g, diff_lambda, diff_subln_g, w_out, rel_bias_table,
        cross_norm_g, mem_norm_g, w_cq, w_ck, w_cv, w_co, ffn_norm_g, w_gate, w_up, w_down,
        final_norm_g,
    )
    return second_block(
        x, p_2, positions_2, mix_norm_2, ffn_norm_2, ffn_w_up_2, ffn_conv_w_2, ffn_conv_b_2,
        ffn_w_down_2, ple_norm_2, ple_w_gate_2, ple_w_proj_2, hy_w_in_2, hy_q_norm_2,
        hy_k_norm_2, hy_sinks_2, hy_conv_w_2, hy_w_out_2, gla_w_in_2, gla_w_gate_up_2,
        gla_gate_bias_2, gla_o_norm_2, gla_w_out_2,
    )


_drawn_inputs = setup_inputs


def setup_inputs(seed=0):
    import zlib

    import numpy as np

    out = dict(_drawn_inputs(seed))
    spreads = {}
    factors = {'moba_out_g': 3.037,
     'diff_subln_g': 3.437,
     'cross_norm_g': 8.0,
     'mem_norm_g': 8.0,
     'ffn_norm_g': 3.022,
     'ffn_conv_b_2': 3.083,
     'ple_norm_2': 5.677,
     'hy_q_norm_2': 8.0,
     'hy_k_norm_2': 8.0,
     'gla_gate_bias_2': 2.961,
     'gla_o_norm_2': 3.019,
     'hy_sinks_2': 6.493}
    for name, (base, spread) in spreads.items():
        noise = np.random.default_rng([zlib.crc32(name.encode()), seed]).standard_normal(out[name].shape)
        drawn = base * np.exp(spread * noise) if base else spread * noise
        out[name] = __import__('jax').numpy.asarray(drawn.astype(out[name].dtype))
    for name, factor in factors.items():
        out[name] = (out[name] * factor).astype(out[name].dtype)
    return out
```

```python
from contextlib import ExitStack
import math

import numpy as np
import concourse.bass as bass
from concourse import mybir

F32 = mybir.dt.float32
F32R = mybir.dt.float32r
I32 = mybir.dt.int32
U8 = mybir.dt.uint8
ALU = mybir.AluOpType
ACT = mybir.ActivationFunctionType
AX_X = mybir.AxisListType.X

P = 128
T = 256
TT = T // P
DM = 1024
KT = DM // P
FF = 2816
FT = FF // P
U = 3
CHUNK = 16 * P
DVE_COLS = 1280
AHEAD = 2
EPS = 1e-6
MASKED = -1e30
QK_SCALE = 0.125
LAMBDA_INIT = 0.8 - 0.6 * math.exp(-0.3 * 0)
N_DIST = 384
N_BUCKETS = 32
ATT_HEADS = 12
LEVELS = (64, 32, 16, 8, 4, 2, 1)

C_IDENT, C_ONES, C_HALF, C_ROT, C_SWAP, C_WIN, C_FREQ = 0, 128, 256, 384, 512, 640, 896
N_CONST = 897

PARAMS = [("mix_norm_g", 8), ("moba_out_g", 4), ("diff_subln_g", 1), ("cross_norm_g", 8), ("mem_norm_g", 8),
          ("ffn_norm_g", 8), ("final_norm_g", 8), ("mix_norm_2", 16), ("ffn_norm_2", 16), ("ple_norm_2", 16),
          ("gla_o_norm_2", 2), ("gla_gate_bias_2", 4), ("hy_conv_w_2", 12), ("hy_q_norm_2", 1), ("hy_k_norm_2", 1)]
PCOL = {}
_n = 0
for _name, _rows in PARAMS:
    PCOL[_name] = _n
    _n += _rows
N_PARAM = _n
CONV_COL = 128
N_CONV = 2 * 3 * 2 * FT
CONVB_COL = CONV_COL + N_CONV
N_PCOLS = CONVB_COL + 2 * 2 * FT

PHASES = [("w_in", 12, 0), ("w_ck", 4, 0), ("w_cv", 4, 0), ("w_out", 4, 0), ("w_cq", 4, 0), ("w_co", 4, 0),
          ("up0", FT, 0), ("down0", FT // 2, 1), ("hy_in", 9, 0), ("hy_out", 4, 0), ("up1", FT, 0),
          ("down1", FT // 2, 1), ("proj1", 1, 1), ("gate1", 4, 0), ("gla_in", 12, 0), ("gla_out", 4, 0),
          ("up2", FT, 0), ("down2", FT // 2, 1), ("proj2", 1, 1), ("gate2", 4, 0)]
FIRST, COUNT, FIRST_OUT = {}, {}, {}
_c = _o = 0
for _name, _k, _over_k in PHASES:
    FIRST[_name], COUNT[_name], FIRST_OUT[_name] = _c, _k, _o
    _c += _k
    _o += 0 if _over_k else _k
CHUNKS = _c
PHASE_OVER_K = {_name: _over_k for _name, _, _over_k in PHASES}


class Counts:

    def __init__(self, engine):
        self.engine, self.taken, self.sent = engine, {}, {}
        self.per_turn = {}

    def next(self, sem, events=1):
        self.taken[sem] = self.taken.get(sem, 0) + events
        return self.taken[sem]

    def one(self, sem):
        self.sent[sem] = self.sent.get(sem, 0) + 1
        return 1

    def each(self, n, body, peel=3, ahead_of_loop=None):
        def counts():
            return [(d, s, v) for d in (self.taken, self.sent) for s, v in d.items()]

        peel = min(peel, n)
        for j in range(peel):
            before = {(id(d), s): v for d, s, v in counts()}
            body(j, j % U)
        turns = (n - peel) // U
        if turns < 2:
            turns = 0
        if turns:
            start = [(d, s, v, v - before.get((id(d), s), 0)) for d, s, v in counts() if s not in self.per_turn]
            start_turn = {s: self.taken[s] for s in self.per_turn}
            if ahead_of_loop:
                ahead_of_loop()
            with self.engine.Fori(0, turns) as turn:
                for s, v in start_turn.items():
                    self.taken[s] = turn * self.per_turn[s] + v
                for u in range(U):
                    for d, s, v, step in start:
                        if step:
                            d[s] = turn * (U * step) + (v + u * step)
                    body(turn * U + (peel + u), (peel + u) % U)
            for d, s, v, step in start:
                d[s] = v + turns * U * step
            for s, v in start_turn.items():
                self.taken[s] = turns * self.per_turn[s] + v
        for j in range(peel + turns * U, n):
            body(j, j % U)


def program(nc, io, out):
    with ExitStack() as stack:
        place = {"at": (nc.sbuf_base + 31) // 32 * 32}

        def at(name, offset, shape, dtype=F32):
            return nc.alloc_sbuf_tensor_at(name, [P] + shape, dtype, offset=offset)

        def sb(name, shape, dtype=F32, size=None):
            offset = place["at"]
            nbytes = int(np.prod(shape)) * (1 if dtype == U8 else 4) if size is None else size
            place["at"] = offset + (nbytes + 31) // 32 * 32
            return at(name, offset, shape, dtype)

        raw = sb("raw", [U, CHUNK])
        w_hi = sb("w_hi", [U, CHUNK], F32R)
        w_lo = sb("w_lo", [U, CHUNK], F32R)
        x = sb("x", [KT, T])
        a_hi, a_lo = sb("a_hi", [KT, T], F32R), sb("a_lo", [KT, T], F32R)
        b_hi, b_lo = sb("b_hi", [KT, T], F32R), sb("b_lo", [KT, T], F32R)
        A, B = (a_hi, a_lo), (b_hi, b_lo)
        sq = sb("sq", [2, 2 * T])
        sq_sum = sb("sq_sum", [2 * T])
        mean_sq = sb("mean_sq", [2 * T])
        rough = sb("rough", [2 * T])
        newton = sb("newton", [2 * T])
        rstd = sb("rstd", [T])
        rstd_mem = sb("rstd_mem", [T])
        const = sb("const", [N_CONST])
        level_mask = sb("level_mask", [len(LEVELS) + 1, P], U8)
        par = sb("par", [N_PCOLS])
        cos_t = sb("cos_t", [T])
        sin_t = sb("sin_t", [T])
        sinks = sb("sinks", [8])
        subln_g = sb("subln_g", [1])
        neg_lam = sb("neg_lam", [1])
        lam_dot = sb("lam_dot", [2])
        lam_exp = sb("lam_exp", [2])
        row_max = sb("row_max", [2, 8])
        neg_max = sb("neg_max", [2, 8])
        row_sum = sb("row_sum", [2, 8])
        row_rec = sb("row_rec", [2, 8])
        ident = const[:, C_IDENT:C_IDENT + P]
        ones = const[:, C_ONES:C_ONES + P]
        half_ones = const[:, C_HALF:C_HALF + P]
        rot_half = const[:, C_ROT:C_ROT + P]
        swap_half = const[:, C_SWAP:C_SWAP + P]
        window = const[:, C_WIN:C_WIN + 2 * P]
        inv_freq = const[:, C_FREQ:C_FREQ + 1]

        H = place["at"]
        H_SIZE = 52 * 1024
        TR = H + H_SIZE
        assert TR + 20 * 1024 <= nc.sbuf_usable_end, (TR + 20 * 1024, nc.sbuf_usable_end)
        KB = 1024
        qkv = at("qkv", H, [24, T])
        v_tok = at("v_tok", H + 24 * KB, [TT, DM])
        scores = at("scores", H + 32 * KB, [8, 3 * P])
        probs_t = at("probs_t", H + 44 * KB, [4, 512])
        att_a = at("att_a", H, [4, T])
        mem_v_t = at("mem_v_t", H + 4 * KB, [2, 2, T])
        mem_v = [at("mem_v0", H + 8 * KB, [DM]), at("mem_v1", H + 20 * KB, [DM])]
        att_b = at("att_b", H + 12 * KB, [4, T])
        bias_tab = at("bias_tab", TR, [ATT_HEADS, 2 * P])
        mem_k = at("mem_k", TR + 12 * KB, [KT, T])
        x_tok = at("x_tok", H, [TT, DM])
        rows = at("rows", H + 8 * KB, [4, P])
        lam_in = at("lam_in", H + 10 * KB, [4, 64])
        lam_mul = at("lam_mul", H + 11 * KB, [2, 64])
        bias_rows = at("bias_rows", H + 24 * KB, [ATT_HEADS, N_DIST])
        onehot = at("onehot", H + 42 * KB, [N_DIST])
        table = at("table", H + 43 * KB + 512, [ATT_HEADS])
        mem_tok = at("mem_tok", TR + 12 * KB, [TT, DM])
        mem_t = at("mem_t", H + 44 * KB, [KT, T])
        q_mem = at("q_mem", H + 24 * KB, [KT, T])
        scores_mem = at("scores_mem", H + 32 * KB, [8, T])
        hid_hi = at("hid_hi", H, [FT, T], F32R)
        hid_lo = at("hid_lo", H + 22 * KB, [FT, T], F32R)
        gate_z = at("gate_z", TR, [U, T])
        up_z = at("up_z", TR + 3 * KB, [U, T])
        gate_act = at("gate_act", TR + 6 * KB, [U, T])
        hid = at("hid", TR + 9 * KB, [U, T])
        CONV_T = 2 + T
        conv_in = at("conv_in", TR, [U, 2, CONV_T])
        conv_out = at("conv_out", TR + 6208, [U, 2, T])
        conv_gelu = at("conv_gelu", TR + 6208 + 6 * KB, [U, T])
        conv_hid = at("conv_hid", TR + 6208 + 9 * KB, [U, T])
        p_tok = at("p_tok", H + 44 * KB, [TT, T])
        p_hi = at("p_hi", H + 46 * KB, [2, T], F32R)
        p_lo = at("p_lo", H + 48 * KB, [2, T], F32R)
        ple_z = at("ple_z", TR, [2, 2, T])
        ple_sig = at("ple_sig", TR + 4 * KB, [2, 2, T])
        ple_mul = at("ple_mul", TR + 8 * KB, [2, 2, T])
        x_out = at("x_out", H, [TT, DM])
        hy = at("hy", H, [18, T])
        hy_v = at("hy_v", H + 18 * KB, [TT, P])
        hy_qk = at("hy_qk", H + 39 * KB, [5, T])
        hy_rot = at("hy_rot", H + 46 * KB, [5, T])
        hy_kswap = at("hy_kswap", H + 51 * KB, [T])
        hy_scores = at("hy_scores", H + 19 * KB, [8, 3 * P])
        hy_probs_t = at("hy_probs_t", H + 31 * KB, [4, 512])
        hy_conv_in = at("hy_conv_in", TR, [4, CONV_T])
        hy_conv = at("hy_conv", TR + 4128, [4, T])
        hy_att = at("hy_att", TR + 4128 + 4 * KB, [4, T])
        hy_sink = at("hy_sink", TR + 4128 + 8 * KB, [2, 8])
        rope_i = at("rope_i", TR + 14 * KB, [T], I32)
        rope_a = at("rope_a", TR + 15 * KB, [T])
        rope_n = at("rope_n", TR + 16 * KB, [T])
        rope_r = at("rope_r", TR + 17 * KB, [2, T])
        gla = at("gla", H, [24, T])
        gla_v = at("gla_v", H + 24 * KB, [TT, DM])
        gla_s = at("gla_s", H + 32 * KB, [3, 4, P])
        gla_g = at("gla_g", H + 38 * KB, [4, T])
        level_mask_f = at("level_mask_f", H + 38 * KB, [(len(LEVELS) + 1) * P])
        gla_e = at("gla_e", H + 42 * KB, [4, T])
        gla_w = [at("gla_w0", H + 46 * KB, [4, T]), at("gla_w1", TR + 8 * KB, [4, T])]
        gla_lr = at("gla_lr", H + 50 * KB, [T])
        gla_o = at("gla_o", TR, [8, T])
        gla_z = at("gla_z", TR + 12 * KB, [4, T])
        gla_wlr = at("gla_wlr", TR + 16 * KB, [KT, 16])
        gla_up = at("gla_up", TR + 17 * KB, [512])

        G = [stack.enter_context(nc.psum_tensor(f"g{i}", [P, 512], F32)) for i in range(U)]
        D = [stack.enter_context(nc.psum_tensor(f"d{i}", [P, 512], F32)) for i in range(5)]
        STAT = 4
        bias_dram = nc.dram_tensor("bias_dram", (P, ATT_HEADS * N_DIST), F32, kind="Internal").ap()

        def sem(name):
            return stack.enter_context(nc.semaphore(name))

        loaded = [sem(f"loaded{i}") for i in range(U)]
        hi_done, lo_dve, lo_pool = sem("hi_done"), sem("lo_dve"), sem("lo_pool")
        chunk_done, evicted = sem("chunk_done"), sem("evicted")
        full_dve, full_act = sem("full_dve"), sem("full_act")
        drained_dve, drained_act = sem("drained_dve"), sem("drained_act")
        x_ready, x_gated, x_normed = sem("x_ready"), sem("x_gated"), sem("x_normed")
        x_hi_done, x_split = sem("x_hi_done"), sem("x_split")
        sq_done, sq_added, sq_total, sq_for_pe = sem("sq_done"), sem("sq_added"), sem("sq_total"), sem("sq_for_pe")
        mean_done, rough_done = sem("mean_done"), sem("rough_done")
        max_done, exp_done, probs_done = sem("max_done"), sem("exp_done"), sem("probs_done")
        mixed_ready = sem("mixed_ready")
        lam_dots_done, lam_exp_done = sem("lam_dots_done"), sem("lam_exp_done")
        gate_done, act_done, tap_done, conv_done = sem("gate_done"), sem("act_done"), sem("tap_done"), sem("conv_done")
        hid_done, hid_hi_done, hid_split = sem("hid_done"), sem("hid_hi_done"), sem("hid_split")
        p_hi_done, p_split = sem("p_hi_done"), sem("p_split")
        angles_done, rope_done, qk_normed, qk_rotated, sink_done = (
            sem(s) for s in ("angles_done", "rope_done", "qk_normed", "qk_rotated", "sink_done"))
        lr_scaled, lr_ready, logit_done, soft_done, decay_done, expo_done, level_ready, gla_scores_done, silu_done = (
            sem(s) for s in ("lr_scaled", "lr_ready", "logit_done", "soft_done", "decay_done", "expo_done", "level_ready",
                             "gla_scores_done", "silu_done"))
        got_const, got_x, got_rows, got_mem, got_bias, got_small, got_rope, got_p, got_gla = (sem(s) for s in (
            "got_const", "got_x", "got_rows", "got_mem", "got_bias", "got_small", "got_rope", "got_p", "got_gla"))
        par_ready, bias_stored, masked_row = sem("par_ready"), sem("bias_stored"), sem("masked_row")
        out_ready, out_stored = sem("out_ready"), sem("out_stored")
        act_own, dve_own = sem("act_own"), sem("dve_own")

        def pcol(name, i=0):
            c = PCOL[name] + i
            return par[:, c:c + 1]

        def reused(n):
            return not isinstance(n, int) or n >= U

        def over(ap, n):
            return ap.unsqueeze(1).broadcast_to([P, n, ap.shape[-1]])

        def along(ap, n):
            return ap.unsqueeze(2).broadcast_to([P, ap.shape[-1], n])

        def flat(ap):
            return ap.rearrange("p a t -> p (a t)")

        def tile_at(ap, j):
            return flat(ap)[:, bass.ds(j * T, T)]

        def as_tiles(ap, width=T):
            return ap.rearrange("p (f t) -> p f t", t=width)

        def pair_at(ap, j):
            return as_tiles(flat(ap)[:, bass.ds(j * 2 * T, 2 * T)])

        def maps_of(b, t):
            return range(b % 2 + 4 * (b // 2), 4 * (b // 2) + (4 if t else 8), 2)

        block = stack.enter_context(nc.Block())

        @block.sync
        def _(sp):
            count = Counts(sp)

            sp.dma_start(x_tok[:], io["x"].rearrange("b (t p) d -> p (b t) d", p=P)).then_inc(got_x, 16)
            sp.dma_start(const[:], io["const"]).then_inc(got_const, 16)
            for name, n in PARAMS:
                c = PCOL[name]
                if name in ("hy_q_norm_2", "hy_k_norm_2"):
                    for half in range(2):
                        sp.dma_start(rows[c:c + 1, 0, 64 * half:64 * half + 64], io[name]).then_inc(got_rows, 16)
                    continue
                vectors = io[name].rearrange({1: "(r c) -> r c", 2: "l (r c) -> (l r) c", 3: "l t (r c) -> (l t r) c"}[
                    len(io[name].shape)], c=P)
                sp.dma_start(rows[c:c + n, 0, :], vectors).then_inc(got_rows, 16)
            conv_rows = io["ffn_conv_w_2"].rearrange("l t (r c) -> (l t r) c", c=P)
            for i in range(3):
                a, b = i * P, min((i + 1) * P, N_CONV)
                sp.dma_start(rows[0:b - a, 1 + i, :], conv_rows[a:b, :]).then_inc(got_rows, 16)
            tail = N_CONV - 2 * P
            sp.dma_start(rows[tail:tail + 4 * FT, 3, :], io["ffn_conv_b_2"].rearrange("l (r c) -> (l r) c", c=P)).then_inc(got_rows, 16)

            def by_k(w):
                return w.rearrange("(k p) n -> p k n", p=P)

            def weight_parts(name, j):
                if name in ("up0", "up1", "up2"):
                    if name == "up0":
                        src = [by_k(io[w][0])[:, :, bass.ds(j * P, P)] for w in ("w_gate", "w_up")]
                    else:
                        w = by_k(io["ffn_w_up_2"][int(name[-1]) - 1])
                        src = [w[:, :, bass.ds(j * P + f * FF, P)] for f in range(2)]
                    return [(src[f], lambda s, f=f: s.rearrange("p (k c) -> p k c", c=2 * P)[:, :, f * P:(f + 1) * P]) for f in range(2)]
                if PHASE_OVER_K[name]:
                    w = {"down0": io["w_down"][0], "down1": io["ffn_w_down_2"][0], "down2": io["ffn_w_down_2"][1],
                         "proj1": io["ple_w_proj_2"][0], "proj2": io["ple_w_proj_2"][1]}[name]
                    return [(w[bass.ds(j * 2 * P + h * P, P), :], lambda s, h=h: s[:, h * DM:(h + 1) * DM]) for h in range(2)]
                w = {"w_in": io["w_in"][0], "w_ck": io["w_ck"][0], "w_cv": io["w_cv"][0], "w_out": io["w_out"][0],
                     "w_cq": io["w_cq"][0], "w_co": io["w_co"][0], "hy_in": io["hy_w_in_2"][0], "hy_out": io["hy_w_out_2"][0],
                     "gate1": io["ple_w_gate_2"][0], "gate2": io["ple_w_gate_2"][1], "gla_in": io["gla_w_in_2"][0],
                     "gla_out": io["gla_w_out_2"][0]}[name]
                column = j * 2 * P
                if name == "gla_in" and j >= 8:
                    column = column + 16
                return [(by_k(w)[:, 4 * h:4 * h + 4, bass.ds(column, 2 * P)],
                         lambda s, h=h: s.rearrange("p (k c) -> p k c", c=2 * P)[:, 4 * h:4 * h + 4, :]) for h in range(2)]

            def load(name, j, jm):
                c = j + FIRST[name]
                slot = (FIRST[name] + jm) % U
                if reused(c):
                    sp.wait_ge(lo_dve, c - (U - 1))
                    sp.wait_ge(lo_pool, c - (U - 1))
                for src, dst in weight_parts(name, j):
                    sp.dma_start(dst(raw[:, slot, :]), src).then_inc(loaded[slot], 16)

            def stream(name, lo=0, hi=None):
                if lo == 0 and hi is None:
                    count.each(COUNT[name], lambda j, jm: load(name, j, jm))
                else:
                    for j in range(lo, hi):
                        load(name, j, j % U)

            stream("w_in", 0, 3)
            sp.dma_start(onehot[0:N_BUCKETS + 1, :], io["onehot"]).then_inc(got_small, 16)
            sp.dma_start(table[0:N_BUCKETS, :], io["rel_bias_table"]).then_inc(got_small, 16)
            sp.dma_start(lam_in[:].rearrange("p a b -> p (a b)"), io["diff_lambda"].rearrange("l a b -> (l a b)").partition_broadcast(P)).then_inc(got_small, 16)
            sp.dma_start(sinks[:], io["hy_sinks_2"].rearrange("l h -> (l h)").partition_broadcast(P)).then_inc(got_small, 16)
            sp.dma_start(mem_tok[:], io["mem"].rearrange("b (t p) d -> p (b t) d", p=P)).then_inc(got_mem, 16)
            stream("w_in", 3, 6)
            sp.wait_ge(drained_act, ATT_HEADS)
            sp.dma_start(bias_dram, bias_rows[:].rearrange("p h c -> p (h c)")).then_inc(bias_stored, 16)
            sp.wait_ge(bias_stored, count.next(bias_stored, 16))
            width = ATT_HEADS * N_DIST
            skewed = bass.AP(bias_dram.tensor, P - 1, [[width - 1, P], [N_DIST, ATT_HEADS], [1, 2 * P]])
            sp.dma_start(bias_tab[:], skewed).then_inc(got_bias, 16)
            stream("w_in", 6, 12)
            for name in ("w_ck", "w_cv", "w_out", "w_cq", "w_co", "up0", "down0"):
                stream(name)
            sp.dma_start(rope_i[:], io["positions_2"].rearrange("b s -> (b s)").partition_broadcast(P)).then_inc(got_rope, 16)
            stream("hy_in")
            stream("hy_out")
            for layer in (1, 2):
                stream(f"up{layer}")
                sp.dma_start(p_tok[:], io["p_2"][layer - 1].rearrange("b (t p) d -> p (b t) d", p=P)).then_inc(got_p, 16)
                stream(f"down{layer}")
                stream(f"proj{layer}")
                stream(f"gate{layer}")
                if layer == 1:
                    sp.dma_start(gla_wlr[:], by_k(io["gla_w_in_2"][0])[:, :, 2048:2064]).then_inc(got_gla, 16)
                    sp.dma_start(gla_up[0:16, :], io["gla_w_gate_up_2"][0]).then_inc(got_gla, 16)
                    sp.dma_start(level_mask_f[:], io["level_mask"]).then_inc(got_gla, 16)
                    stream("gla_in", 0, 8)
                    stream("gla_in", 8, 12)
                    stream("gla_out")
            for t in range(TT):
                sp.wait_ge(out_ready, count.next(out_ready, 2))
                sp.dma_start(out[0, t * P:(t + 1) * P, :], x_out[:, t, :]).then_inc(out_stored, 16)
            sp.wait_ge(out_stored, count.next(out_stored, 16 * TT))

        @block.tensor
        def _(pe):
            count = Counts(pe)
            due = {}
            free_at = {}

            def acquire(b):
                if b in free_at:
                    pe.wait_ge(*free_at[b])

            def fill(b, last, full, drained):
                if last is not None:
                    last.then_inc(full, 1)
                due[drained] = due.get(drained, 0) + 1
                free_at[b] = (drained, due[drained])
                return free_at[b]

            def mm(out, lhsT, rhs, start=True, stop=True):
                return pe.matmul(out, lhsT, rhs, start=start, stop=stop, skip_group_check=True)

            def turn(out, src, n=P):
                return pe.transpose(out, src, ident[0:n, 0:n])

            def chunk(name, j, jm, moving, fresh=False):
                c, n = j + FIRST[name], j + FIRST_OUT[name]
                slot, bank = (FIRST[name] + jm) % U, G[(FIRST_OUT[name] + jm) % U]
                pe.wait_ge(lo_dve, c + 1)
                pe.wait_ge(lo_pool, c + 1)
                if reused(n):
                    pe.wait_ge(evicted, n - (U - 1))
                for k in range(KT):
                    if fresh:
                        pe.wait_ge(x_split, count.next(x_split))
                    for f in range(2):
                        cols = slice(k * 2 * P + f * P, k * 2 * P + (f + 1) * P)
                        to = bank[:, f * T:(f + 1) * T]
                        mm(to, w_hi[:, slot, cols], moving[0][:, k, :], k == 0 and f == 0, False)
                        mm(to, w_hi[:, slot, cols], moving[1][:, k, :], False, False)
                        last = mm(to, w_lo[:, slot, cols], moving[0][:, k, :], False, k == KT - 1)
                last.then_inc(chunk_done, 1)

            def chunk_k(name, j, jm, moving, k0):
                c, slot = j + FIRST[name], (FIRST[name] + jm) % U
                first = isinstance(j, int) and j == 0
                final = isinstance(j, int) and j == COUNT[name] - 1
                pe.wait_ge(lo_dve, c + 1)
                pe.wait_ge(lo_pool, c + 1)
                if first:
                    for b in range(4):
                        acquire(b)
                order = [(h, f) for f in range(KT) for h in range(2)] if final else [(h, f) for h in range(2) for f in range(KT)]
                for h, f in order:
                    to = D[f // 2][:, (f % 2) * T:(f % 2 + 1) * T]
                    cols = slice(h * DM + f * P, h * DM + (f + 1) * P)
                    m_hi, m_lo = (tile_at(m, k0 + h) for m in moving)
                    mm(to, w_hi[:, slot, cols], m_hi, first and h == 0 and f % 2 == 0, False)
                    mm(to, w_hi[:, slot, cols], m_lo, False, False)
                    last = mm(to, w_lo[:, slot, cols], m_hi, False, final and h == 1)
                    if final and h == 1 and f in (1, 3, 5) and name[:4] == "down":
                        fill(f // 2, last, full_dve, x_ready)
                last.then_inc(chunk_done, 1)
                if final and name[:4] == "down":
                    fill(3, None, None, x_ready)

            def norm_sum():
                pe.wait_ge(sq_total, count.next(sq_total))
                acquire(STAT)
                mm(D[STAT][:, 0:T], ones, sq_sum[:, 0:T], True, False)
                fill(STAT, mm(D[STAT][:, 0:T], ones, sq_sum[:, T:2 * T], False, True), full_dve, mean_done)

            def outputs(name, moving):
                def body(j, jm):
                    fresh = isinstance(j, int) and j == 0
                    chunk(name, j, jm, moving, fresh)
                    if fresh:
                        norm_sum()
                count.each(COUNT[name], body)

            pe.wait_ge(got_const, count.next(got_const, 16))
            pe.wait_ge(got_rows, count.next(got_rows, 16 * (len(PARAMS) + 2 + 4)))
            turn(D[STAT][:, 0:N_PARAM], rows[0:N_PARAM, 0, :], N_PARAM)
            turn(D[STAT][:, CONV_COL:CONV_COL + P], rows[:, 1, :])
            turn(D[STAT][:, CONV_COL + P:CONV_COL + 2 * P], rows[:, 2, :])
            tail = N_CONV + 4 * FT - 2 * P
            fill(STAT, turn(D[STAT][:, CONV_COL + 2 * P:CONV_COL + 2 * P + tail], rows[0:tail, 3, :], tail), full_dve, par_ready)

            def turn_in(src):
                for b in range(4):
                    acquire(b)
                    for f in range(2):
                        for t in range(TT):
                            last = turn(D[b][:, f * T + t * P:f * T + (t + 1) * P], src[:, t, (2 * b + f) * P:(2 * b + f + 1) * P])
                    fill(b, last, full_dve, x_ready)

            pe.wait_ge(got_x, count.next(got_x, 16))
            turn_in(x_tok)

            def first_body(j, jm):
                fixed = isinstance(j, int)
                chunk("w_in", j, jm, A, fresh=fixed and j == 0)
                if fixed and j == 0:
                    norm_sum()
                if fixed and j == 1:
                    pe.wait_ge(got_small, count.next(got_small, 16 * 4))
                    pe.wait_ge(masked_row, count.next(masked_row))
                    for h in range(ATT_HEADS):
                        acquire(h % 4)
                        column = table[0:N_BUCKETS + 1, h:h + 1].broadcast_to([N_BUCKETS + 1, P])
                        fill(h % 4, mm(D[h % 4][:, 0:N_DIST], column, onehot[0:N_BUCKETS + 1, :]), full_act, drained_act)
                if fixed and j == 3:
                    pe.wait_ge(got_mem, count.next(got_mem, 16))
                    turn_in(mem_tok)
                if fixed and j == 4:
                    norm_sum()

            count.each(COUNT["w_in"], first_body, peel=6)

            def turn_values(src, f0, banks):
                for i, b in enumerate(banks):
                    acquire(b)
                    for f in range(4):
                        last = turn(D[b][:, f * P:(f + 1) * P], src[:, f0[i // 2] + f, (i % 2) * P:(i % 2 + 1) * P])
                    last = fill(b, last, full_act, drained_act)
                return last

            def score_tiles(q, key, q0, t):
                keys = (t + 1) * P
                for b in range(4 if t else 2):
                    acquire(b)
                    for i, m in enumerate(maps_of(b, t)):
                        half = slice((m % 2) * 64, (m % 2) * 64 + 64)
                        last = mm(D[b][:, i * keys:(i + 1) * keys], q[half, q0 + m // 2, t * P:(t + 1) * P], key(m)[half, 0:keys])
                    fill(b, last, full_dve, drained_dve)

            def weigh_values(heads, values, place_of, per_bank, probs, probs_t):
                turned = {}
                for step in range(heads + 1):
                    if step < heads:
                        b = step % 2
                        acquire(b)
                        for i in range(3):
                            last = turn(D[b][:, i * P:(i + 1) * P], probs[:, step, i * P:(i + 1) * P])
                        turned[step] = fill(b, last, full_act, drained_act)
                    if step >= 1:
                        h = step - 1
                        b = 2 + h // per_bank
                        to = place_of(h)
                        pe.wait_ge(*turned[h])
                        if h % per_bank == 0:
                            acquire(b)
                        mm(to, values(0, h), probs_t[:, h % 4, 0:T], True, False)
                        last = mm(to[:, P:T], values(1, h), probs_t[:, h % 4, T:3 * P], False, True)
                        if h % per_bank == per_bank - 1:
                            fill(b, last, full_act, drained_act)

            def half_place(h):
                return D[2 + h // 4][(h % 2) * 64:(h % 2) * 64 + 64, (h // 2 % 2) * T:(h // 2 % 2 + 1) * T]

            def whole_place(h):
                return D[2 + h // 2][:, (h % 2) * T:(h % 2 + 1) * T]

            def turn_mem_values(j):
                pe.wait_ge(evicted, FIRST_OUT["w_cv"] + j + 1)
                acquire(STAT)
                for t in range(TT):
                    for f in range(2):
                        last = turn(D[STAT][:, t * 2 * P + f * P:t * 2 * P + (f + 1) * P], mem_v_t[:, j % 2, f, t * P:(t + 1) * P])
                fill(STAT, last, full_act, drained_act)

            pe.wait_ge(evicted, COUNT["w_in"])
            values_turned = turn_values(qkv, (8, 20), (0, 1, 2, 3))
            score_tiles(qkv, lambda m: qkv[:, 4 + m // 2, :], 0, 1)
            score_tiles(qkv, lambda m: qkv[:, 4 + m // 2, :], 0, 0)
            for j in range(3):
                chunk("w_ck", j, j % U, B, fresh=j == 0)
            pe.wait_ge(*values_turned)
            pe.wait_ge(probs_done, count.next(probs_done))
            weigh_values(8, lambda t, h: v_tok[:, t, h * 64:(h + 1) * 64], half_place, 4, scores, probs_t)
            score_tiles(qkv, lambda m: qkv[:, 16 + m // 2, :], 12, 1)
            score_tiles(qkv, lambda m: qkv[:, 16 + m // 2, :], 12, 0)
            chunk("w_ck", 3, 3 % U, B)
            chunk("w_cv", 0, 0, B)
            pe.wait_ge(sq_for_pe, count.next(sq_for_pe, 2))
            acquire(STAT)
            for f in range(4):
                last = mm(D[STAT][:, 0:T], ones, sq[:, f // 2, (f % 2) * T:(f % 2 + 1) * T], f == 0, f == 3)
            fill(STAT, last, full_dve, mean_done)
            chunk("w_cv", 1, 1, B)
            turn_mem_values(0)
            pe.wait_ge(probs_done, count.next(probs_done))
            weigh_values(4, lambda t, h: v_tok[:, t, 512 + h * P:512 + (h + 1) * P], whole_place, 2, scores, probs_t)
            chunk("w_cv", 2, 2, B)
            turn_mem_values(1)
            for b in range(2):
                pe.wait_ge(sq_for_pe, count.next(sq_for_pe))
                acquire(b)
                for f in range(2):
                    last = mm(D[b][:, f * T:(f + 1) * T], ones, sq[:, b, f * T:(f + 1) * T])
                fill(b, last, full_dve, mean_done)
            chunk("w_cv", 3, 0, B)
            turn_mem_values(2)
            turn_mem_values(3)
            mem_v_turned = free_at[STAT]
            for j in range(COUNT["w_out"]):
                chunk("w_out", j, j % U, A, fresh=j == 0)

            outputs("w_cq", B)
            pe.wait_ge(evicted, FIRST_OUT["w_cq"] + COUNT["w_cq"])
            for b in range(4):
                acquire(b)
                for i in range(2):
                    t, h = (2 * b + i) // 4, (2 * b + i) % 4
                    for d in range(2):
                        last = mm(D[b][:, i * T:(i + 1) * T], q_mem[:, 2 * h + d, t * P:(t + 1) * P], mem_k[:, 2 * h + d, :],
                                  d == 0, d == 1)
                fill(b, last, full_dve, drained_dve)
            pe.wait_ge(probs_done, count.next(probs_done))
            pe.wait_ge(*mem_v_turned)
            turned = {}
            for step in range(5):
                if step < 4:
                    acquire(step % 2)
                    for s in range(2):
                        for t in range(TT):
                            last = turn(D[step % 2][:, s * T + t * P:s * T + (t + 1) * P], scores_mem[:, t * 4 + step, s * P:(s + 1) * P])
                    turned[step] = fill(step % 2, last, full_act, drained_act)
                if step >= 1:
                    h = step - 1
                    b = 2 + h % 2
                    pe.wait_ge(*turned[h])
                    acquire(b)
                    for d in range(2):
                        to, v = D[b][:, d * T:(d + 1) * T], slice((2 * h + d) * P, (2 * h + d + 1) * P)
                        mm(to, mem_v[0][:, v], probs_t[:, h, 0:T], True, False)
                        last = mm(to, mem_v[1][:, v], probs_t[:, h, T:2 * T], False, True)
                    last.then_inc(full_act, 1)
                    free_at[b] = (x_split, count.taken[x_split] + 2 * (h + 1))
            for j in range(COUNT["w_co"]):
                chunk("w_co", j, j % U, A, fresh=j == 0)

            def ffn(layer, moving):
                outputs(f"up{layer}", moving)

                def body(j, jm):
                    pe.wait_ge(hid_split, count.next(hid_split, 2))
                    chunk_k(f"down{layer}", j, jm, (hid_hi, hid_lo), j * 2)
                count.each(COUNT[f"down{layer}"], body)

            ffn(0, B)
            norm_sum()

            for j in range(4):
                chunk("hy_in", j, j % U, A, fresh=j == 0)
                if j == 0:
                    norm_sum()
            tiles_of = (2, 2, 1)
            for i in range(3):
                pe.wait_ge(sq_for_pe, count.next(sq_for_pe))
                acquire(i)
                for f in range(tiles_of[i]):
                    last = mm(D[i][:, f * T:(f + 1) * T], half_ones, hy_rot[:, 2 * i + f, :])
                fill(i, last, full_dve, mean_done)
            chunk("hy_in", 4, 4 % U, A)
            for i in range(3):
                pe.wait_ge(qk_normed, count.next(qk_normed))
                acquire(i)
                for f in range(tiles_of[i]):
                    last = mm(D[i][:, f * T:(f + 1) * T], rot_half, hy_qk[:, 2 * i + f, :])
                fill(i, last, full_dve, drained_dve)
            acquire(3)
            for t in range(TT):
                last = turn(D[3][:, t * P:(t + 1) * P], hy[:, 5, t * P:(t + 1) * P])
            hy_v_turned = fill(3, last, full_act, drained_act)
            chunk("hy_in", 5, 5 % U, A)
            pe.wait_ge(qk_rotated, count.next(qk_rotated))
            acquire(STAT)
            pe.wait_ge(*fill(STAT, mm(D[STAT][:, 0:T], swap_half, hy_qk[:, 4, :]), full_act, drained_act))

            def hy_key(m):
                return hy_qk[:, 4, :] if m % 2 == m // 4 else hy_kswap[:, :]

            score_tiles(hy_qk, hy_key, 0, 1)
            score_tiles(hy_qk, hy_key, 0, 0)
            chunk("hy_in", 6, 6 % U, A)
            chunk("hy_in", 7, 7 % U, A)
            pe.wait_ge(probs_done, count.next(probs_done))
            pe.wait_ge(*hy_v_turned)
            weigh_values(8, lambda t, h: hy_v[:, t, (h // 4) * 64:(h // 4 + 1) * 64], half_place, 4, hy_scores, hy_probs_t)
            chunk("hy_in", 8, 8 % U, A)
            for j in range(COUNT["hy_out"]):
                chunk("hy_out", j, j % U, B, fresh=j == 0)

            def embedding(layer, moving):
                pe.wait_ge(got_p, count.next(got_p, 16))
                acquire(STAT)
                for f in range(2):
                    for t in range(TT):
                        last = turn(D[STAT][:, f * T + t * P:f * T + (t + 1) * P], p_tok[:, t, f * P:(f + 1) * P])
                fill(STAT, last, full_act, p_split)
                pe.wait_ge(p_split, count.next(p_split))
                chunk_k(f"proj{layer}", 0, 0, (p_hi, p_lo), 0)
                for b in range(4):
                    fill(b, None, None, drained_dve)
                for j in range(COUNT[f"gate{layer}"]):
                    chunk(f"gate{layer}", j, j % U, moving, fresh=j == 0)
                    if j == 0:
                        norm_sum()

            ffn(1, A)
            embedding(1, B)

            def gla_chunk(j):
                chunk("gla_in", j, j % U, A, fresh=j == 0)

            gla_chunk(0)
            norm_sum()
            pe.wait_ge(lr_scaled, count.next(lr_scaled))
            acquire(0)
            for k in range(KT):
                last = mm(D[0][0:16, 0:T], gla_wlr[:, k, :], x[:, k, :], k == 0, k == KT - 1)
            fill(0, last, full_dve, lr_ready)
            gla_chunk(1)
            pe.wait_ge(lr_ready, count.next(lr_ready))
            for b in (1, 2):
                acquire(b)
                for f in range(2):
                    h = 2 * (b - 1) + f
                    last = mm(D[b][:, f * T:(f + 1) * T], gla_up[0:16, h * P:(h + 1) * P], gla_lr[0:16, :])
                fill(b, last, full_dve, drained_dve)
            gla_chunk(2)
            gla_chunk(3)

            def gla_level(i):
                if i == 0:
                    pe.wait_ge(evicted, FIRST_OUT["gla_in"] + 4)
                else:
                    pe.wait_ge(level_ready, count.next(level_ready))
                for t in range(TT):
                    b = (2 * i + t) % 4
                    cols = slice(t * P, (t + 1) * P)
                    acquire(b)
                    for h in range(4):
                        k, q = (gla[:, 4 + h, cols], gla[:, h, cols]) if i == 0 else (gla_w[i % 2][:, h, cols],) * 2
                        last = mm(D[b][:, h * P:(h + 1) * P], k, q)
                    fill(b, last, full_dve, drained_dve)

            gla_level(0)
            gla_chunk(4)
            for i in range(len(LEVELS)):
                gla_level(i + 1)
                gla_chunk(5 + i)
            pe.wait_ge(level_ready, count.next(level_ready))
            acquire(0)
            for h in range(4):
                last = mm(D[0][:, h * P:(h + 1) * P], gla_w[0][:, h, 0:P], gla_w[0][:, h, P:2 * P])
            fill(0, last, full_dve, gla_scores_done)
            pe.wait_ge(evicted, FIRST_OUT["gla_in"] + 8)
            pe.wait_ge(*turn_values(gla, (8, 12), (1, 2, 3, 1)))
            pe.wait_ge(gla_scores_done, count.next(gla_scores_done))
            for b in range(4):
                acquire(b)
                for f in range(2):
                    v = slice((2 * b + f) * P, (2 * b + f + 1) * P)
                    to = D[b][:, f * T:(f + 1) * T]
                    mm(to[:, 0:P], gla_v[:, 0, v], gla_s[:, 0, b, :], f == 0, True)
                    mm(to[:, P:T], gla_v[:, 0, v], gla_s[:, 2, b, :], False, False)
                    last = mm(to[:, P:T], gla_v[:, 1, v], gla_s[:, 1, b, :], False, True)
                fill(b, last, full_act, drained_act)
            for pair in range(2):
                acquire(pair)
                for i in range(2):
                    pe.wait_ge(sq_for_pe, count.next(sq_for_pe))
                    for f in range(2):
                        last = mm(D[pair][:, i * T:(i + 1) * T], ones, sq[:, i, f * T:(f + 1) * T], f == 0 and i == 0, f == 1)
                fill(pair, last, full_dve, mean_done)
            for j in range(COUNT["gla_out"]):
                chunk("gla_out", j, j % U, B, fresh=j == 0)

            ffn(2, A)
            embedding(2, B)

            pe.wait_ge(x_gated, count.next(x_gated, 8))
            for i in range(4):
                acquire(i)
                for f in range(4):
                    last = turn(D[i][:, f * P:(f + 1) * P], x[:, (i % 2) * 4 + f, (i // 2) * P:(i // 2 + 1) * P])
                fill(i, last, full_dve, out_ready)

        @block.scalar
        def _(act):
            count = Counts(act)
            count.per_turn = {s: 2 * 16 for s in loaded}

            def fn(out, in_, func=ACT.Copy, **kw):
                return act.activation(out, in_, func, **kw)

            def split_hi(c, slot):
                if isinstance(c, int) and c >= CHUNKS:
                    return
                act.wait_ge(loaded[slot], count.next(loaded[slot], 32))
                if reused(c):
                    act.wait_ge(chunk_done, c - (U - 1))
                fn(w_hi[:, slot, :], raw[:, slot, :]).then_inc(hi_done, 1)

            def ahead(name, j, jm):
                split_hi(j + (FIRST[name] + AHEAD), (FIRST[name] + jm + AHEAD) % U)

            def out_count(name, j):
                return j + (FIRST_OUT[name] + 1)

            def loop(n, body, peel=3, function=ACT.Copy):
                count.each(n, body, peel, lambda: act.preload_act_table(function))

            def hi_parts(moving, first, src, gains=None):
                for f in range(len(src)):
                    scale = {} if gains is None else {"scale": gains[f]}
                    fn(moving[0][:, first + f, :], src[f], **scale).then_inc(x_hi_done, 1)

            def prep_pair(moving, gain, g0, src, i):
                if moving is not None:
                    hi_parts(moving, 2 * i, [src[:, 2 * i + f, :] for f in range(2)], [pcol(gain, g0 + 2 * i + f) for f in range(2)])
                pair = flat(src[:, 2 * i:2 * i + 2, :])
                if i == 0:
                    fn(sq_sum[:], pair, ACT.Square).then_inc(sq_done, 1)
                else:
                    if i == 3:
                        act.wait_ge(sq_added, count.next(sq_added, 2) - 1)
                    fn(sq[:, i % 2, :], pair, ACT.Square).then_inc(sq_done, 1)

            def prep(ready, moving, gain, g0=0, src=x):
                for i in range(KT // 2):
                    act.wait_ge(ready, count.next(ready))
                    prep_pair(moving, gain, g0, src, i)

            def rough_rstd(width=T):
                act.wait_ge(mean_done, count.next(mean_done))
                fn(rough[:, 0:width], mean_sq[:, 0:width], ACT.Ln).then_inc(act_own, count.one(act_own))
                act.wait_ge(act_own, count.sent[act_own])
                fn(rough[:, 0:width], rough[:, 0:width], ACT.Exp, scale=-0.5).then_inc(rough_done, 1)

            def exps(s, t, maps, cols):
                act.wait_ge(max_done, count.next(max_done))
                for m in range(maps):
                    last = fn(s[:, m, cols], s[:, m, cols], ACT.Exp, bias=neg_max[:, t, m:m + 1], accum_out=row_sum[:, t, m:m + 1])
                last.then_inc(exp_done, 1)

            def from_bank(out, in_):
                act.wait_ge(full_act, count.next(full_act))
                fn(out, in_).then_inc(drained_act, count.one(drained_act))

            def weigh_values(heads, per_bank, probs_t, att, after):
                for step in range(heads + 1):
                    if step < heads:
                        from_bank(probs_t[:, step % 4, 0:3 * P], D[step % 2][:, 0:3 * P])
                    if step >= 1 and (step - 1) % per_bank == per_bank - 1:
                        i = (step - 1) // per_bank
                        from_bank(flat(att[:, 2 * i:2 * i + 2, :]), D[2 + i][:])
                        act.wait_ge(drained_act, count.sent[drained_act])
                        after(i)

            def square_of(att):
                def after(i):
                    fn(sq[:, i, :], flat(att[:, 2 * i:2 * i + 2, :]), ACT.Square).then_inc(sq_for_pe, 1)
                return after

            def residual(name, moving, gain, g0=0):
                for j in range(COUNT[name]):
                    ahead(name, j, j % U)
                    act.wait_ge(evicted, out_count(name, j))
                    prep_pair(moving, gain, g0, x, j)

            split_hi(0, 0)
            act.wait_ge(par_ready, count.next(par_ready))
            prep(x_ready, A, "mix_norm_g")
            split_hi(1, 1)

            def first_body(j, jm):
                ahead("w_in", j, jm)
                if not isinstance(j, int):
                    return
                if j == 0:
                    rough_rstd()
                if j == 1:
                    for h in range(ATT_HEADS):
                        from_bank(bias_rows[:, h, :], D[h % 4][:, 0:N_DIST])
                    act.wait_ge(lam_dots_done, count.next(lam_dots_done))
                    fn(lam_exp[:], lam_dot[:], ACT.Exp).then_inc(lam_exp_done, 1)
                if j == 3:
                    prep(x_ready, B, "mem_norm_g", src=mem_t)
                if j == 4:
                    rough_rstd()

            loop(COUNT["w_in"], first_body, peel=6)

            def values_to_tokens(v):
                for i in range(4):
                    from_bank(v[:, i % 2, (i // 2) * 512:(i // 2 + 1) * 512], D[(0, 1, 2, 3)[i] if v is v_tok else (1, 2, 3, 1)[i]][:])

            def mem_values(j):
                act.wait_ge(full_act, count.next(full_act))
                for t in range(TT):
                    last = fn(mem_v[t][:, j * 2 * P:(j + 1) * 2 * P], D[STAT][:, t * 2 * P:(t + 1) * 2 * P])
                last.then_inc(drained_act, count.one(drained_act))

            act.wait_ge(got_bias, count.next(got_bias, 16))
            values_to_tokens(v_tok)
            exps(scores, 1, 8, slice(P, 3 * P))
            exps(scores, 0, 8, slice(0, P))
            for j in range(3):
                ahead("w_ck", j, j)
            weigh_values(8, 4, probs_t, att_a, square_of(att_a))
            ahead("w_ck", 3, 0)
            exps(scores, 1, 8, slice(P, 3 * P))
            exps(scores, 0, 8, slice(0, P))
            ahead("w_cv", 0, 0)
            rough_rstd()
            act.wait_ge(mixed_ready, count.next(mixed_ready))
            hi_parts(A, 0, [att_a[:, f, :] for f in range(4)], [pcol("moba_out_g", f) for f in range(4)])
            ahead("w_cv", 1, 1)
            mem_values(0)
            weigh_values(4, 2, probs_t, att_b, square_of(att_b))
            ahead("w_cv", 2, 2)
            mem_values(1)
            for b in range(2):
                rough_rstd(2 * T)
                act.wait_ge(mixed_ready, count.next(mixed_ready))
                hi_parts(A, 4 + 2 * b, [att_b[:, 2 * b + f, :] for f in range(2)], [subln_g[:, 0:1]] * 2)
            ahead("w_cv", 3, 0)
            mem_values(2)
            mem_values(3)
            residual("w_out", B, "cross_norm_g")

            for j in range(COUNT["w_cq"]):
                ahead("w_cq", j, j % U)
                if j == 0:
                    rough_rstd()
            exps(scores_mem, 0, 8, slice(0, T))
            for step in range(5):
                if step < 4:
                    from_bank(probs_t[:, step, :], D[step % 2][:])
                if step >= 1:
                    h = step - 1
                    act.wait_ge(full_act, count.next(full_act))
                    hi_parts(A, 2 * h, [D[2 + h % 2][:, d * T:(d + 1) * T] for d in range(2)])
            residual("w_co", B, "ffn_norm_g")

            def hidden_hi(j, jm, ring):
                act.wait_ge(hid_done, count.next(hid_done))
                fn(tile_at(hid_hi, j), ring[:, jm % U, :]).then_inc(hid_hi_done, 1)

            def down(layer):
                name = f"down{layer}"
                loop(COUNT[name], lambda j, jm: ahead(name, j, jm))

            def gated_body(j, jm):
                ahead("up0", j, jm)
                if isinstance(j, int) and j == 0:
                    rough_rstd()
                act.wait_ge(gate_done, count.next(gate_done))
                fn(gate_act[:, jm, :], gate_z[:, jm, :], ACT.Silu).then_inc(act_done, 1)
                if not isinstance(j, int) or j >= 1:
                    hidden_hi(j - 1, jm + 2, hid)

            loop(FT, gated_body, 3, ACT.Silu)
            hidden_hi(FT - 1, (FT - 1) % U, hid)
            down(0)
            prep(x_ready, None, None)
            rough_rstd()
            prep(x_normed, A, "mix_norm_2")

            def hy_ahead(j):
                ahead("hy_in", j, j % U)

            hy_ahead(0)
            rough_rstd()
            for j in (1, 2):
                hy_ahead(j)
            for i in range(3):
                act.wait_ge(evicted, out_count("hy_in", i))
                tiles = slice(2 * i, min(2 * i + 2, 5))
                fn(flat(hy_rot[:, tiles, :]), flat(hy[:, tiles, :]), ACT.Square).then_inc(sq_for_pe, 1)
            hy_ahead(3)
            for i in range(3):
                rough_rstd((2, 2, 1)[i] * T)
            act.wait_ge(angles_done, count.next(angles_done))
            fn(sin_t[:], rope_r[:, 0, :], ACT.Sin)
            fn(cos_t[:], rope_r[:, 1, :], ACT.Sin).then_inc(rope_done, 1)
            hy_ahead(4)
            from_bank(flat(hy_v), D[3][:, 0:T])
            hy_ahead(5)
            from_bank(hy_kswap[:], D[STAT][:, 0:T])
            for t, cols in ((1, slice(P, 3 * P)), (0, slice(0, P))):
                act.wait_ge(max_done, count.next(max_done))
                fn(hy_sink[:, t, :], hy_sink[:, t, :], ACT.Exp).then_inc(sink_done, 1)
                for m in range(8):
                    last = fn(hy_scores[:, m, cols], hy_scores[:, m, cols], ACT.Exp, bias=neg_max[:, t, m:m + 1],
                              accum_out=row_sum[:, t, m:m + 1])
                last.then_inc(exp_done, 1)
            hy_ahead(6)
            hy_ahead(7)
            weigh_values(8, 4, hy_probs_t, hy_att, lambda i: hi_parts(B, 2 * i, [hy_att[:, 2 * i + f, :] for f in range(2)]))
            hy_ahead(8)
            for i in range(2):
                act.wait_ge(mixed_ready, count.next(mixed_ready))
                hi_parts(B, 4 + 2 * i, [hy_conv[:, 2 * i + f, :] for f in range(2)])
            residual("hy_out", A, "ffn_norm_2")

            def conv_ffn(layer, moving, ple_moving):
                name = f"up{layer}"

                def column(base, tap, f, j):
                    return par[:, bass.ds(j + (base + ((layer - 1) * tap[1] + tap[0]) * 2 * FT + f * FT), 1)]

                def gelu(j, jm):
                    act.wait_ge(conv_done, count.next(conv_done))
                    fn(conv_gelu[:, jm % U, :], conv_out[:, jm % U, 0, :], ACT.Gelu).then_inc(act_done, 1)

                def body(j, jm):
                    early = isinstance(j, int)
                    ahead(name, j, jm)
                    if early and j == 0:
                        rough_rstd()
                    act.wait_ge(evicted, out_count(name, j))
                    for f in range(2):
                        last = fn(conv_out[:, jm, f, :], conv_in[:, jm, f, 2:2 + T], ACT.Identity,
                                  scale=column(CONV_COL, (2, 3), f, j), bias=column(CONVB_COL, (0, 1), f, j))
                    last.then_inc(tap_done, 1)
                    if not early or j >= 1:
                        gelu(j - 1, jm + 2)
                    if not early or j >= 2:
                        hidden_hi(j - 2, jm + 1, conv_hid)

                loop(FT, body, 4, ACT.Gelu)
                gelu(FT - 1, (FT - 1) % U)
                hidden_hi(FT - 2, (FT - 2) % U, conv_hid)
                hidden_hi(FT - 1, (FT - 1) % U, conv_hid)
                down(layer)
                act.wait_ge(full_act, count.next(full_act))
                fn(flat(p_hi), D[STAT][:]).then_inc(p_hi_done, 1)
                prep(x_ready, ple_moving, "ple_norm_2", (layer - 1) * KT)
                ahead(f"proj{layer}", 0, 0)
                for j in range(COUNT[f"gate{layer}"]):
                    ahead(f"gate{layer}", j, j % U)
                    if j == 0:
                        rough_rstd()
                    act.wait_ge(evicted, out_count(f"gate{layer}", j))
                    fn(flat(ple_sig[:, j % 2, :, :]), flat(ple_z[:, j % 2, :, :]), ACT.Sigmoid).then_inc(act_done, 1)
                    if layer == 1 and j >= 1:
                        act.wait_ge(x_gated, count.next(x_gated))
                        prep_pair(A, "mix_norm_2", KT, x, j - 1)
                if layer == 1:
                    act.wait_ge(x_gated, count.next(x_gated))
                    prep_pair(A, "mix_norm_2", KT, x, 3)

            conv_ffn(1, A, B)

            def gla_ahead(j):
                ahead("gla_in", j, j % U)

            def decays(i):
                act.wait_ge(decay_done, count.next(decay_done))
                e = flat((gla_e, gla_z)[i % 2])
                fn(e, e, ACT.Exp, scale=1.0 / 16.0).then_inc(expo_done, 1)

            gla_ahead(0)
            rough_rstd()
            gla_ahead(1)
            act.wait_ge(logit_done, count.next(logit_done))
            fn(flat(gla_e), flat(gla_e), ACT.Exp).then_inc(act_own, count.one(act_own))
            act.wait_ge(act_own, count.sent[act_own])
            fn(flat(gla_e), flat(gla_e), ACT.Ln, bias=ones[:, 0:1]).then_inc(soft_done, 1)
            gla_ahead(2)
            decays(1)
            gla_ahead(3)
            for i in range(1, len(LEVELS) + 1):
                decays(i + 1)
                gla_ahead(3 + i)
            gla_ahead(11)
            for i in range(4):
                act.wait_ge(evicted, out_count("gla_in", 8 + i))
                og = flat(gla[:, 16 + 2 * i:18 + 2 * i, :])
                last = fn(og, og, ACT.Silu)
            last.then_inc(silu_done, 1)
            values_to_tokens(gla_v)
            for b in range(4):
                from_bank(flat(gla_o[:, 2 * b:2 * b + 2, :]), D[b][:])
                if b < 2:
                    act.wait_ge(drained_act, count.sent[drained_act])
                    fn(sq[:, b, :], flat(gla_o[:, 2 * b:2 * b + 2, :]), ACT.Square).then_inc(sq_for_pe, 1)
            rough_rstd(2 * T)
            for b in (2, 3):
                fn(sq[:, b % 2, :], flat(gla_o[:, 2 * b:2 * b + 2, :]), ACT.Square).then_inc(sq_for_pe, 1)
            rough_rstd(2 * T)
            for i in range(2):
                act.wait_ge(mixed_ready, count.next(mixed_ready))
                hi_parts(B, 4 * i, [gla_o[:, 4 * i + f, :] for f in range(4)])
            residual("gla_out", A, "ffn_norm_2", KT)
            conv_ffn(2, A, B)

        @block.vector
        def _(dve):
            count = Counts(dve)

            def mul(out, a, b):
                return dve.tensor_tensor(out, a, b, ALU.mult)

            def add(out, a, b):
                return dve.tensor_tensor(out, a, b, ALU.add)

            def sub(out, a, b):
                return dve.tensor_tensor(out, a, b, ALU.subtract)

            def fused(out, a, scalar, b, op0, op1):
                return dve.scalar_tensor_tensor(out, a, scalar, b, op0, op1)

            def split_lo(c, slot):
                if isinstance(c, int) and c >= CHUNKS:
                    return
                dve.wait_ge(hi_done, c + 1)
                cols = slice(0, DVE_COLS)
                sub(w_lo[:, slot, cols], raw[:, slot, cols], w_hi[:, slot, cols].bitcast(F32)).then_inc(lo_dve, 1)

            def ahead(name, j, jm):
                split_lo(j + (FIRST[name] + AHEAD), (FIRST[name] + jm + AHEAD) % U)

            def bank_of(name, j, jm):
                dve.wait_ge(chunk_done, j + (FIRST[name] + 1))
                return as_tiles(G[(FIRST_OUT[name] + jm) % U][:])

            def lo_parts(moving, first, src, gains=None):
                for f in range(len(src)):
                    dve.wait_ge(x_hi_done, count.next(x_hi_done))
                    hi, lo = moving[0][:, first + f, :].bitcast(F32), moving[1][:, first + f, :]
                    if gains is None:
                        sub(lo, src[f], hi).then_inc(x_split, 1)
                    else:
                        fused(lo, src[f], gains[f], hi, ALU.mult, ALU.subtract).then_inc(x_split, 1)

            def prep_pair(moving, gain, g0, src, i):
                lo_parts(moving, 2 * i, [src[:, 2 * i + f, :] for f in range(2)], [pcol(gain, g0 + 2 * i + f) for f in range(2)])

            def prep(moving, gain, g0=0, src=x):
                for i in range(KT // 2):
                    prep_pair(moving, gain, g0, src, i)

            def mean(bank, features, width=T):
                dve.wait_ge(full_dve, count.next(full_dve))
                dve.tensor_scalar(mean_sq[:, 0:width], D[bank][:, 0:width], 1.0 / features, EPS, ALU.mult, ALU.add).then_inc(mean_done, count.one(mean_done))

            def refine(to, width=T):
                dve.wait_ge(rough_done, count.next(rough_done))
                m, r, n = mean_sq[:, 0:width], rough[:, 0:width], newton[:, 0:width]
                dve.wait_ge(mean_done, count.sent[mean_done])
                fused(n, m, -0.5, r, ALU.mult, ALU.mult).then_inc(dve_own, count.one(dve_own))
                dve.wait_ge(dve_own, count.sent[dve_own])
                mul(n, n, r).then_inc(dve_own, count.one(dve_own))
                dve.wait_ge(dve_own, count.sent[dve_own])
                fused(to[:, 0:width], n, 1.5, r, ALU.add, ALU.mult).then_inc(dve_own, count.one(dve_own))
                dve.wait_ge(dve_own, count.sent[dve_own])

            def token_norm(to=rstd):
                mean(STAT, DM)
                refine(to)

            def evict(name, j, jm, to, scale=rstd):
                mul(to, bank_of(name, j, jm), over(scale[:], 2)).then_inc(evicted, count.one(evicted))

            def negate_max(s, t, cols, maps=8):
                dve.tensor_reduce(row_max[:, t, 0:maps], s[:, :, cols], AX_X, ALU.max).then_inc(dve_own, count.one(dve_own))
                dve.wait_ge(dve_own, count.sent[dve_own])
                dve.tensor_scalar(neg_max[:, t, 0:maps], row_max[:, t, 0:maps], -1.0, None, ALU.mult).then_inc(max_done, 1)

            def normalise(s, t, cols, width):
                return mul(s[:, :, cols], s[:, :, cols], along(row_rec[:, t, :], width))

            def residual(name, moving, gain, g0=0):
                for j in range(COUNT[name]):
                    ahead(name, j, j % U)
                    pair = x[:, 2 * j:2 * j + 2, :]
                    add(pair, pair, bank_of(name, j, j % U)).then_inc(evicted, count.one(evicted))
                    if j >= 1:
                        prep_pair(moving, gain, g0, x, j - 1)
                dve.wait_ge(evicted, count.sent[evicted])
                prep_pair(moving, gain, g0, x, COUNT[name] - 1)

            TILE0, TILE1 = slice(0, P), slice(P, 3 * P)

            def turn_in(to):
                for b in range(4):
                    dve.wait_ge(full_dve, count.next(full_dve))
                    dve.tensor_copy(to[:, 2 * b:2 * b + 2, :], as_tiles(D[b][:])).then_inc(x_ready, count.one(x_ready))

            dve.wait_ge(full_dve, count.next(full_dve))
            dve.tensor_copy(par[:, 0:N_PARAM], D[STAT][:, 0:N_PARAM]).then_inc(dve_own, count.one(dve_own))
            dve.tensor_copy(par[:, CONV_COL:N_PCOLS], D[STAT][:, CONV_COL:N_PCOLS]).then_inc(par_ready, count.one(par_ready))
            turn_in(x)
            split_lo(0, 0)
            dve.wait_ge(dve_own, count.sent[dve_own])
            dve.wait_ge(par_ready, count.sent[par_ready])
            dve.wait_ge(x_ready, count.sent[x_ready])
            prep(A, "mix_norm_g")
            split_lo(1, 1)

            def first_body(j, jm):
                fixed = isinstance(j, int)
                ahead("w_in", j, jm)
                if fixed and j == 0:
                    token_norm()
                evict("w_in", j, jm, pair_at(qkv, j))
                if not fixed:
                    return
                if j == 1:
                    dve.wait_ge(got_small, count.next(got_small, 16 * 4))
                    mul(lam_mul[:], lam_in[:, 0::2, :], lam_in[:, 1::2, :]).then_inc(dve_own, count.one(dve_own))
                    dve.wait_ge(dve_own, count.sent[dve_own])
                    dve.tensor_reduce(lam_dot[:], lam_mul[:], AX_X, ALU.add).then_inc(lam_dots_done, 1)
                    dve.tensor_scalar(subln_g[:], pcol("diff_subln_g"), 1.0 - LAMBDA_INIT, None, ALU.mult).then_inc(dve_own, count.one(dve_own))
                if j == 2:
                    dve.wait_ge(lam_exp_done, count.next(lam_exp_done))
                    fused(neg_lam[:], lam_exp[:, 1:2], LAMBDA_INIT, lam_exp[:, 0:1], ALU.subtract, ALU.subtract).then_inc(dve_own, count.one(dve_own))
                if j == 3:
                    dve.wait_ge(got_mem, count.next(got_mem, 16))
                    turn_in(mem_t)
                if j == 4:
                    dve.wait_ge(x_ready, count.sent[x_ready])
                    prep(B, "mem_norm_g", src=mem_t)
                    token_norm(rstd_mem)

            count.each(COUNT["w_in"], first_body, peel=6)

            def score_tiles(s, bias):
                for t, cols in ((1, TILE1), (0, TILE0)):
                    for b in range(4 if t else 2):
                        maps = maps_of(b, t)
                        dve.wait_ge(full_dve, count.next(full_dve))
                        fused(s[:, maps.start:maps.stop:2, cols], as_tiles(D[b][:], (t + 1) * P), QK_SCALE,
                                        bias(maps, slice(0 if t else P, 2 * P)), ALU.mult, ALU.add).then_inc(drained_dve, count.one(drained_dve))
                    dve.wait_ge(drained_dve, count.sent[drained_dve])
                    yield t, cols

            def mem_keys(j):
                ahead("w_ck", j, j % U)
                evict("w_ck", j, j % U, pair_at(mem_k, j), rstd_mem)

            def mem_values(j):
                ahead("w_cv", j, j % U)
                evict("w_cv", j, j % U, mem_v_t[:, j % 2, :, :], rstd_mem)

            def reciprocals():
                dve.wait_ge(exp_done, count.next(exp_done, 2))
                dve.reciprocal(row_rec[:], row_sum[:]).then_inc(dve_own, count.one(dve_own))
                dve.wait_ge(dve_own, count.sent[dve_own])

            dve.wait_ge(got_bias, count.next(got_bias, 16))
            for t, cols in score_tiles(scores, lambda maps, c: bias_tab[:, maps.start:maps.stop:2, c]):
                negate_max(scores, t, cols)
            mem_keys(0)
            reciprocals()
            normalise(scores, 1, TILE1, 2 * P).then_inc(dve_own, count.one(dve_own))
            normalise(scores, 0, TILE0, P).then_inc(probs_done, 1)
            mem_keys(1)
            mem_keys(2)
            for t, cols in score_tiles(scores, lambda maps, c: bias_tab[:, 8 + maps.start // 2:8 + maps.stop // 2, c]):
                negate_max(scores, t, cols)
            mem_keys(3)
            reciprocals()
            second = row_rec[:, :, 1::2]
            dve.tensor_scalar(second, second, neg_lam[:, 0:1], None, ALU.mult).then_inc(dve_own, count.one(dve_own))
            dve.wait_ge(dve_own, count.sent[dve_own])
            normalise(scores, 1, TILE1, 2 * P).then_inc(dve_own, count.one(dve_own))
            normalise(scores, 0, TILE0, P).then_inc(dve_own, count.one(dve_own))
            dve.wait_ge(dve_own, count.sent[dve_own])
            add(scores[:, 0:4, :], scores[:, 0::2, :], scores[:, 1::2, :]).then_inc(probs_done, 1)
            mem_values(0)
            mean(STAT, 4 * P)
            refine(rstd)
            mul(att_a[:], att_a[:], over(rstd[:], 4)).then_inc(mixed_ready, count.one(mixed_ready))
            mem_values(1)
            dve.wait_ge(mixed_ready, count.sent[mixed_ready])
            lo_parts(A, 0, [att_a[:, f, :] for f in range(4)], [pcol("moba_out_g", f) for f in range(4)])
            mem_values(2)
            for b in range(2):
                mean(b, P, 2 * T)
                refine(mean_sq, 2 * T)
                tiles = att_b[:, 2 * b:2 * b + 2, :]
                mul(tiles, tiles, as_tiles(mean_sq[:])).then_inc(mixed_ready, count.one(mixed_ready))
                dve.wait_ge(mixed_ready, count.sent[mixed_ready])
            mem_values(3)
            lo_parts(A, 4, [att_b[:, f, :] for f in range(4)], [subln_g[:, 0:1]] * 4)
            residual("w_out", B, "cross_norm_g")

            for j in range(COUNT["w_cq"]):
                ahead("w_cq", j, j % U)
                if j == 0:
                    token_norm()
                evict("w_cq", j, j % U, pair_at(q_mem, j))
            for b in range(4):
                dve.wait_ge(full_dve, count.next(full_dve))
                dve.tensor_scalar(scores_mem[:, 2 * b:2 * b + 2, :], as_tiles(D[b][:]), 0.0625, None, ALU.mult).then_inc(drained_dve, count.one(drained_dve))
            dve.wait_ge(drained_dve, count.sent[drained_dve])
            negate_max(scores_mem, 0, slice(0, T))
            dve.wait_ge(exp_done, count.next(exp_done))
            dve.reciprocal(row_rec[:, 0, :], row_sum[:, 0, :]).then_inc(dve_own, count.one(dve_own))
            dve.wait_ge(dve_own, count.sent[dve_own])
            normalise(scores_mem, 0, slice(0, T), T).then_inc(probs_done, 1)
            for h in range(4):
                dve.wait_ge(x_hi_done, count.taken[x_hi_done] + 2)
                lo_parts(A, 2 * h, [D[2 + h % 2][:, d * T:(d + 1) * T] for d in range(2)])
            residual("w_co", B, "ffn_norm_g")

            def hidden_lo(j, jm, ring):
                dve.wait_ge(hid_hi_done, count.next(hid_hi_done))
                dve.wait_ge(hid_done, count.sent[hid_done])
                sub(tile_at(hid_lo, j), ring[:, jm % U, :], tile_at(hid_hi, j).bitcast(F32)).then_inc(hid_split, 1)

            def down(layer):
                name = f"down{layer}"
                count.each(COUNT[name], lambda j, jm: ahead(name, j, jm))
                for b in range(4):
                    if b < 3:
                        dve.wait_ge(full_dve, count.next(full_dve))
                    else:
                        dve.wait_ge(chunk_done, FIRST[name] + COUNT[name])
                    pair = x[:, 2 * b:2 * b + 2, :]
                    add(pair, pair, as_tiles(D[b][:])).then_inc(x_ready, count.one(x_ready))
                dve.wait_ge(x_ready, count.sent[x_ready])

            def gated_hid(j, jm):
                dve.wait_ge(act_done, count.next(act_done))
                dve.wait_ge(evicted, j + (FIRST_OUT["up0"] + 1))
                mul(hid[:, jm % U, :], gate_act[:, jm % U, :], up_z[:, jm % U, :]).then_inc(hid_done, count.one(hid_done))

            def gated_body(j, jm):
                early = isinstance(j, int)
                ahead("up0", j, jm)
                if early and j == 0:
                    token_norm()
                z = bank_of("up0", j, jm)
                mul(gate_z[:, jm, :], z[:, 0, :], rstd[:]).then_inc(gate_done, 1)
                mul(up_z[:, jm, :], z[:, 1, :], rstd[:]).then_inc(evicted, count.one(evicted))
                if not early or j >= 1:
                    gated_hid(j - 1, jm + 2)
                if not early or j >= 2:
                    hidden_lo(j - 2, jm + 1, hid)

            count.each(FT, gated_body)
            gated_hid(FT - 1, (FT - 1) % U)
            hidden_lo(FT - 2, (FT - 2) % U, hid)
            hidden_lo(FT - 1, (FT - 1) % U, hid)
            down(0)
            token_norm()
            for i in range(KT // 2):
                for f in (2 * i, 2 * i + 1):
                    last = fused(x[:, f, :], x[:, f, :], pcol("final_norm_g", f), rstd[:], ALU.mult, ALU.mult)
                    if f == 2 * i:
                        last.then_inc(dve_own, count.one(dve_own))
                last.then_inc(x_normed, count.one(x_normed))
            dve.wait_ge(x_normed, count.sent[x_normed])
            prep(A, "mix_norm_2")

            def hy_evict(j):
                ahead("hy_in", j, j % U)
                if j == 0:
                    token_norm()
                evict("hy_in", j, j % U, hy[:, 2 * j:2 * j + 2, :])

            def rope_angles():
                two_pi, magic = 2.0 * math.pi, 1.5 * 2.0 ** 23
                c1 = 6.28125
                c2 = float(np.round((two_pi - c1) * 2.0 ** 21) * 2.0 ** -21)
                c3 = two_pi - c1 - c2
                dve.wait_ge(got_rope, count.next(got_rope, 16))
                dve.tensor_copy(rope_a[:], rope_i[:]).then_inc(dve_own, count.one(dve_own))
                dve.wait_ge(dve_own, count.sent[dve_own])
                mul(rope_a[:], rope_a[:], inv_freq.broadcast_to([P, T])).then_inc(dve_own, count.one(dve_own))
                dve.wait_ge(dve_own, count.sent[dve_own])
                for i, shift in enumerate((0.0, 0.5 * math.pi)):
                    r = rope_r[:, i, :]
                    dve.tensor_scalar(rope_n[:], rope_a[:], shift, 1.0 / two_pi, ALU.add, ALU.mult).then_inc(dve_own, count.one(dve_own))
                    dve.wait_ge(dve_own, count.sent[dve_own])
                    dve.tensor_scalar(rope_n[:], rope_n[:], magic, None, ALU.add).then_inc(dve_own, count.one(dve_own))
                    dve.wait_ge(dve_own, count.sent[dve_own])
                    dve.tensor_scalar(rope_n[:], rope_n[:], magic, None, ALU.subtract).then_inc(dve_own, count.one(dve_own))
                    dve.wait_ge(dve_own, count.sent[dve_own])
                    fused(r, rope_n[:], -c1, rope_a[:], ALU.mult, ALU.add).then_inc(dve_own, count.one(dve_own))
                    dve.wait_ge(dve_own, count.sent[dve_own])
                    fused(r, rope_n[:], -c2, r, ALU.mult, ALU.add).then_inc(dve_own, count.one(dve_own))
                    dve.wait_ge(dve_own, count.sent[dve_own])
                    fused(r, rope_n[:], -c3, r, ALU.mult, ALU.add).then_inc(dve_own, count.one(dve_own))
                    dve.wait_ge(dve_own, count.sent[dve_own])
                    if shift:
                        dve.tensor_scalar(r, r, shift, None, ALU.add).then_inc(dve_own, count.one(dve_own))
                        dve.wait_ge(dve_own, count.sent[dve_own])
                    limit = float(np.nextafter(np.float32(math.pi), np.float32(0)))
                    last = dve.tensor_scalar(r, r, limit, -limit, ALU.min, ALU.max)
                    if i == 0:
                        last.then_inc(dve_own, count.one(dve_own))
                last.then_inc(angles_done, 1)

            dve.memset(hy_conv_in[:, :, 0:2], 0.0).then_inc(dve_own, count.one(dve_own))
            hy_evict(0)
            hy_evict(1)
            rope_angles()
            hy_evict(2)
            hy_evict(3)
            tiles_of = (slice(0, 2), slice(2, 4), slice(4, 5))
            dve.wait_ge(evicted, count.sent[evicted])
            for i in range(3):
                width = (2, 2, 1)[i] * T
                mean(i, 64, width)
                refine(mean_sq, width)
                for f in range(tiles_of[i].start, tiles_of[i].stop):
                    gain = pcol("hy_k_norm_2" if f == 4 else "hy_q_norm_2")
                    at_f = (f - 2 * i) * T
                    last = fused(hy_qk[:, f, :], hy[:, f, :], gain, mean_sq[:, at_f:at_f + T], ALU.mult, ALU.mult)
                    if f + 1 < tiles_of[i].stop:
                        last.then_inc(dve_own, count.one(dve_own))
                last.then_inc(qk_normed, count.one(qk_normed))
                dve.wait_ge(qk_normed, count.sent[qk_normed])
            hy_evict(4)
            dve.wait_ge(rope_done, count.next(rope_done))
            for i in range(3):
                tiles = tiles_of[i]
                dve.wait_ge(full_dve, count.next(full_dve))
                n = tiles.stop - tiles.start
                mul(hy_rot[:, tiles, :], as_tiles(D[i][:, 0:n * T]), over(sin_t[:], n)).then_inc(drained_dve, count.one(drained_dve))
            mul(hy_qk[:], hy_qk[:], over(cos_t[:], 5)).then_inc(dve_own, count.one(dve_own))
            dve.wait_ge(dve_own, count.sent[dve_own])
            dve.wait_ge(drained_dve, count.sent[drained_dve])
            add(hy_qk[:], hy_qk[:], hy_rot[:]).then_inc(qk_rotated, 1)
            hy_evict(5)
            for t, cols in score_tiles(hy_scores, lambda maps, c: over(window[:, c], len(maps))):
                dve.tensor_reduce(row_max[:, t, :], hy_scores[:, :, cols], AX_X, ALU.max).then_inc(dve_own, count.one(dve_own))
                dve.wait_ge(dve_own, count.sent[dve_own])
                dve.tensor_tensor(row_max[:, t, :], row_max[:, t, :], sinks[:], ALU.max).then_inc(dve_own, count.one(dve_own))
                dve.wait_ge(dve_own, count.sent[dve_own])
                dve.tensor_scalar(neg_max[:, t, :], row_max[:, t, :], -1.0, None, ALU.mult).then_inc(dve_own, count.one(dve_own))
                sub(hy_sink[:, t, :], sinks[:], row_max[:, t, :]).then_inc(max_done, 1)
            hy_evict(6)
            dve.wait_ge(exp_done, count.next(exp_done, 2))
            dve.wait_ge(sink_done, count.next(sink_done, 2))
            add(row_sum[:], row_sum[:], hy_sink[:]).then_inc(dve_own, count.one(dve_own))
            dve.wait_ge(dve_own, count.sent[dve_own])
            dve.reciprocal(row_rec[:], row_sum[:]).then_inc(dve_own, count.one(dve_own))
            dve.wait_ge(dve_own, count.sent[dve_own])
            normalise(hy_scores, 1, TILE1, 2 * P).then_inc(dve_own, count.one(dve_own))
            normalise(hy_scores, 0, TILE0, P).then_inc(probs_done, 1)
            hy_evict(7)
            lo_parts(B, 0, [hy_att[:, f, :] for f in range(4)])
            hy_evict(8)
            dve.wait_ge(evicted, count.sent[evicted])
            mul(hy_conv_in[:, :, 2:2 + T], hy[:, 10:14, :], hy[:, 14:18, :]).then_inc(dve_own, count.one(dve_own))
            dve.wait_ge(dve_own, count.sent[dve_own])
            for tap in range(3):
                for f in range(4):
                    w = pcol("hy_conv_w_2", tap * 4 + f)
                    src = hy_conv_in[:, f, tap:tap + T]
                    if tap == 0:
                        dve.tensor_scalar(hy_conv[:, f, :], src, w, None, ALU.mult).then_inc(dve_own, count.one(dve_own))
                    else:
                        fused(hy_conv[:, f, :], src, w, hy_conv[:, f, :], ALU.mult, ALU.add).then_inc(dve_own, count.one(dve_own))
                dve.wait_ge(dve_own, count.sent[dve_own])
            for i in range(2):
                tiles = hy_conv[:, 2 * i:2 * i + 2, :]
                mul(tiles, tiles, hy[:, 6 + 2 * i:8 + 2 * i, :]).then_inc(mixed_ready, count.one(mixed_ready))
            dve.wait_ge(mixed_ready, count.sent[mixed_ready])
            lo_parts(B, 4, [hy_conv[:, f, :] for f in range(4)])
            residual("hy_out", A, "ffn_norm_2")

            def conv_ffn(layer, ple_moving):
                name = f"up{layer}"

                def tap_column(tap, f, j):
                    return par[:, bass.ds(j + (CONV_COL + ((layer - 1) * 3 + tap) * 2 * FT + f * FT), 1)]

                def taps(j, jm):
                    m = jm % U
                    dve.wait_ge(tap_done, count.next(tap_done))
                    dve.wait_ge(evicted, j + (FIRST_OUT[name] + 1))
                    for f in range(2):
                        o = conv_out[:, m, f, :]
                        fused(o, conv_in[:, m, f, 1:1 + T], tap_column(1, f, j), o, ALU.mult, ALU.add).then_inc(dve_own, count.one(dve_own))
                    dve.wait_ge(dve_own, count.sent[dve_own])
                    for f in range(2):
                        o = conv_out[:, m, f, :]
                        last = fused(o, conv_in[:, m, f, 0:T], tap_column(0, f, j), o, ALU.mult, ALU.add)
                        if f == 0:
                            last.then_inc(conv_done, 1)
                        else:
                            last.then_inc(dve_own, count.one(dve_own))

                def conv_hidden(j, jm):
                    dve.wait_ge(act_done, count.next(act_done))
                    dve.wait_ge(dve_own, count.sent[dve_own])
                    mul(conv_hid[:, jm % U, :], conv_gelu[:, jm % U, :], conv_out[:, jm % U, 1, :]).then_inc(hid_done, count.one(hid_done))

                def body(j, jm):
                    early = isinstance(j, int)
                    ahead(name, j, jm)
                    if early and j == 0:
                        token_norm()
                    mul(conv_in[:, jm, :, 2:2 + T], bank_of(name, j, jm), over(rstd[:], 2)).then_inc(evicted, count.one(evicted))
                    if not early or j >= 2:
                        conv_hidden(j - 2, jm + 1)
                    if not early or j >= 3:
                        hidden_lo(j - 3, jm, conv_hid)
                    if not early or j >= 1:
                        taps(j - 1, jm + 2)

                dve.memset(conv_in[:, :, :, 0:2], 0.0).then_inc(dve_own, count.one(dve_own))
                count.each(FT, body, 4)
                m = FT % U
                conv_hidden(FT - 2, m + 1)
                hidden_lo(FT - 3, m, conv_hid)
                taps(FT - 1, m + 2)
                conv_hidden(FT - 1, m + 2)
                hidden_lo(FT - 2, m + 1, conv_hid)
                hidden_lo(FT - 1, m + 2, conv_hid)
                down(layer)
                dve.wait_ge(p_hi_done, count.next(p_hi_done))
                sub(flat(p_lo), D[STAT][:], flat(p_hi).bitcast(F32)).then_inc(p_split, 1)
                prep(ple_moving, "ple_norm_2", (layer - 1) * KT)
                gate = f"gate{layer}"
                ahead(f"proj{layer}", 0, 0)

                def finish(j):
                    dve.wait_ge(act_done, count.next(act_done))
                    m, pair = ple_mul[:, j % 2, :, :], x[:, 2 * j:2 * j + 2, :]
                    mul(m, ple_sig[:, j % 2, :, :], as_tiles(D[j][:])).then_inc(drained_dve, count.one(drained_dve))
                    dve.wait_ge(drained_dve, count.sent[drained_dve])
                    add(pair, pair, m).then_inc(x_gated, count.one(x_gated))

                for j in range(COUNT[gate]):
                    ahead(gate, j, j % U)
                    if j == 0:
                        token_norm()
                    evict(gate, j, j % U, ple_z[:, j % 2, :, :])
                    if j >= 1:
                        finish(j - 1)
                    if layer == 1 and j >= 2:
                        prep_pair(A, "mix_norm_2", KT, x, j - 2)
                finish(3)
                if layer == 1:
                    dve.wait_ge(x_gated, count.sent[x_gated])
                    prep_pair(A, "mix_norm_2", KT, x, 2)
                    prep_pair(A, "mix_norm_2", KT, x, 3)

            conv_ffn(1, B)

            def gla_evict(j):
                ahead("gla_in", j, j % U)
                if j == 0:
                    token_norm()
                if j < 2:
                    fused(gla[:, 2 * j:2 * j + 2, :], bank_of("gla_in", j, j % U), float(P) ** -0.5, over(rstd[:], 2),
                                    ALU.mult, ALU.mult).then_inc(evicted, count.one(evicted))
                else:
                    evict("gla_in", j, j % U, gla[:, 2 * j:2 * j + 2, :])

            sums = flat(gla_g)

            def blocks(ap, level):
                return flat(ap).rearrange("p (b h t) -> p b h t", h=2, t=level)

            def exponents(i):
                e = (gla_e, gla_z)[i % 2]
                if i <= len(LEVELS):
                    level = LEVELS[i - 1]
                    s, to = blocks(gla_g, level), blocks(e, level)
                    n = 4 * T // (2 * level)
                    middle = s[:, :, 0, level - 1:level].broadcast_to([P, n, level])
                    if level == 64:
                        dve.tensor_copy(to[:, :, 1, :], s[:, :, 1, :]).then_inc(dve_own, count.one(dve_own))
                    else:
                        sub(to[:, :, 1, :], s[:, :, 1, :], middle).then_inc(dve_own, count.one(dve_own))
                    sub(to[:, :, 0, :], middle, s[:, :, 0, :]).then_inc(decay_done, 1)
                    return
                s4 = gla_g[:].rearrange("p h (c t) -> p h c t", t=64)
                e4 = e[:].rearrange("p h (c t) -> p h c t", t=64)
                for c in range(2):
                    sub(e4[:, :, c, :], s4[:, :, c, 63:64].broadcast_to([P, 4, 64]), s4[:, :, c, :]).then_inc(dve_own, count.one(dve_own))
                dve.wait_ge(dve_own, count.sent[dve_own])
                add(e4[:, :, 0, :], e4[:, :, 0, :], s4[:, :, 1, 63:64].broadcast_to([P, 4, 64])).then_inc(dve_own, count.one(dve_own))
                dve.tensor_copy(e4[:, :, 2, :], s4[:, :, 2, :]).then_inc(dve_own, count.one(dve_own))
                add(e4[:, :, 3, :], s4[:, :, 3, :], s4[:, :, 2, 63:64].broadcast_to([P, 4, 64])).then_inc(decay_done, 1)

            def decayed(i):
                e = (gla_e, gla_z)[i % 2]
                dve.wait_ge(expo_done, count.next(expo_done))
                level = LEVELS[i - 1] if i <= len(LEVELS) else P
                to, ev = blocks(gla_w[i % 2], level), blocks(e, level)
                q, k = (flat(gla[:, f:f + 4, :]).rearrange("p (b h t) -> p b h t", h=2, t=level) for f in (0, 4))
                mul(to[:, :, 0, :], k[:, :, 0, :], ev[:, :, 0, :]).then_inc(dve_own, count.one(dve_own))
                mul(to[:, :, 1, :], q[:, :, 1, :], ev[:, :, 1, :]).then_inc(level_ready, count.one(level_ready))

            def keep_level(i):
                dve.wait_ge(drained_dve, count.sent[drained_dve])
                for t in range(TT):
                    dve.wait_ge(full_dve, count.next(full_dve))
                    dve.copy_predicated(gla_s[:, t, :, :], over(level_mask[:, i, :], 4),
                                                  as_tiles(D[(2 * i + t) % 4][:], P)).then_inc(drained_dve, count.one(drained_dve))

            dve.wait_ge(got_gla, count.next(got_gla, 16 * 3))
            dve.tensor_copy(flat(level_mask), level_mask_f[:]).then_inc(dve_own, count.one(dve_own))
            g0 = PCOL["mix_norm_2"] + KT
            mul(gla_wlr[:], gla_wlr[:], along(par[:, g0:g0 + KT], 16)).then_inc(lr_scaled, 1)
            restart = flat(gla_w[0])
            dve.memset(restart, 1.0).then_inc(dve_own, count.one(dve_own))
            dve.memset(gla_s[:], 0.0).then_inc(dve_own, count.one(dve_own))
            dve.wait_ge(dve_own, count.sent[dve_own])
            dve.memset(restart[:, 0::64], 0.0).then_inc(dve_own, count.one(dve_own))
            gla_evict(0)
            dve.wait_ge(full_dve, count.next(full_dve))
            mul(gla_lr[0:16, :], D[0][0:16, 0:T], rstd[0:16, :]).then_inc(lr_ready, 1)
            gla_evict(1)
            for b in range(2):
                dve.wait_ge(full_dve, count.next(full_dve))
                for f in range(2):
                    h = 2 * b + f
                    last = dve.tensor_scalar(gla_z[:, h, :], D[1 + b][:, f * T:(f + 1) * T], pcol("gla_gate_bias_2", h), None, ALU.add)
                    if f == 0:
                        last.then_inc(dve_own, count.one(dve_own))
                last.then_inc(drained_dve, count.one(drained_dve))
            dve.wait_ge(dve_own, count.sent[dve_own])
            dve.wait_ge(drained_dve, count.sent[drained_dve])
            fused(flat(gla_e), flat(gla_z), -1.0, flat(gla_z), ALU.mult, ALU.min).then_inc(logit_done, 1)
            gla_evict(2)
            dve.wait_ge(soft_done, count.next(soft_done))
            fused(flat(gla_z), flat(gla_z), 0.0, flat(gla_e), ALU.min, ALU.subtract).then_inc(dve_own, count.one(dve_own))
            dve.wait_ge(dve_own, count.sent[dve_own])
            dve.tensor_tensor_scan(sums, restart, flat(gla_z), 0.0, ALU.mult, ALU.add).then_inc(dve_own, count.one(dve_own))
            dve.wait_ge(dve_own, count.sent[dve_own])
            exponents(1)
            gla_evict(3)
            dve.wait_ge(evicted, count.sent[evicted])
            for i in range(1, len(LEVELS) + 1):
                if i > 1:
                    dve.wait_ge(level_ready, count.sent[level_ready])
                exponents(i + 1)
                decayed(i)
                keep_level(i - 1)
                gla_evict(3 + i)
            decayed(len(LEVELS) + 1)
            keep_level(len(LEVELS))
            gla_evict(11)
            dve.wait_ge(full_dve, count.next(full_dve))
            dve.tensor_copy(gla_s[:, 2, :, :], as_tiles(D[0][:], P)).then_inc(gla_scores_done, 1)
            dve.wait_ge(silu_done, count.next(silu_done))
            for pair in range(2):
                mean(pair, 2 * P, 2 * T)
                refine(mean_sq, 2 * T)
                for f in range(4):
                    o = gla_o[:, 4 * pair + f, :]
                    scale = mean_sq[:, (f // 2) * T:(f // 2 + 1) * T]
                    fused(o, o, pcol("gla_o_norm_2", f % 2), scale, ALU.mult, ALU.mult).then_inc(dve_own, count.one(dve_own))
                dve.wait_ge(dve_own, count.sent[dve_own])
                o = gla_o[:, 4 * pair:4 * pair + 4, :]
                mul(o, o, gla[:, 16 + 4 * pair:20 + 4 * pair, :]).then_inc(mixed_ready, count.one(mixed_ready))
            dve.wait_ge(mixed_ready, count.sent[mixed_ready])
            lo_parts(B, 0, [gla_o[:, f, :] for f in range(8)])
            residual("gla_out", A, "ffn_norm_2", KT)
            conv_ffn(2, B)

            for i in range(4):
                dve.wait_ge(full_dve, count.next(full_dve))
                dve.tensor_copy(x_out[:, i // 2, (i % 2) * 512:(i % 2 + 1) * 512], D[i][:]).then_inc(out_ready, 1)

        @block.gpsimd
        def _(pool):
            count = Counts(pool)

            def split_lo(c, slot):
                if isinstance(c, int) and c >= CHUNKS:
                    return
                pool.wait_ge(hi_done, c + 1)
                cols = slice(DVE_COLS, CHUNK)
                pool.tensor_tensor(w_lo[:, slot, cols], raw[:, slot, cols], w_hi[:, slot, cols].bitcast(F32), ALU.subtract).then_inc(lo_pool, 1)

            def ahead(name, j, jm):
                split_lo(j + (FIRST[name] + AHEAD), (FIRST[name] + jm + AHEAD) % U)

            def add_squares(i):
                pool.wait_ge(sq_done, count.next(sq_done))
                if i == 0:
                    return
                if i > 1:
                    pool.wait_ge(sq_added, count.sent[sq_added])
                total = pool.tensor_tensor(sq_sum[:], sq_sum[:], sq[:, i % 2, :], ALU.add)
                if i == 3:
                    total.then_inc(sq_total, 1)
                else:
                    total.then_inc(sq_added, count.one(sq_added))

            def all_squares():
                for i in range(KT // 2):
                    add_squares(i)

            def residual(name):
                for j in range(COUNT[name]):
                    ahead(name, j, j % U)
                    add_squares(j)

            def stream(name):
                count.each(COUNT[name], lambda j, jm: ahead(name, j, jm))

            pool.memset(table[N_BUCKETS:N_BUCKETS + 1, :], MASKED).then_inc(masked_row, count.one(masked_row))
            pool.wait_ge(masked_row, count.sent[masked_row])
            split_lo(0, 0)
            all_squares()
            split_lo(1, 1)

            def first_body(j, jm):
                ahead("w_in", j, jm)
                if isinstance(j, int) and j == 3:
                    all_squares()

            count.each(COUNT["w_in"], first_body, peel=6)
            stream("w_ck")
            stream("w_cv")
            residual("w_out")
            stream("w_cq")
            residual("w_co")
            stream("up0")
            stream("down0")
            all_squares()
            all_squares()
            stream("hy_in")
            residual("hy_out")
            for layer in (1, 2):
                stream(f"up{layer}")
                stream(f"down{layer}")
                all_squares()
                stream(f"proj{layer}")
                stream(f"gate{layer}")
                if layer == 1:
                    all_squares()
                    stream("gla_in")
                    residual("gla_out")


def constants():
    c = np.zeros((P, N_CONST), np.float32)
    i = np.arange(P)
    c[i, C_IDENT + i] = 1.0
    c[:, C_ONES:C_ONES + P] = 1.0
    c[:, C_HALF:C_HALF + P] = (i[:, None] // 64 == i[None, :] // 64)
    low = i[i % 64 < 32]
    c[low + 32, C_ROT + low] = -1.0
    c[low, C_ROT + low + 32] = 1.0
    c[(i + 64) % P, C_SWAP + i] = 1.0
    dist = P + i[:, None] - np.arange(2 * P)[None, :]
    c[:, C_WIN:C_WIN + 2 * P] = np.where((dist >= 0) & (dist < P), 0.0, MASKED)
    exponent = -np.arange(0, 64, 2, dtype=np.float32) / np.float32(64)
    c[:, C_FREQ] = np.power(np.float32(10000.0), exponent)[i % 32]
    dist = N_DIST - P - 1 - np.arange(N_DIST)
    exact = N_BUCKETS // 2
    ratio = np.log(np.maximum(dist, exact).astype(np.float32) / np.float32(exact)) / np.float32(math.log(P / exact))
    large = np.minimum(exact + (ratio * np.float32(N_BUCKETS - exact)).astype(np.int32), N_BUCKETS - 1)
    bucket = np.where(dist < 0, N_BUCKETS, np.where(dist < exact, dist, large))
    onehot = np.zeros((N_BUCKETS + 1, N_DIST), np.float32)
    onehot[bucket, np.arange(N_DIST)] = 1.0
    s, t = i[:, None], i[None, :]
    masks = [s == t] + [(s // (2 * n) == t // (2 * n)) & (s % (2 * n) < n) & (t % (2 * n) >= n) for n in LEVELS]
    return {"const": c, "onehot": onehot, "level_mask": np.concatenate(masks, axis=1).astype(np.float32)}


def kernel(**inputs):
    import concourse.bacc as bacc
    from concourse.bass_utils import run_bass_kernel_spmd

    arrays = {name: np.ascontiguousarray(np.asarray(a)) for name, a in inputs.items()}
    arrays.update(constants())
    nc = bacc.Bacc("TRN2", target_bir_lowering=False, num_devices=1)
    io = {name: nc.dram_tensor(name, a.shape, mybir.dt.from_np(a.dtype), kind="ExternalInput").ap() for name, a in arrays.items()}
    out = nc.dram_tensor("out", (1, T, DM), F32, kind="ExternalOutput").ap()
    program(nc, io, out)
    r = run_bass_kernel_spmd(nc, [arrays], core_ids=[0])
    return r.results[0]["out"]
```

```python
from contextlib import ExitStack
import math

import numpy as np
import concourse.bass as bass
from concourse import mybir

F32 = mybir.dt.float32
F32R = mybir.dt.float32r
I32 = mybir.dt.int32
U8 = mybir.dt.uint8
ALU = mybir.AluOpType
ACT = mybir.ActivationFunctionType
AX_X = mybir.AxisListType.X

P = 128
T = 256
TT = T // P
DM = 1024
KT = DM // P
FF = 2816
FT = FF // P
U = 3
CHUNK = 16 * P
DVE_COLS = 1024
AHEAD = 2
EPS = 1e-6
MASKED = -1e30
QK_SCALE = 0.125
LAMBDA_INIT = 0.8 - 0.6 * math.exp(-0.3 * 0)
N_DIST = 384
N_BUCKETS = 32
ATT_HEADS = 12
LEVELS = (64, 32, 16, 8, 4, 2, 1)
VALUE_TILES = ((8, 0), (8, 1), (12, 0), (12, 1))

C_IDENT, C_ONES, C_HALF, C_ROT, C_SWAP, C_WIN, C_FREQ = 0, 128, 256, 384, 512, 640, 896
N_CONST = 897

PARAMS = [("mix_norm_g", 8), ("moba_out_g", 4), ("diff_subln_g", 1), ("cross_norm_g", 8), ("mem_norm_g", 8),
          ("ffn_norm_g", 8), ("final_norm_g", 8), ("mix_norm_2", 16), ("ffn_norm_2", 16), ("ple_norm_2", 16),
          ("gla_o_norm_2", 2), ("gla_gate_bias_2", 4), ("hy_conv_w_2", 12), ("hy_q_norm_2", 1), ("hy_k_norm_2", 1)]
PCOL = {}
_n = 0
for _name, _rows in PARAMS:
    PCOL[_name] = _n
    _n += _rows
N_PARAM = _n
CONV_COL = N_PARAM
N_CONV = 2 * 3 * 2 * FT
CONVB_COL = CONV_COL + N_CONV
N_PCOLS = CONVB_COL + 2 * 2 * FT

PHASES = [("w_in", 12, 0), ("w_ck", 4, 0), ("w_out", 4, 0), ("w_cq", 4, 0), ("w_cv", 4, 0), ("w_co", 4, 0),
          ("up0", FT, 0), ("down0", FT // 2, 1), ("hy_in", 9, 0), ("hy_out", 4, 0), ("up1", FT, 0),
          ("down1", FT // 2, 1), ("proj1", 1, 1), ("gate1", 4, 0), ("gla_in", 12, 0), ("gla_out", 4, 0),
          ("up2", FT, 0), ("down2", FT // 2, 1), ("proj2", 1, 1), ("gate2", 4, 0)]
W_IN_Q = 6
FIRST, COUNT, FIRST_OUT = {}, {}, {}
_c = _o = 0
for _name, _k, _over_k in PHASES:
    FIRST[_name], COUNT[_name], FIRST_OUT[_name] = _c, _k, _o
    _c += _k
    _o += 0 if _over_k else _k
CHUNKS = _c
PHASE_OVER_K = {_name: _over_k for _name, _, _over_k in PHASES}


class Counts:

    def __init__(self, engine):
        self.engine, self.taken, self.sent = engine, {}, {}
        self.per_turn = {}

    def next(self, sem, events=1):
        self.taken[sem] = self.taken.get(sem, 0) + events
        return self.taken[sem]

    def one(self, sem):
        self.sent[sem] = self.sent.get(sem, 0) + 1
        return 1

    def each(self, n, body, peel=3, ahead_of_loop=None):
        def counts():
            return [(d, s, v) for d in (self.taken, self.sent) for s, v in d.items()]

        peel = min(peel, n)
        for j in range(peel):
            before = {(id(d), s): v for d, s, v in counts()}
            body(j, j % U)
        turns = (n - peel) // U
        if turns < 2:
            turns = 0
        if turns:
            start = [(d, s, v, v - before.get((id(d), s), 0)) for d, s, v in counts() if s not in self.per_turn]
            start_turn = {s: self.taken[s] for s in self.per_turn}
            if ahead_of_loop:
                ahead_of_loop()
            with self.engine.Fori(0, turns) as turn:
                for s, v in start_turn.items():
                    self.taken[s] = turn * self.per_turn[s] + v
                for u in range(U):
                    for d, s, v, step in start:
                        if step:
                            d[s] = turn * (U * step) + (v + u * step)
                    body(turn * U + (peel + u), (peel + u) % U)
            for d, s, v, step in start:
                d[s] = v + turns * U * step
            for s, v in start_turn.items():
                self.taken[s] = turns * self.per_turn[s] + v
        for j in range(peel + turns * U, n):
            body(j, j % U)


def program(nc, io, out):
    with ExitStack() as stack:
        place = {"at": (nc.sbuf_base + 31) // 32 * 32}

        def at(name, offset, shape, dtype=F32):
            return nc.alloc_sbuf_tensor_at(name, [P] + shape, dtype, offset=offset)

        def sb(name, shape, dtype=F32, size=None):
            offset = place["at"]
            nbytes = int(np.prod(shape)) * (1 if dtype == U8 else 4) if size is None else size
            place["at"] = offset + (nbytes + 31) // 32 * 32
            return at(name, offset, shape, dtype)

        raw = sb("raw", [U, CHUNK])
        w_hi = sb("w_hi", [U, CHUNK], F32R)
        w_lo = sb("w_lo", [U, CHUNK], F32R)
        x = sb("x", [KT, T])
        a_hi, a_lo = sb("a_hi", [KT, T], F32R), sb("a_lo", [KT, T], F32R)
        b_hi, b_lo = sb("b_hi", [KT, T], F32R), sb("b_lo", [KT, T], F32R)
        A, B = (a_hi, a_lo), (b_hi, b_lo)
        sq = sb("sq", [2, 2 * T])
        sq_sum = sb("sq_sum", [2 * T])
        mean_sq = sb("mean_sq", [2 * T])
        rough = sb("rough", [2 * T])
        newton = sb("newton", [2 * T])
        rstd = sb("rstd", [T])
        rstd_mem = sb("rstd_mem", [T])
        const = sb("const", [N_CONST])
        level_mask = sb("level_mask", [len(LEVELS) + 1, P], U8)
        par = sb("par", [N_PCOLS])
        cos_t = sb("cos_t", [T])
        sin_t = sb("sin_t", [T])
        sinks = sb("sinks", [8])
        subln_g = sb("subln_g", [1])
        neg_lam = sb("neg_lam", [1])
        lam_dot = sb("lam_dot", [2])
        lam_exp = sb("lam_exp", [2])
        row_max = sb("row_max", [2, 8])
        neg_max = sb("neg_max", [2, 8])
        row_sum = sb("row_sum", [2, 8])
        row_rec = sb("row_rec", [2, 8])
        ident = const[:, C_IDENT:C_IDENT + P]
        ones = const[:, C_ONES:C_ONES + P]
        half_ones = const[:, C_HALF:C_HALF + P]
        rot_half = const[:, C_ROT:C_ROT + P]
        swap_half = const[:, C_SWAP:C_SWAP + P]
        window = const[:, C_WIN:C_WIN + 2 * P]
        inv_freq = const[:, C_FREQ:C_FREQ + 1]

        H = place["at"]
        H_SIZE = 52 * 1024
        TR = H + H_SIZE
        assert TR + 20 * 1024 <= nc.sbuf_usable_end, (TR + 20 * 1024, nc.sbuf_usable_end)
        KB = 1024
        qkv = at("qkv", H, [24, T])
        v_tok = at("v_tok", H + 24 * KB, [TT, DM])
        scores = at("scores", H + 32 * KB, [8, 3 * P])
        probs_t = at("probs_t", H + 44 * KB, [4, 512])
        att_a = at("att_a", H, [4, T])
        mem_v_t = at("mem_v_t", H + 4 * KB, [2, 2, T])
        mem_v = [at("mem_v0", H + 8 * KB, [DM]), at("mem_v1", H + 20 * KB, [DM])]
        att_b = at("att_b", H + 12 * KB, [4, T])
        bias_tab = at("bias_tab", TR, [ATT_HEADS, 2 * P])
        mem_k = at("mem_k", TR + 12 * KB, [KT, T])
        lam_in = at("lam_in", H + 10 * KB, [4, 64])
        lam_mul = at("lam_mul", H + 11 * KB, [2, 64])
        bias_rows = at("bias_rows", H + 24 * KB, [ATT_HEADS, N_DIST])
        onehot = at("onehot", H + 42 * KB, [N_DIST])
        table = at("table", H + 43 * KB + 512, [ATT_HEADS])
        mem_t = at("mem_t", H + 44 * KB, [KT, T])
        q_mem = at("q_mem", H + 24 * KB, [KT, T])
        C = (at("c_hi", H + 32 * KB, [KT, T], F32R), at("c_lo", H + 44 * KB, [KT, T], F32R))
        scores_mem = at("scores_mem", H + 32 * KB, [8, T])
        hid_hi = at("hid_hi", H, [FT, T], F32R)
        hid_lo = at("hid_lo", H + 22 * KB, [FT, T], F32R)
        gate_z = at("gate_z", TR, [U, T])
        up_z = at("up_z", TR + 3 * KB, [U, T])
        gate_act = at("gate_act", TR + 6 * KB, [U, T])
        hid = at("hid", TR + 9 * KB, [U, T])
        CONV_T = 2 + T
        conv_in = at("conv_in", TR, [U, 2, CONV_T])
        conv_out = at("conv_out", TR + 6208, [U, 2, T])
        conv_gelu = at("conv_gelu", TR + 6208 + 6 * KB, [U, T])
        conv_hid = at("conv_hid", TR + 6208 + 9 * KB, [U, T])
        p_in = at("p_in", H + 44 * KB, [2, T])
        p_hi = at("p_hi", H + 46 * KB, [2, T], F32R)
        p_lo = at("p_lo", H + 48 * KB, [2, T], F32R)
        ple_z = at("ple_z", TR, [2, 2, T])
        ple_sig = at("ple_sig", TR + 4 * KB, [2, 2, T])
        ple_mul = at("ple_mul", TR + 8 * KB, [2, 2, T])
        hy = at("hy", H, [18, T])
        hy_v = at("hy_v", H + 18 * KB, [TT, P])
        hy_qk = at("hy_qk", H + 39 * KB, [5, T])
        hy_rot = at("hy_rot", H + 46 * KB, [5, T])
        hy_kswap = at("hy_kswap", H + 51 * KB, [T])
        hy_scores = at("hy_scores", H + 19 * KB, [8, 3 * P])
        hy_probs_t = at("hy_probs_t", H + 31 * KB, [4, 512])
        hy_conv_in = at("hy_conv_in", TR, [4, CONV_T])
        hy_conv = at("hy_conv", TR + 4128, [4, T])
        hy_att = at("hy_att", TR + 4128 + 4 * KB, [4, T])
        hy_sink = at("hy_sink", TR + 4128 + 8 * KB, [2, 8])
        rope_i = at("rope_i", TR + 14 * KB, [T], I32)
        rope_a = at("rope_a", TR + 15 * KB, [T])
        rope_n = at("rope_n", TR + 16 * KB, [T])
        rope_r = at("rope_r", TR + 17 * KB, [2, T])
        gla = at("gla", H, [24, T])
        gla_v = at("gla_v", H + 24 * KB, [TT, DM])
        gla_s = at("gla_s", H + 32 * KB, [3, 4, P])
        gla_g = at("gla_g", H + 38 * KB, [4, T])
        level_mask_f = at("level_mask_f", H + 38 * KB, [(len(LEVELS) + 1) * P])
        gla_e = at("gla_e", H + 42 * KB, [4, T])
        gla_w = [at("gla_w0", H + 46 * KB, [4, T]), at("gla_w1", TR + 8 * KB, [4, T])]
        gla_lr = at("gla_lr", H + 50 * KB, [T])
        gla_o = at("gla_o", TR, [8, T])
        gla_z = at("gla_z", TR + 12 * KB, [4, T])
        gla_wlr = at("gla_wlr", TR + 16 * KB, [KT, 16])
        gla_up = at("gla_up", TR + 17 * KB, [512])

        G = [stack.enter_context(nc.psum_tensor(f"g{i}", [P, 512], F32)) for i in range(U)]
        D = [stack.enter_context(nc.psum_tensor(f"d{i}", [P, 512], F32)) for i in range(5)]
        STAT = 4
        bias_dram = nc.dram_tensor("bias_dram", (P, ATT_HEADS * N_DIST), F32, kind="Internal").ap()

        def sem(name):
            return stack.enter_context(nc.semaphore(name))

        loaded = [sem(f"loaded{i}") for i in range(U)]
        hi_done, lo_dve, lo_pool = sem("hi_done"), sem("lo_dve"), sem("lo_pool")
        chunk_done, evicted = sem("chunk_done"), sem("evicted")
        full_dve, full_act = sem("full_dve"), sem("full_act")
        drained_dve, drained_act = sem("drained_dve"), sem("drained_act")
        x_ready, x_gated, x_normed = sem("x_ready"), sem("x_gated"), sem("x_normed")
        x_hi_done, x_split = sem("x_hi_done"), sem("x_split")
        sq_done, sq_added, sq_total, sq_for_pe = sem("sq_done"), sem("sq_added"), sem("sq_total"), sem("sq_for_pe")
        mean_done, rough_done = sem("mean_done"), sem("rough_done")
        max_done, exp_done, probs_done = sem("max_done"), sem("exp_done"), sem("probs_done")
        mixed_ready = sem("mixed_ready")
        lam_dots_done, lam_exp_done = sem("lam_dots_done"), sem("lam_exp_done")
        gate_done, act_done, tap_done, conv_done = sem("gate_done"), sem("act_done"), sem("tap_done"), sem("conv_done")
        hid_done, hid_hi_done, hid_split = sem("hid_done"), sem("hid_hi_done"), sem("hid_split")
        p_hi_done, p_split = sem("p_hi_done"), sem("p_split")
        angles_done, rope_done, qk_normed, qk_rotated, sink_done = (
            sem(s) for s in ("angles_done", "rope_done", "qk_normed", "qk_rotated", "sink_done"))
        lr_scaled, lr_ready, logit_done, soft_done, decay_done, expo_done, level_ready, gla_scores_done, silu_done = (
            sem(s) for s in ("lr_scaled", "lr_ready", "logit_done", "soft_done", "decay_done", "expo_done", "level_ready",
                             "gla_scores_done", "silu_done"))
        got_x = [sem(f"got_x{i}") for i in range(KT // 2)]
        got_const, got_par, got_conv, got_mem, got_bias, got_small, got_rope, got_p, got_gla = (sem(s) for s in (
            "got_const", "got_par", "got_conv", "got_mem", "got_bias", "got_small", "got_rope", "got_p", "got_gla"))
        bias_stored, masked_row, out_stored = sem("bias_stored"), sem("masked_row"), sem("out_stored")
        act_own, dve_own = sem("act_own"), sem("dve_own")

        def pcol(name, i=0):
            c = PCOL[name] + i
            return par[:, c:c + 1]

        def reused(n):
            return not isinstance(n, int) or n >= U

        def over(ap, n):
            return ap.unsqueeze(1).broadcast_to([P, n, ap.shape[-1]])

        def along(ap, n):
            return ap.unsqueeze(2).broadcast_to([P, ap.shape[-1], n])

        def flat(ap):
            return ap.rearrange("p a t -> p (a t)")

        def tile_at(ap, j):
            return flat(ap)[:, bass.ds(j * T, T)]

        def as_tiles(ap, width=T):
            return ap.rearrange("p (f t) -> p f t", t=width)

        def pair_at(ap, j):
            return as_tiles(flat(ap)[:, bass.ds(j * 2 * T, 2 * T)])

        def maps_of(b, t):
            return range(b % 2 + 4 * (b // 2), 4 * (b // 2) + (4 if t else 8), 2)

        def head_squares(b):
            return sq[:, b, :] if b < 2 else flat(gla_w[1])[:, (b - 2) * 2 * T:(b - 1) * 2 * T]

        block = stack.enter_context(nc.Block())

        @block.sync
        def _(sp):
            count = Counts(sp)

            def load(c, slot):
                if reused(c):
                    sp.wait_ge(lo_dve, c - (U - 1))
                    sp.wait_ge(lo_pool, c - (U - 1))
                sp.dma_start(raw[:, slot, :], io["weights"][bass.ds(c, 1)].rearrange("o p c -> p (o c)")).then_inc(loaded[slot], 16)

            def stream(first, last):
                count.each(last - first, lambda i, im: load(i + first, (im + first) % U))

            sp.dma_start(par[:, 0:N_PARAM], io["par"][:, 0:N_PARAM]).then_inc(got_par, 16)
            for i in range(KT // 2):
                sp.dma_start(x[:, 2 * i:2 * i + 2, :], io["x_t"][:, 2 * i:2 * i + 2, :]).then_inc(got_x[i], 16)
                if i == 0:
                    load(0, 0)
            sp.dma_start(const[:], io["const"]).then_inc(got_const, 16)
            load(1, 1)
            load(2, 2)
            sp.dma_start(onehot[0:N_BUCKETS + 1, :], io["onehot"]).then_inc(got_small, 16)
            sp.dma_start(table[0:N_BUCKETS, :], io["rel_bias_table"]).then_inc(got_small, 16)
            lambdas = io["diff_lambda"].rearrange("l a b -> (l a b)").partition_broadcast(P)
            sp.dma_start(lam_in[:].rearrange("p a b -> p (a b)"), lambdas).then_inc(got_small, 16)
            sp.dma_start(sinks[:], io["hy_sinks_2"].rearrange("l h -> (l h)").partition_broadcast(P)).then_inc(got_small, 16)
            sp.dma_start(mem_t[:], io["mem_t"]).then_inc(got_mem, 16)
            for c in range(3, 6):
                load(c, c % U)
            sp.wait_ge(drained_act, ATT_HEADS)
            sp.dma_start(bias_dram, bias_rows[:].rearrange("p h c -> p (h c)")).then_inc(bias_stored, 16)
            sp.wait_ge(bias_stored, count.next(bias_stored, 16))
            width = ATT_HEADS * N_DIST
            skewed = bass.AP(bias_dram.tensor, P - 1, [[width - 1, P], [N_DIST, ATT_HEADS], [1, 2 * P]])
            sp.dma_start(bias_tab[:], skewed).then_inc(got_bias, 16)
            stream(6, FIRST["up0"] + U)
            sp.dma_start(par[:, CONV_COL:N_PCOLS], io["par"][:, CONV_COL:N_PCOLS]).then_inc(got_conv, 16)
            sp.dma_start(rope_i[:], io["positions_2"].rearrange("b s -> (b s)").partition_broadcast(P)).then_inc(got_rope, 16)
            stream(FIRST["up0"] + U, FIRST["down1"])
            sp.dma_start(p_in[:], io["p_t"][0]).then_inc(got_p, 16)
            stream(FIRST["down1"], FIRST["gla_in"])
            sp.dma_start(gla_wlr[:], io["gla_w_lr"]).then_inc(got_gla, 16)
            sp.dma_start(gla_up[0:16, :], io["gla_w_gate_up_2"][0]).then_inc(got_gla, 16)
            sp.dma_start(level_mask_f[:], io["level_mask"]).then_inc(got_gla, 16)
            stream(FIRST["gla_in"], FIRST["down2"])
            sp.dma_start(p_in[:], io["p_t"][1]).then_inc(got_p, 16)
            stream(FIRST["down2"], CHUNKS)
            for i in range(KT // 2):
                sp.wait_ge(x_gated, KT // 2 + i + 1)
                sp.dma_start(out[:, 2 * i:2 * i + 2, :], x[:, 2 * i:2 * i + 2, :]).then_inc(out_stored, 16)
            sp.wait_ge(out_stored, 16 * (KT // 2))

        @block.tensor
        def _(pe):
            count = Counts(pe)
            due = {}
            free_at = {}

            def acquire(b):
                if b in free_at:
                    pe.wait_ge(*free_at[b])

            def fill(b, last, full, drained):
                if last is not None:
                    last.then_inc(full, 1)
                due[drained] = due.get(drained, 0) + 1
                free_at[b] = (drained, due[drained])
                return free_at[b]

            def mm(out, lhsT, rhs, start=True, stop=True):
                return pe.matmul(out, lhsT, rhs, start=start, stop=stop, skip_group_check=True)

            def turn(out, src, n=P):
                return pe.transpose(out, src, ident[0:n, 0:n])

            def chunk(name, j, jm, moving, fresh=False):
                c, n = j + FIRST[name], j + FIRST_OUT[name]
                slot, bank = (FIRST[name] + jm) % U, G[(FIRST_OUT[name] + jm) % U]
                pe.wait_ge(lo_dve, c + 1)
                pe.wait_ge(lo_pool, c + 1)
                if reused(n):
                    pe.wait_ge(evicted, n - (U - 1))
                for k in range(KT):
                    if fresh:
                        pe.wait_ge(x_split, count.next(x_split))
                    for f in range(2):
                        cols = slice(k * 2 * P + f * P, k * 2 * P + (f + 1) * P)
                        to = bank[:, f * T:(f + 1) * T]
                        mm(to, w_hi[:, slot, cols], moving[0][:, k, :], k == 0 and f == 0, False)
                        mm(to, w_hi[:, slot, cols], moving[1][:, k, :], False, False)
                        last = mm(to, w_lo[:, slot, cols], moving[0][:, k, :], False, k == KT - 1)
                last.then_inc(chunk_done, 1)

            def chunk_k(name, j, jm, moving, k0):
                c, slot = j + FIRST[name], (FIRST[name] + jm) % U
                first = isinstance(j, int) and j == 0
                final = isinstance(j, int) and j == COUNT[name] - 1
                pe.wait_ge(lo_dve, c + 1)
                pe.wait_ge(lo_pool, c + 1)
                order = [(h, f) for f in range(KT) for h in range(2)] if final else [(h, f) for h in range(2) for f in range(KT)]
                for h, f in order:
                    if first and h == 0 and f % 2 == 0:
                        acquire(f // 2)
                    to = D[f // 2][:, (f % 2) * T:(f % 2 + 1) * T]
                    cols = slice(h * DM + f * P, h * DM + (f + 1) * P)
                    m_hi, m_lo = (tile_at(m, k0 + h) for m in moving)
                    mm(to, w_hi[:, slot, cols], m_hi, first and h == 0 and f % 2 == 0, False)
                    mm(to, w_hi[:, slot, cols], m_lo, False, False)
                    last = mm(to, w_lo[:, slot, cols], m_hi, False, final and h == 1)
                    if final and h == 1 and f in (1, 3, 5) and name[:4] == "down":
                        fill(f // 2, last, full_dve, x_ready)
                last.then_inc(chunk_done, 1)
                if final and name[:4] == "down":
                    fill(3, None, None, x_ready)

            def norm_sum():
                pe.wait_ge(sq_total, count.next(sq_total))
                acquire(STAT)
                mm(D[STAT][:, 0:T], ones, sq_sum[:, 0:T], True, False)
                fill(STAT, mm(D[STAT][:, 0:T], ones, sq_sum[:, T:2 * T], False, True), full_dve, mean_done)

            def outputs(name, moving):
                def body(j, jm):
                    fresh = isinstance(j, int) and j == 0
                    chunk(name, j, jm, moving, fresh)
                    if fresh:
                        norm_sum()
                count.each(COUNT[name], body)

            for j in range(W_IN_Q):
                chunk("w_in", j, j % U, A, fresh=j == 0)
                if j == 0:
                    pe.wait_ge(got_const, 16)
                    norm_sum()
                if j == 1:
                    pe.wait_ge(got_small, count.next(got_small, 16 * 4))
                    pe.wait_ge(masked_row, count.next(masked_row))
                    for h in range(ATT_HEADS):
                        acquire(h % 4)
                        column = table[0:N_BUCKETS + 1, h:h + 1].broadcast_to([N_BUCKETS + 1, P])
                        fill(h % 4, mm(D[h % 4][:, 0:N_DIST], column, onehot[0:N_BUCKETS + 1, :]), full_act, drained_act)
                if j == 4:
                    norm_sum()

            def turn_value_tile(src, f0, t, b):
                acquire(b)
                for f in range(4):
                    last = turn(D[b][:, f * P:(f + 1) * P], src[:, f0 + f, t * P:(t + 1) * P])
                return fill(b, last, full_act, drained_act)

            def turn_values(src, f0, banks):
                for t, b in enumerate(banks):
                    turned = turn_value_tile(src, f0, t, b)
                return turned

            def score_tiles(q, key, q0, t):
                keys = (t + 1) * P
                for b in range(4 if t else 2):
                    acquire(b)
                    for i, m in enumerate(maps_of(b, t)):
                        half = slice((m % 2) * 64, (m % 2) * 64 + 64)
                        last = mm(D[b][:, i * keys:(i + 1) * keys], q[half, q0 + m // 2, t * P:(t + 1) * P], key(m)[half, 0:keys])
                    fill(b, last, full_dve, drained_dve)

            def weigh_values(heads, values, place_of, per_bank, probs, probs_t):
                turned = {}
                for step in range(heads + 1):
                    if step < heads:
                        b = step % 2
                        acquire(b)
                        for i in range(3):
                            last = turn(D[b][:, i * P:(i + 1) * P], probs[:, step, i * P:(i + 1) * P])
                        turned[step] = fill(b, last, full_act, drained_act)
                    if step >= 1:
                        h = step - 1
                        b = 2 + h // per_bank
                        to = place_of(h)
                        pe.wait_ge(*turned[h])
                        if h % per_bank == 0:
                            acquire(b)
                        mm(to, values(0, h), probs_t[:, h % 4, 0:T], True, False)
                        last = mm(to[:, P:T], values(1, h), probs_t[:, h % 4, T:3 * P], False, True)
                        if h % per_bank == per_bank - 1:
                            fill(b, last, full_act, drained_act)

            def half_place(h):
                return D[2 + h // 4][(h % 2) * 64:(h % 2) * 64 + 64, (h // 2 % 2) * T:(h // 2 % 2 + 1) * T]

            def whole_place(h):
                return D[2 + h // 2][:, (h % 2) * T:(h % 2 + 1) * T]

            def turn_mem_values(j):
                pe.wait_ge(evicted, FIRST_OUT["w_cv"] + j + 1)
                acquire(STAT)
                for t in range(TT):
                    for f in range(2):
                        last = turn(D[STAT][:, t * 2 * P + f * P:t * 2 * P + (f + 1) * P], mem_v_t[:, j % 2, f, t * P:(t + 1) * P])
                return fill(STAT, last, full_act, drained_act)

            pe.wait_ge(evicted, W_IN_Q)
            values_turned = turn_values(qkv, 8, (2, 3))
            score_tiles(qkv, lambda m: qkv[:, 4 + m // 2, :], 0, 1)
            score_tiles(qkv, lambda m: qkv[:, 4 + m // 2, :], 0, 0)
            for j in (6, 7, 8):
                chunk("w_in", j, j % U, A)
            pe.wait_ge(*values_turned)
            pe.wait_ge(probs_done, count.next(probs_done))
            weigh_values(8, lambda t, h: v_tok[:, t, h * 64:(h + 1) * 64], half_place, 4, scores, probs_t)
            chunk("w_in", 9, 0, A)
            pe.wait_ge(evicted, 10)
            score_tiles(qkv, lambda m: qkv[:, 16 + m // 2, :], 12, 1)
            score_tiles(qkv, lambda m: qkv[:, 16 + m // 2, :], 12, 0)
            chunk("w_in", 10, 1, A)
            pe.wait_ge(sq_for_pe, count.next(sq_for_pe, 2))
            acquire(STAT)
            for f in range(4):
                last = mm(D[STAT][:, 0:T], ones, sq[:, f // 2, (f % 2) * T:(f % 2 + 1) * T], f == 0, f == 3)
            fill(STAT, last, full_dve, mean_done)
            chunk("w_in", 11, 2, A)
            chunk("w_ck", 0, 0, B, fresh=True)
            pe.wait_ge(evicted, COUNT["w_in"])
            values_turned = turn_values(qkv, 20, (2, 3))
            pe.wait_ge(*values_turned)
            pe.wait_ge(probs_done, count.next(probs_done))
            weigh_values(4, lambda t, h: v_tok[:, t, 512 + h * P:512 + (h + 1) * P], whole_place, 2, scores, probs_t)
            chunk("w_ck", 1, 1, B)
            for b in range(2):
                pe.wait_ge(sq_for_pe, count.next(sq_for_pe))
                acquire(b)
                for f in range(2):
                    last = mm(D[b][:, f * T:(f + 1) * T], ones, sq[:, b, f * T:(f + 1) * T])
                fill(b, last, full_dve, mean_done)
            chunk("w_ck", 2, 2, B)
            chunk("w_ck", 3, 0, B)
            for j in range(COUNT["w_out"]):
                chunk("w_out", j, j % U, A, fresh=j == 0)

            outputs("w_cq", C)
            pe.wait_ge(evicted, FIRST_OUT["w_cq"] + COUNT["w_cq"])
            for b in range(4):
                acquire(b)
                for i in range(2):
                    t, h = (2 * b + i) // 4, (2 * b + i) % 4
                    for d in range(2):
                        last = mm(D[b][:, i * T:(i + 1) * T], q_mem[:, 2 * h + d, t * P:(t + 1) * P], mem_k[:, 2 * h + d, :],
                                  d == 0, d == 1)
                fill(b, last, full_dve, drained_dve)
            mem_v_turned = {}
            for j in range(COUNT["w_cv"]):
                chunk("w_cv", j, j % U, B)
                if j >= 1:
                    mem_v_turned[j - 1] = turn_mem_values(j - 1)
            pe.wait_ge(probs_done, count.next(probs_done))
            turned = {}
            for step in range(5):
                if step == 2:
                    mem_v_turned[3] = turn_mem_values(3)
                if step < 4:
                    acquire(step % 2)
                    for s in range(2):
                        for t in range(TT):
                            last = turn(D[step % 2][:, s * T + t * P:s * T + (t + 1) * P], scores_mem[:, t * 4 + step, s * P:(s + 1) * P])
                    turned[step] = fill(step % 2, last, full_act, drained_act)
                if step >= 1:
                    h = step - 1
                    b = 2 + h % 2
                    pe.wait_ge(*turned[h])
                    pe.wait_ge(*mem_v_turned[h])
                    acquire(b)
                    for d in range(2):
                        to, v = D[b][:, d * T:(d + 1) * T], slice((2 * h + d) * P, (2 * h + d + 1) * P)
                        mm(to, mem_v[0][:, v], probs_t[:, h, 0:T], True, False)
                        last = mm(to, mem_v[1][:, v], probs_t[:, h, T:2 * T], False, True)
                    last.then_inc(full_act, 1)
                    free_at[b] = (x_split, count.taken[x_split] + 2 * (h + 1))
            for j in range(COUNT["w_co"]):
                chunk("w_co", j, j % U, A, fresh=j == 0)

            def ffn(layer, moving):
                outputs(f"up{layer}", moving)

                def body(j, jm):
                    pe.wait_ge(hid_split, count.next(hid_split, 2))
                    chunk_k(f"down{layer}", j, jm, (hid_hi, hid_lo), j * 2)
                count.each(COUNT[f"down{layer}"], body)

            ffn(0, B)
            norm_sum()

            for j in range(4):
                chunk("hy_in", j, j % U, A, fresh=j == 0)
                if j == 0:
                    norm_sum()
            tiles_of = (2, 2, 1)
            for i in range(3):
                pe.wait_ge(sq_for_pe, count.next(sq_for_pe))
                acquire(i)
                for f in range(tiles_of[i]):
                    last = mm(D[i][:, f * T:(f + 1) * T], half_ones, hy_rot[:, 2 * i + f, :])
                fill(i, last, full_dve, mean_done)
            chunk("hy_in", 4, 4 % U, A)
            for i in range(3):
                pe.wait_ge(qk_normed, count.next(qk_normed))
                acquire(i)
                for f in range(tiles_of[i]):
                    last = mm(D[i][:, f * T:(f + 1) * T], rot_half, hy_qk[:, 2 * i + f, :])
                fill(i, last, full_dve, drained_dve)
            acquire(3)
            for t in range(TT):
                last = turn(D[3][:, t * P:(t + 1) * P], hy[:, 5, t * P:(t + 1) * P])
            hy_v_turned = fill(3, last, full_act, drained_act)
            chunk("hy_in", 5, 5 % U, A)
            pe.wait_ge(qk_rotated, count.next(qk_rotated))
            acquire(STAT)
            pe.wait_ge(*fill(STAT, mm(D[STAT][:, 0:T], swap_half, hy_qk[:, 4, :]), full_act, drained_act))

            def hy_key(m):
                return hy_qk[:, 4, :] if m % 2 == m // 4 else hy_kswap[:, :]

            score_tiles(hy_qk, hy_key, 0, 1)
            score_tiles(hy_qk, hy_key, 0, 0)
            for j in (6, 7, 8):
                chunk("hy_in", j, j % U, A)
            pe.wait_ge(probs_done, count.next(probs_done))
            pe.wait_ge(*hy_v_turned)
            weigh_values(8, lambda t, h: hy_v[:, t, (h // 4) * 64:(h // 4 + 1) * 64], half_place, 4, hy_scores, hy_probs_t)
            for j in range(COUNT["hy_out"]):
                chunk("hy_out", j, j % U, B, fresh=j == 0)

            def embedding(layer, moving):
                pe.wait_ge(p_split, count.next(p_split))
                chunk_k(f"proj{layer}", 0, 0, (p_hi, p_lo), 0)
                for b in range(4):
                    fill(b, None, None, drained_dve)
                for j in range(COUNT[f"gate{layer}"]):
                    chunk(f"gate{layer}", j, j % U, moving, fresh=j == 0)
                    if j == 0:
                        norm_sum()

            ffn(1, A)
            embedding(1, B)

            def gla_chunk(j):
                chunk("gla_in", j, j % U, A, fresh=j == 0)

            gla_chunk(0)
            norm_sum()
            pe.wait_ge(lr_scaled, count.next(lr_scaled))
            acquire(0)
            for k in range(KT):
                last = mm(D[0][0:16, 0:T], gla_wlr[:, k, :], x[:, k, :], k == 0, k == KT - 1)
            fill(0, last, full_dve, lr_ready)
            gla_chunk(1)
            pe.wait_ge(lr_ready, count.next(lr_ready))
            for b in (1, 2):
                acquire(b)
                for f in range(2):
                    h = 2 * (b - 1) + f
                    last = mm(D[b][:, f * T:(f + 1) * T], gla_up[0:16, h * P:(h + 1) * P], gla_lr[0:16, :])
                fill(b, last, full_dve, drained_dve)
            gla_chunk(2)
            gla_chunk(3)

            def gla_level(i):
                if i == 0:
                    pe.wait_ge(evicted, FIRST_OUT["gla_in"] + 4)
                else:
                    pe.wait_ge(level_ready, count.next(level_ready))
                for t in range(TT):
                    b = (2 * i + t) % 4
                    cols = slice(t * P, (t + 1) * P)
                    acquire(b)
                    for h in range(4):
                        k, q = (gla[:, 4 + h, cols], gla[:, h, cols]) if i == 0 else (gla_w[i % 2][:, h, cols],) * 2
                        last = mm(D[b][:, h * P:(h + 1) * P], k, q)
                    fill(b, last, full_dve, drained_dve)

            gla_level(0)
            gla_chunk(4)
            gla_chunk(5)
            for i in range(1, len(LEVELS) + 1):
                gla_level(i)
                if i % 2:
                    gla_chunk(6 + i // 2)
                if i == 5:
                    pe.wait_ge(evicted, FIRST_OUT["gla_in"] + 8)
                if i >= 5:
                    turn_value_tile(gla, *VALUE_TILES[i - 5], STAT)
            pe.wait_ge(level_ready, count.next(level_ready))
            acquire(0)
            for h in range(4):
                last = mm(D[0][:, h * P:(h + 1) * P], gla_w[0][:, h, 0:P], gla_w[0][:, h, P:2 * P])
            fill(0, last, full_dve, gla_scores_done)
            pe.wait_ge(*turn_value_tile(gla, *VALUE_TILES[3], STAT))
            pe.wait_ge(gla_scores_done, count.next(gla_scores_done))
            for b in range(4):
                acquire(b)
                for f in range(2):
                    v = slice((2 * b + f) * P, (2 * b + f + 1) * P)
                    to = D[b][:, f * T:(f + 1) * T]
                    mm(to[:, 0:P], gla_v[:, 0, v], gla_s[:, 0, b, :], f == 0, True)
                    mm(to[:, P:T], gla_v[:, 0, v], gla_s[:, 2, b, :], False, False)
                    last = mm(to[:, P:T], gla_v[:, 1, v], gla_s[:, 1, b, :], False, True)
                fill(b, last, full_act, drained_act)
            gla_chunk(10)
            for pair in range(2):
                acquire(pair)
                for i in range(2):
                    pe.wait_ge(sq_for_pe, count.next(sq_for_pe))
                    for f in range(2):
                        last = mm(D[pair][:, i * T:(i + 1) * T], ones, head_squares(2 * pair + i)[:, f * T:(f + 1) * T],
                                  f == 0 and i == 0, f == 1)
                fill(pair, last, full_dve, mean_done)
            gla_chunk(11)
            for j in range(COUNT["gla_out"]):
                chunk("gla_out", j, j % U, B, fresh=j == 0)

            ffn(2, A)
            embedding(2, B)

        @block.scalar
        def _(act):
            count = Counts(act)
            count.per_turn = {s: 16 for s in loaded}

            def fn(out, in_, func=ACT.Copy, **kw):
                return act.activation(out, in_, func, **kw)

            def split_hi(c, slot):
                if isinstance(c, int) and c >= CHUNKS:
                    return
                act.wait_ge(loaded[slot], count.next(loaded[slot], 16))
                if reused(c):
                    act.wait_ge(chunk_done, c - (U - 1))
                fn(w_hi[:, slot, :], raw[:, slot, :]).then_inc(hi_done, 1)

            def ahead(name, j, jm):
                split_hi(j + (FIRST[name] + AHEAD), (FIRST[name] + jm + AHEAD) % U)

            def out_count(name, j):
                return j + (FIRST_OUT[name] + 1)

            def loop(n, body, peel=3, function=ACT.Copy):
                count.each(n, body, peel, lambda: act.preload_act_table(function))

            def hi_parts(moving, first, src, gains=None):
                for f in range(len(src)):
                    scale = {} if gains is None else {"scale": gains[f]}
                    fn(moving[0][:, first + f, :], src[f], **scale).then_inc(x_hi_done, 1)

            def prep_pair(moving, gain, g0, src, i):
                if moving is not None:
                    hi_parts(moving, 2 * i, [src[:, 2 * i + f, :] for f in range(2)], [pcol(gain, g0 + 2 * i + f) for f in range(2)])
                pair = flat(src[:, 2 * i:2 * i + 2, :])
                if i == 0:
                    fn(sq_sum[:], pair, ACT.Square).then_inc(sq_done, 1)
                else:
                    if i == 3:
                        act.wait_ge(sq_added, count.next(sq_added, 2) - 1)
                    fn(sq[:, i % 2, :], pair, ACT.Square).then_inc(sq_done, 1)

            def prep(ready, moving, gain, g0=0):
                for i in range(KT // 2):
                    act.wait_ge(ready, count.next(ready))
                    prep_pair(moving, gain, g0, x, i)

            def rough_rstd(width=T):
                act.preload_act_table(ACT.Abs_reciprocal_sqrt)
                act.wait_ge(mean_done, count.next(mean_done))
                fn(rough[:, 0:width], mean_sq[:, 0:width], ACT.Abs_reciprocal_sqrt).then_inc(rough_done, 1)

            def exps(s, t, maps, cols):
                act.wait_ge(max_done, count.next(max_done))
                for m in range(maps):
                    last = fn(s[:, m, cols], s[:, m, cols], ACT.Exp, bias=neg_max[:, t, m:m + 1], accum_out=row_sum[:, t, m:m + 1])
                last.then_inc(exp_done, 1)

            def from_bank(out, in_):
                act.wait_ge(full_act, count.next(full_act))
                fn(out, in_).then_inc(drained_act, count.one(drained_act))

            def weigh_values(heads, per_bank, probs_t, att, after):
                for step in range(heads + 1):
                    if step < heads:
                        from_bank(probs_t[:, step % 4, 0:3 * P], D[step % 2][:, 0:3 * P])
                    if step >= 1 and (step - 1) % per_bank == per_bank - 1:
                        i = (step - 1) // per_bank
                        from_bank(flat(att[:, 2 * i:2 * i + 2, :]), D[2 + i][:])
                        act.wait_ge(drained_act, count.sent[drained_act])
                        after(i)

            def square_of(att):
                def after(i):
                    fn(sq[:, i, :], flat(att[:, 2 * i:2 * i + 2, :]), ACT.Square).then_inc(sq_for_pe, 1)
                return after

            def residual(name, moving, gain, g0=0):
                for j in range(COUNT[name]):
                    ahead(name, j, j % U)
                    act.wait_ge(evicted, out_count(name, j))
                    prep_pair(moving, gain, g0, x, j)

            act.wait_ge(got_par, 16)
            for i in range(KT // 2):
                act.wait_ge(got_x[i], 16)
                prep_pair(A, "mix_norm_g", 0, x, i)
                if i == 0:
                    split_hi(0, 0)
            split_hi(1, 1)

            for j in range(W_IN_Q):
                ahead("w_in", j, j % U)
                if j == 0:
                    rough_rstd()
                if j == 1:
                    for h in range(ATT_HEADS):
                        from_bank(bias_rows[:, h, :], D[h % 4][:, 0:N_DIST])
                    act.wait_ge(lam_dots_done, count.next(lam_dots_done))
                    fn(lam_exp[:], lam_dot[:], ACT.Exp).then_inc(lam_exp_done, 1)
                if j == 3:
                    act.wait_ge(got_mem, 16)
                    for i in range(KT // 2):
                        prep_pair(B, "mem_norm_g", 0, mem_t, i)
                if j == 4:
                    rough_rstd()


            def values_to_tokens(v, f0, banks):
                for t, b in enumerate(banks):
                    from_bank(v[:, t, f0 * P:(f0 + 4) * P], D[b][:])

            def mem_values(j):
                act.wait_ge(full_act, count.next(full_act))
                for t in range(TT):
                    last = fn(mem_v[t][:, j * 2 * P:(j + 1) * 2 * P], D[STAT][:, t * 2 * P:(t + 1) * 2 * P])
                last.then_inc(drained_act, count.one(drained_act))

            act.wait_ge(got_bias, count.next(got_bias, 16))
            values_to_tokens(v_tok, 0, (2, 3))
            exps(scores, 1, 8, slice(P, 3 * P))
            exps(scores, 0, 8, slice(0, P))
            for j in (6, 7, 8):
                ahead("w_in", j, j % U)
            weigh_values(8, 4, probs_t, att_a, square_of(att_a))
            ahead("w_in", 9, 0)
            exps(scores, 1, 8, slice(P, 3 * P))
            exps(scores, 0, 8, slice(0, P))
            ahead("w_in", 10, 1)
            ahead("w_in", 11, 2)
            rough_rstd()
            ahead("w_ck", 0, 0)
            values_to_tokens(v_tok, 4, (2, 3))
            weigh_values(4, 2, probs_t, att_b, square_of(att_b))
            ahead("w_ck", 1, 1)
            act.wait_ge(chunk_done, COUNT["w_in"])
            act.wait_ge(mixed_ready, count.next(mixed_ready))
            hi_parts(A, 0, [att_a[:, f, :] for f in range(4)], [pcol("moba_out_g", f) for f in range(4)])
            for b in range(2):
                rough_rstd(2 * T)
                act.wait_ge(mixed_ready, count.next(mixed_ready))
                hi_parts(A, 4 + 2 * b, [att_b[:, 2 * b + f, :] for f in range(2)], [subln_g[:, 0:1]] * 2)
            ahead("w_ck", 2, 2)
            ahead("w_ck", 3, 0)
            residual("w_out", C, "cross_norm_g")

            for j in range(COUNT["w_cq"]):
                ahead("w_cq", j, j % U)
                if j == 0:
                    rough_rstd()
            exps(scores_mem, 0, 8, slice(0, T))
            for j in range(COUNT["w_cv"]):
                ahead("w_cv", j, j % U)
                if j >= 1:
                    mem_values(j - 1)
            for step in range(5):
                if step == 2:
                    mem_values(3)
                if step < 4:
                    from_bank(probs_t[:, step, :], D[step % 2][:])
                if step >= 1:
                    h = step - 1
                    act.wait_ge(full_act, count.next(full_act))
                    hi_parts(A, 2 * h, [D[2 + h % 2][:, d * T:(d + 1) * T] for d in range(2)])
            residual("w_co", B, "ffn_norm_g")

            def hidden_hi(j, jm, ring):
                act.wait_ge(hid_done, count.next(hid_done))
                fn(tile_at(hid_hi, j), ring[:, jm % U, :]).then_inc(hid_hi_done, 1)

            def down(layer):
                name = f"down{layer}"
                loop(COUNT[name], lambda j, jm: ahead(name, j, jm))

            def gated_body(j, jm):
                ahead("up0", j, jm)
                if isinstance(j, int) and j == 0:
                    rough_rstd()
                act.wait_ge(gate_done, count.next(gate_done))
                fn(gate_act[:, jm, :], gate_z[:, jm, :], ACT.Silu).then_inc(act_done, 1)
                if not isinstance(j, int) or j >= 1:
                    hidden_hi(j - 1, jm + 2, hid)

            loop(FT, gated_body, 3, ACT.Silu)
            hidden_hi(FT - 1, (FT - 1) % U, hid)
            down(0)
            act.wait_ge(angles_done, 1)
            fn(sin_t[:], rope_r[:, 0, :], ACT.Sin)
            fn(cos_t[:], rope_r[:, 1, :], ACT.Sin).then_inc(rope_done, 1)
            prep(x_ready, None, None)
            rough_rstd()
            prep(x_normed, A, "mix_norm_2")

            def hy_ahead(j):
                ahead("hy_in", j, j % U)

            hy_ahead(0)
            rough_rstd()
            for j in (1, 2):
                hy_ahead(j)
            for i in range(3):
                act.wait_ge(evicted, out_count("hy_in", i))
                tiles = slice(2 * i, min(2 * i + 2, 5))
                fn(flat(hy_rot[:, tiles, :]), flat(hy[:, tiles, :]), ACT.Square).then_inc(sq_for_pe, 1)
            hy_ahead(3)
            for i in range(3):
                rough_rstd((2, 2, 1)[i] * T)
            hy_ahead(4)
            from_bank(flat(hy_v), D[3][:, 0:T])
            hy_ahead(5)
            from_bank(hy_kswap[:], D[STAT][:, 0:T])
            for t, cols in ((1, slice(P, 3 * P)), (0, slice(0, P))):
                act.wait_ge(max_done, count.next(max_done))
                fn(hy_sink[:, t, :], hy_sink[:, t, :], ACT.Exp).then_inc(sink_done, 1)
                for m in range(8):
                    last = fn(hy_scores[:, m, cols], hy_scores[:, m, cols], ACT.Exp, bias=neg_max[:, t, m:m + 1],
                              accum_out=row_sum[:, t, m:m + 1])
                last.then_inc(exp_done, 1)
            for j in (6, 7, 8):
                hy_ahead(j)
            weigh_values(8, 4, hy_probs_t, hy_att, lambda i: hi_parts(B, 2 * i, [hy_att[:, 2 * i + f, :] for f in range(2)]))
            for i in range(2):
                act.wait_ge(mixed_ready, count.next(mixed_ready))
                hi_parts(B, 4 + 2 * i, [hy_conv[:, 2 * i + f, :] for f in range(2)])
            residual("hy_out", A, "ffn_norm_2")

            def conv_ffn(layer, moving, ple_moving):
                name = f"up{layer}"

                def column(base, tap, f, j):
                    return par[:, bass.ds(j + (base + ((layer - 1) * tap[1] + tap[0]) * 2 * FT + f * FT), 1)]

                def gelu(j, jm):
                    act.wait_ge(conv_done, count.next(conv_done))
                    fn(conv_gelu[:, jm % U, :], conv_out[:, jm % U, 0, :], ACT.Gelu).then_inc(act_done, 1)

                def body(j, jm):
                    early = isinstance(j, int)
                    ahead(name, j, jm)
                    if early and j == 0:
                        rough_rstd()
                    act.wait_ge(evicted, out_count(name, j))
                    for f in range(2):
                        last = fn(conv_out[:, jm, f, :], conv_in[:, jm, f, 2:2 + T], ACT.Identity,
                                  scale=column(CONV_COL, (2, 3), f, j), bias=column(CONVB_COL, (0, 1), f, j))
                    last.then_inc(tap_done, 1)
                    if not early or j >= 2:
                        hidden_hi(j - 2, jm + 1, conv_hid)
                    if not early or j >= 1:
                        gelu(j - 1, jm + 2)

                act.wait_ge(got_conv, 16)
                loop(FT, body, 4, ACT.Gelu)
                hidden_hi(FT - 2, (FT - 2) % U, conv_hid)
                gelu(FT - 1, (FT - 1) % U)
                hidden_hi(FT - 1, (FT - 1) % U, conv_hid)
                act.wait_ge(got_p, count.next(got_p, 16))
                fn(flat(p_hi), flat(p_in)).then_inc(p_hi_done, 1)
                down(layer)
                prep(x_ready, ple_moving, "ple_norm_2", (layer - 1) * KT)
                ahead(f"proj{layer}", 0, 0)
                for j in range(COUNT[f"gate{layer}"]):
                    ahead(f"gate{layer}", j, j % U)
                    if j == 0:
                        rough_rstd()
                    act.wait_ge(evicted, out_count(f"gate{layer}", j))
                    fn(flat(ple_sig[:, j % 2, :, :]), flat(ple_z[:, j % 2, :, :]), ACT.Sigmoid).then_inc(act_done, 1)
                    if layer == 1 and j >= 1:
                        act.wait_ge(x_gated, count.next(x_gated))
                        prep_pair(A, "mix_norm_2", KT, x, j - 1)
                if layer == 1:
                    act.wait_ge(x_gated, count.next(x_gated))
                    prep_pair(A, "mix_norm_2", KT, x, 3)

            conv_ffn(1, A, B)

            def gla_ahead(j):
                ahead("gla_in", j, j % U)

            def decays(i):
                act.wait_ge(decay_done, count.next(decay_done))
                e = flat((gla_e, gla_z)[i % 2])
                fn(e, e, ACT.Exp, scale=1.0 / 16.0).then_inc(expo_done, 1)

            gla_ahead(0)
            rough_rstd()
            gla_ahead(1)
            act.wait_ge(logit_done, count.next(logit_done))
            fn(flat(gla_e), flat(gla_e), ACT.Exp).then_inc(act_own, count.one(act_own))
            act.wait_ge(act_own, count.sent[act_own])
            fn(flat(gla_e), flat(gla_e), ACT.Ln, bias=ones[:, 0:1]).then_inc(soft_done, 1)
            gla_ahead(2)
            decays(1)
            for j in (3, 4, 5):
                gla_ahead(j)

            def value_tile(i):
                f0, t = VALUE_TILES[i]
                from_bank(gla_v[:, t, (f0 - 8) * P:(f0 - 4) * P], D[STAT][:])

            def open_gate(i):
                act.wait_ge(evicted, out_count("gla_in", i))
                og = flat(gla[:, 2 * i:2 * i + 2, :])
                return fn(og, og, ACT.Silu)

            for i in range(1, len(LEVELS) + 1):
                decays(i + 1)
                if i % 2:
                    gla_ahead(6 + i // 2)
                if i >= 5:
                    value_tile(i - 5)
            value_tile(3)
            open_gate(8)
            open_gate(9).then_inc(silu_done, 1)
            for b in range(4):
                from_bank(flat(gla_o[:, 2 * b:2 * b + 2, :]), D[b][:])
                act.wait_ge(drained_act, count.sent[drained_act])
                fn(head_squares(b), flat(gla_o[:, 2 * b:2 * b + 2, :]), ACT.Square).then_inc(sq_for_pe, 1)
            gla_ahead(10)
            rough_rstd(2 * T)
            act.wait_ge(mixed_ready, count.next(mixed_ready))
            hi_parts(B, 0, [gla_o[:, f, :] for f in range(4)])
            rough_rstd(2 * T)
            gla_ahead(11)
            open_gate(10)
            open_gate(11).then_inc(silu_done, 1)
            act.wait_ge(mixed_ready, count.next(mixed_ready))
            hi_parts(B, 4, [gla_o[:, 4 + f, :] for f in range(4)])
            residual("gla_out", A, "ffn_norm_2", KT)
            conv_ffn(2, A, B)

        @block.vector
        def _(dve):
            count = Counts(dve)

            def mul(out, a, b):
                return dve.tensor_tensor(out, a, b, ALU.mult)

            def add(out, a, b):
                return dve.tensor_tensor(out, a, b, ALU.add)

            def sub(out, a, b):
                return dve.tensor_tensor(out, a, b, ALU.subtract)

            def fused(out, a, scalar, b, op0, op1):
                return dve.scalar_tensor_tensor(out, a, scalar, b, op0, op1)

            def split_lo(c, slot):
                if isinstance(c, int) and c >= CHUNKS:
                    return
                dve.wait_ge(hi_done, c + 1)
                cols = slice(0, DVE_COLS)
                sub(w_lo[:, slot, cols], raw[:, slot, cols], w_hi[:, slot, cols].bitcast(F32)).then_inc(lo_dve, 1)

            def ahead(name, j, jm):
                split_lo(j + (FIRST[name] + AHEAD), (FIRST[name] + jm + AHEAD) % U)

            def bank_of(name, j, jm):
                dve.wait_ge(chunk_done, j + (FIRST[name] + 1))
                return as_tiles(G[(FIRST_OUT[name] + jm) % U][:])

            def lo_parts(moving, first, src, gains=None):
                for f in range(len(src)):
                    dve.wait_ge(x_hi_done, count.next(x_hi_done))
                    hi, lo = moving[0][:, first + f, :].bitcast(F32), moving[1][:, first + f, :]
                    if gains is None:
                        sub(lo, src[f], hi).then_inc(x_split, 1)
                    else:
                        fused(lo, src[f], gains[f], hi, ALU.mult, ALU.subtract).then_inc(x_split, 1)

            def prep_pair(moving, gain, g0, src, i):
                lo_parts(moving, 2 * i, [src[:, 2 * i + f, :] for f in range(2)], [pcol(gain, g0 + 2 * i + f) for f in range(2)])

            def prep(moving, gain, g0=0, src=x):
                for i in range(KT // 2):
                    prep_pair(moving, gain, g0, src, i)

            def mean(bank, features, width=T):
                dve.wait_ge(full_dve, count.next(full_dve))
                dve.tensor_scalar(mean_sq[:, 0:width], D[bank][:, 0:width], 1.0 / features, EPS, ALU.mult, ALU.add).then_inc(mean_done, count.one(mean_done))

            def refine(to, width=T):
                dve.wait_ge(rough_done, count.next(rough_done))
                m, r, n = mean_sq[:, 0:width], rough[:, 0:width], newton[:, 0:width]
                dve.wait_ge(mean_done, count.sent[mean_done])
                fused(n, m, -0.5, r, ALU.mult, ALU.mult).then_inc(dve_own, count.one(dve_own))
                dve.wait_ge(dve_own, count.sent[dve_own])
                mul(n, n, r).then_inc(dve_own, count.one(dve_own))
                dve.wait_ge(dve_own, count.sent[dve_own])
                fused(to[:, 0:width], n, 1.5, r, ALU.add, ALU.mult).then_inc(dve_own, count.one(dve_own))
                dve.wait_ge(dve_own, count.sent[dve_own])

            def token_norm(to=rstd):
                mean(STAT, DM)
                refine(to)

            def evict(name, j, jm, to, scale=rstd):
                mul(to, bank_of(name, j, jm), over(scale[:], 2)).then_inc(evicted, count.one(evicted))

            def negate_max(s, t, cols, maps=8):
                dve.tensor_reduce(row_max[:, t, 0:maps], s[:, :, cols], AX_X, ALU.max).then_inc(dve_own, count.one(dve_own))
                dve.wait_ge(dve_own, count.sent[dve_own])
                dve.tensor_scalar(neg_max[:, t, 0:maps], row_max[:, t, 0:maps], -1.0, None, ALU.mult).then_inc(max_done, 1)

            def normalise(s, t, cols, width):
                return mul(s[:, :, cols], s[:, :, cols], along(row_rec[:, t, :], width))

            def residual(name, moving, gain, g0=0):
                for j in range(COUNT[name]):
                    ahead(name, j, j % U)
                    pair = x[:, 2 * j:2 * j + 2, :]
                    add(pair, pair, bank_of(name, j, j % U)).then_inc(evicted, count.one(evicted))
                    if j >= 1:
                        prep_pair(moving, gain, g0, x, j - 1)
                dve.wait_ge(evicted, count.sent[evicted])
                prep_pair(moving, gain, g0, x, COUNT[name] - 1)

            TILE0, TILE1 = slice(0, P), slice(P, 3 * P)

            dve.wait_ge(got_par, 16)
            for i in range(KT // 2):
                dve.wait_ge(got_x[i], 16)
                prep_pair(A, "mix_norm_g", 0, x, i)
                if i == 0:
                    split_lo(0, 0)
            split_lo(1, 1)

            def first_chunk(j):
                ahead("w_in", j, j % U)
                if j == 0:
                    token_norm()
                evict("w_in", j, j % U, pair_at(qkv, j))

            for j in range(W_IN_Q):
                first_chunk(j)
                if j == 1:
                    dve.wait_ge(got_small, count.next(got_small, 16 * 4))
                    mul(lam_mul[:], lam_in[:, 0::2, :], lam_in[:, 1::2, :]).then_inc(dve_own, count.one(dve_own))
                    dve.wait_ge(dve_own, count.sent[dve_own])
                    dve.tensor_reduce(lam_dot[:], lam_mul[:], AX_X, ALU.add).then_inc(lam_dots_done, 1)
                    dve.tensor_scalar(subln_g[:], pcol("diff_subln_g"), 1.0 - LAMBDA_INIT, None, ALU.mult).then_inc(dve_own, count.one(dve_own))
                if j == 2:
                    dve.wait_ge(lam_exp_done, count.next(lam_exp_done))
                    fused(neg_lam[:], lam_exp[:, 1:2], LAMBDA_INIT, lam_exp[:, 0:1], ALU.subtract, ALU.subtract).then_inc(dve_own, count.one(dve_own))
                if j == 3:
                    dve.wait_ge(got_mem, 16)
                if j == 4:
                    prep(B, "mem_norm_g", src=mem_t)
                    token_norm(rstd_mem)

            def score_tiles(s, bias):
                for t, cols in ((1, TILE1), (0, TILE0)):
                    for b in range(4 if t else 2):
                        maps = maps_of(b, t)
                        dve.wait_ge(full_dve, count.next(full_dve))
                        fused(s[:, maps.start:maps.stop:2, cols], as_tiles(D[b][:], (t + 1) * P), QK_SCALE,
                                        bias(maps, slice(0 if t else P, 2 * P)), ALU.mult, ALU.add).then_inc(drained_dve, count.one(drained_dve))
                    dve.wait_ge(drained_dve, count.sent[drained_dve])
                    yield t, cols

            def mem_keys(j):
                ahead("w_ck", j, j % U)
                evict("w_ck", j, j % U, pair_at(mem_k, j), rstd_mem)

            def mem_values(j):
                ahead("w_cv", j, j % U)
                evict("w_cv", j, j % U, mem_v_t[:, j % 2, :, :], rstd_mem)

            def reciprocals():
                dve.wait_ge(exp_done, count.next(exp_done, 2))
                dve.reciprocal(row_rec[:], row_sum[:]).then_inc(dve_own, count.one(dve_own))
                dve.wait_ge(dve_own, count.sent[dve_own])

            dve.wait_ge(got_bias, count.next(got_bias, 16))
            for t, cols in score_tiles(scores, lambda maps, c: bias_tab[:, maps.start:maps.stop:2, c]):
                negate_max(scores, t, cols)
            first_chunk(6)
            reciprocals()
            normalise(scores, 1, TILE1, 2 * P).then_inc(dve_own, count.one(dve_own))
            normalise(scores, 0, TILE0, P).then_inc(probs_done, 1)
            for j in (7, 8, 9):
                first_chunk(j)
            for t, cols in score_tiles(scores, lambda maps, c: bias_tab[:, 8 + maps.start // 2:8 + maps.stop // 2, c]):
                negate_max(scores, t, cols)
            first_chunk(10)
            first_chunk(11)
            reciprocals()
            second = row_rec[:, :, 1::2]
            dve.tensor_scalar(second, second, neg_lam[:, 0:1], None, ALU.mult).then_inc(dve_own, count.one(dve_own))
            dve.wait_ge(dve_own, count.sent[dve_own])
            normalise(scores, 1, TILE1, 2 * P).then_inc(dve_own, count.one(dve_own))
            normalise(scores, 0, TILE0, P).then_inc(dve_own, count.one(dve_own))
            dve.wait_ge(dve_own, count.sent[dve_own])
            add(scores[:, 0:4, :], scores[:, 0::2, :], scores[:, 1::2, :]).then_inc(probs_done, 1)
            mean(STAT, 4 * P)
            refine(rstd)
            mul(att_a[:], att_a[:], over(rstd[:], 4)).then_inc(mixed_ready, count.one(mixed_ready))
            mem_keys(0)
            mem_keys(1)
            dve.wait_ge(mixed_ready, count.sent[mixed_ready])
            lo_parts(A, 0, [att_a[:, f, :] for f in range(4)], [pcol("moba_out_g", f) for f in range(4)])
            for b in range(2):
                mean(b, P, 2 * T)
                refine(mean_sq, 2 * T)
                tiles = att_b[:, 2 * b:2 * b + 2, :]
                mul(tiles, tiles, as_tiles(mean_sq[:])).then_inc(mixed_ready, count.one(mixed_ready))
                dve.wait_ge(mixed_ready, count.sent[mixed_ready])
            mem_keys(2)
            lo_parts(A, 4, [att_b[:, f, :] for f in range(4)], [subln_g[:, 0:1]] * 4)
            mem_keys(3)
            residual("w_out", C, "cross_norm_g")

            for j in range(COUNT["w_cq"]):
                ahead("w_cq", j, j % U)
                if j == 0:
                    token_norm()
                evict("w_cq", j, j % U, pair_at(q_mem, j))
            for b in range(4):
                dve.wait_ge(full_dve, count.next(full_dve))
                dve.tensor_scalar(scores_mem[:, 2 * b:2 * b + 2, :], as_tiles(D[b][:]), 0.0625, None, ALU.mult).then_inc(drained_dve, count.one(drained_dve))
            dve.wait_ge(drained_dve, count.sent[drained_dve])
            negate_max(scores_mem, 0, slice(0, T))
            mem_values(0)
            dve.wait_ge(exp_done, count.next(exp_done))
            dve.reciprocal(row_rec[:, 0, :], row_sum[:, 0, :]).then_inc(dve_own, count.one(dve_own))
            dve.wait_ge(dve_own, count.sent[dve_own])
            normalise(scores_mem, 0, slice(0, T), T).then_inc(probs_done, 1)
            for j in (1, 2, 3):
                mem_values(j)
            for h in range(4):
                dve.wait_ge(x_hi_done, count.taken[x_hi_done] + 2)
                lo_parts(A, 2 * h, [D[2 + h % 2][:, d * T:(d + 1) * T] for d in range(2)])
            residual("w_co", B, "ffn_norm_g")

            def hidden_lo(j, jm, ring):
                dve.wait_ge(hid_hi_done, count.next(hid_hi_done))
                dve.wait_ge(hid_done, count.sent[hid_done])
                sub(tile_at(hid_lo, j), ring[:, jm % U, :], tile_at(hid_hi, j).bitcast(F32)).then_inc(hid_split, 1)

            def down(layer, between=None):
                name = f"down{layer}"

                def body(j, jm):
                    ahead(name, j, jm)
                    if between and isinstance(j, int) and j < 2:
                        between(j)
                count.each(COUNT[name], body)
                for b in range(4):
                    if b < 3:
                        dve.wait_ge(full_dve, count.next(full_dve))
                    else:
                        dve.wait_ge(chunk_done, FIRST[name] + COUNT[name])
                    pair = x[:, 2 * b:2 * b + 2, :]
                    add(pair, pair, as_tiles(D[b][:])).then_inc(x_ready, count.one(x_ready))
                dve.wait_ge(x_ready, count.sent[x_ready])

            def rope_angles(i):
                two_pi, magic = 2.0 * math.pi, 1.5 * 2.0 ** 23
                c1 = 6.28125
                c2 = float(np.round((two_pi - c1) * 2.0 ** 21) * 2.0 ** -21)
                c3 = two_pi - c1 - c2
                shift, r = (0.0, 0.5 * math.pi)[i], rope_r[:, i, :]

                def step(instruction):
                    instruction.then_inc(dve_own, count.one(dve_own))
                    dve.wait_ge(dve_own, count.sent[dve_own])

                if i == 0:
                    dve.wait_ge(got_rope, 16)
                    step(dve.tensor_copy(rope_a[:], rope_i[:]))
                    step(mul(rope_a[:], rope_a[:], inv_freq.broadcast_to([P, T])))
                step(dve.tensor_scalar(rope_n[:], rope_a[:], shift, 1.0 / two_pi, ALU.add, ALU.mult))
                step(dve.tensor_scalar(rope_n[:], rope_n[:], magic, None, ALU.add))
                step(dve.tensor_scalar(rope_n[:], rope_n[:], magic, None, ALU.subtract))
                step(fused(r, rope_n[:], -c1, rope_a[:], ALU.mult, ALU.add))
                step(fused(r, rope_n[:], -c2, r, ALU.mult, ALU.add))
                step(fused(r, rope_n[:], -c3, r, ALU.mult, ALU.add))
                if shift:
                    step(dve.tensor_scalar(r, r, shift, None, ALU.add))
                limit = float(np.nextafter(np.float32(math.pi), np.float32(0)))
                step(dve.tensor_scalar(r, r, limit, -limit, ALU.min, ALU.max))
                if shift:
                    dve.tensor_copy(rope_n[:, 0:1], r[:, 0:1]).then_inc(angles_done, 1)

            def gated_hid(j, jm):
                dve.wait_ge(act_done, count.next(act_done))
                dve.wait_ge(evicted, j + (FIRST_OUT["up0"] + 1))
                mul(hid[:, jm % U, :], gate_act[:, jm % U, :], up_z[:, jm % U, :]).then_inc(hid_done, count.one(hid_done))

            def gated_body(j, jm):
                early = isinstance(j, int)
                ahead("up0", j, jm)
                if early and j == 0:
                    token_norm()
                z = bank_of("up0", j, jm)
                mul(gate_z[:, jm, :], z[:, 0, :], rstd[:]).then_inc(gate_done, 1)
                mul(up_z[:, jm, :], z[:, 1, :], rstd[:]).then_inc(evicted, count.one(evicted))
                if not early or j >= 1:
                    gated_hid(j - 1, jm + 2)
                if not early or j >= 2:
                    hidden_lo(j - 2, jm + 1, hid)

            count.each(FT, gated_body)
            gated_hid(FT - 1, (FT - 1) % U)
            hidden_lo(FT - 2, (FT - 2) % U, hid)
            hidden_lo(FT - 1, (FT - 1) % U, hid)
            down(0, rope_angles)
            token_norm()
            for i in range(KT // 2):
                for f in (2 * i, 2 * i + 1):
                    last = fused(x[:, f, :], x[:, f, :], pcol("final_norm_g", f), rstd[:], ALU.mult, ALU.mult)
                    if f == 2 * i:
                        last.then_inc(dve_own, count.one(dve_own))
                last.then_inc(x_normed, count.one(x_normed))
            dve.wait_ge(x_normed, count.sent[x_normed])
            prep(A, "mix_norm_2")

            def hy_evict(j):
                ahead("hy_in", j, j % U)
                if j == 0:
                    token_norm()
                evict("hy_in", j, j % U, hy[:, 2 * j:2 * j + 2, :])

            dve.memset(hy_conv_in[:, :, 0:2], 0.0).then_inc(dve_own, count.one(dve_own))
            hy_evict(0)
            hy_evict(1)
            hy_evict(2)
            hy_evict(3)
            tiles_of = (slice(0, 2), slice(2, 4), slice(4, 5))
            dve.wait_ge(evicted, count.sent[evicted])
            for i in range(3):
                width = (2, 2, 1)[i] * T
                mean(i, 64, width)
                refine(mean_sq, width)
                for f in range(tiles_of[i].start, tiles_of[i].stop):
                    gain = pcol("hy_k_norm_2" if f == 4 else "hy_q_norm_2")
                    at_f = (f - 2 * i) * T
                    last = fused(hy_qk[:, f, :], hy[:, f, :], gain, mean_sq[:, at_f:at_f + T], ALU.mult, ALU.mult)
                    if f + 1 < tiles_of[i].stop:
                        last.then_inc(dve_own, count.one(dve_own))
                last.then_inc(qk_normed, count.one(qk_normed))
                dve.wait_ge(qk_normed, count.sent[qk_normed])
            hy_evict(4)
            dve.wait_ge(rope_done, 1)
            for i in range(3):
                tiles = tiles_of[i]
                dve.wait_ge(full_dve, count.next(full_dve))
                n = tiles.stop - tiles.start
                mul(hy_rot[:, tiles, :], as_tiles(D[i][:, 0:n * T]), over(sin_t[:], n)).then_inc(drained_dve, count.one(drained_dve))
            mul(hy_qk[:], hy_qk[:], over(cos_t[:], 5)).then_inc(dve_own, count.one(dve_own))
            dve.wait_ge(dve_own, count.sent[dve_own])
            dve.wait_ge(drained_dve, count.sent[drained_dve])
            add(hy_qk[:], hy_qk[:], hy_rot[:]).then_inc(qk_rotated, 1)
            hy_evict(5)
            for t, cols in score_tiles(hy_scores, lambda maps, c: over(window[:, c], len(maps))):
                dve.tensor_reduce(row_max[:, t, :], hy_scores[:, :, cols], AX_X, ALU.max).then_inc(dve_own, count.one(dve_own))
                dve.wait_ge(dve_own, count.sent[dve_own])
                dve.tensor_tensor(row_max[:, t, :], row_max[:, t, :], sinks[:], ALU.max).then_inc(dve_own, count.one(dve_own))
                dve.wait_ge(dve_own, count.sent[dve_own])
                dve.tensor_scalar(neg_max[:, t, :], row_max[:, t, :], -1.0, None, ALU.mult).then_inc(dve_own, count.one(dve_own))
                sub(hy_sink[:, t, :], sinks[:], row_max[:, t, :]).then_inc(max_done, 1)
            hy_evict(6)
            dve.wait_ge(exp_done, count.next(exp_done, 2))
            dve.wait_ge(sink_done, count.next(sink_done, 2))
            add(row_sum[:], row_sum[:], hy_sink[:]).then_inc(dve_own, count.one(dve_own))
            dve.wait_ge(dve_own, count.sent[dve_own])
            dve.reciprocal(row_rec[:], row_sum[:]).then_inc(dve_own, count.one(dve_own))
            dve.wait_ge(dve_own, count.sent[dve_own])
            normalise(hy_scores, 1, TILE1, 2 * P).then_inc(dve_own, count.one(dve_own))
            normalise(hy_scores, 0, TILE0, P).then_inc(probs_done, 1)
            hy_evict(7)
            hy_evict(8)
            dve.wait_ge(evicted, count.sent[evicted])
            mul(hy_conv_in[:, :, 2:2 + T], hy[:, 10:14, :], hy[:, 14:18, :]).then_inc(dve_own, count.one(dve_own))
            dve.wait_ge(dve_own, count.sent[dve_own])
            for tap in range(3):
                for f in range(4):
                    w = pcol("hy_conv_w_2", tap * 4 + f)
                    src = hy_conv_in[:, f, tap:tap + T]
                    if tap == 0:
                        dve.tensor_scalar(hy_conv[:, f, :], src, w, None, ALU.mult).then_inc(dve_own, count.one(dve_own))
                    else:
                        fused(hy_conv[:, f, :], src, w, hy_conv[:, f, :], ALU.mult, ALU.add).then_inc(dve_own, count.one(dve_own))
                dve.wait_ge(dve_own, count.sent[dve_own])
            for i in range(2):
                tiles = hy_conv[:, 2 * i:2 * i + 2, :]
                mul(tiles, tiles, hy[:, 6 + 2 * i:8 + 2 * i, :]).then_inc(mixed_ready, count.one(mixed_ready))
            dve.wait_ge(mixed_ready, count.sent[mixed_ready])
            lo_parts(B, 0, [hy_att[:, f, :] for f in range(4)])
            lo_parts(B, 4, [hy_conv[:, f, :] for f in range(4)])
            residual("hy_out", A, "ffn_norm_2")

            def conv_ffn(layer, ple_moving):
                name = f"up{layer}"

                def tap_column(tap, f, j):
                    return par[:, bass.ds(j + (CONV_COL + ((layer - 1) * 3 + tap) * 2 * FT + f * FT), 1)]

                def taps(j, jm):
                    m = jm % U
                    dve.wait_ge(tap_done, count.next(tap_done))
                    dve.wait_ge(evicted, j + (FIRST_OUT[name] + 1))
                    for f in range(2):
                        o = conv_out[:, m, f, :]
                        fused(o, conv_in[:, m, f, 1:1 + T], tap_column(1, f, j), o, ALU.mult, ALU.add).then_inc(dve_own, count.one(dve_own))
                    dve.wait_ge(dve_own, count.sent[dve_own])
                    for f in range(2):
                        o = conv_out[:, m, f, :]
                        last = fused(o, conv_in[:, m, f, 0:T], tap_column(0, f, j), o, ALU.mult, ALU.add)
                        if f == 0:
                            last.then_inc(conv_done, 1)
                        else:
                            last.then_inc(dve_own, count.one(dve_own))

                def conv_hidden(j, jm):
                    dve.wait_ge(act_done, count.next(act_done))
                    dve.wait_ge(dve_own, count.sent[dve_own])
                    mul(conv_hid[:, jm % U, :], conv_gelu[:, jm % U, :], conv_out[:, jm % U, 1, :]).then_inc(hid_done, count.one(hid_done))

                def body(j, jm):
                    early = isinstance(j, int)
                    if early and j == 0:
                        token_norm()
                    mul(conv_in[:, jm, :, 2:2 + T], bank_of(name, j, jm), over(rstd[:], 2)).then_inc(evicted, count.one(evicted))
                    if not early or j >= 2:
                        conv_hidden(j - 2, jm + 1)
                    if not early or j >= 3:
                        hidden_lo(j - 3, jm, conv_hid)
                    if not early or j >= 1:
                        taps(j - 1, jm + 2)
                    ahead(name, j, jm)

                dve.memset(conv_in[:, :, :, 0:2], 0.0).then_inc(dve_own, count.one(dve_own))
                dve.wait_ge(got_conv, 16)
                count.each(FT, body, 4)
                m = FT % U
                conv_hidden(FT - 2, m + 1)
                hidden_lo(FT - 3, m, conv_hid)
                taps(FT - 1, m + 2)
                conv_hidden(FT - 1, m + 2)
                hidden_lo(FT - 2, m + 1, conv_hid)
                hidden_lo(FT - 1, m + 2, conv_hid)
                dve.wait_ge(p_hi_done, count.next(p_hi_done))
                sub(flat(p_lo), flat(p_in), flat(p_hi).bitcast(F32)).then_inc(p_split, 1)
                down(layer)
                prep(ple_moving, "ple_norm_2", (layer - 1) * KT)
                gate = f"gate{layer}"
                ahead(f"proj{layer}", 0, 0)

                def finish(j):
                    dve.wait_ge(act_done, count.next(act_done))
                    m, pair = ple_mul[:, j % 2, :, :], x[:, 2 * j:2 * j + 2, :]
                    mul(m, ple_sig[:, j % 2, :, :], as_tiles(D[j][:])).then_inc(drained_dve, count.one(drained_dve))
                    dve.wait_ge(drained_dve, count.sent[drained_dve])
                    add(pair, pair, m).then_inc(x_gated, count.one(x_gated))

                for j in range(COUNT[gate]):
                    ahead(gate, j, j % U)
                    if j == 0:
                        token_norm()
                    evict(gate, j, j % U, ple_z[:, j % 2, :, :])
                    if j >= 1:
                        finish(j - 1)
                    if layer == 1 and j >= 2:
                        prep_pair(A, "mix_norm_2", KT, x, j - 2)
                finish(3)
                if layer == 1:
                    dve.wait_ge(x_gated, count.sent[x_gated])
                    prep_pair(A, "mix_norm_2", KT, x, 2)
                    prep_pair(A, "mix_norm_2", KT, x, 3)

            conv_ffn(1, B)

            def gla_evict(j):
                ahead("gla_in", j, j % U)
                if j == 0:
                    token_norm()
                if j < 2:
                    fused(gla[:, 2 * j:2 * j + 2, :], bank_of("gla_in", j, j % U), float(P) ** -0.5, over(rstd[:], 2),
                                    ALU.mult, ALU.mult).then_inc(evicted, count.one(evicted))
                else:
                    evict("gla_in", j, j % U, gla[:, 2 * j:2 * j + 2, :])

            sums = flat(gla_g)

            def blocks(ap, level):
                return flat(ap).rearrange("p (b h t) -> p b h t", h=2, t=level)

            def exponents(i):
                e = (gla_e, gla_z)[i % 2]
                if i <= len(LEVELS):
                    level = LEVELS[i - 1]
                    s, to = blocks(gla_g, level), blocks(e, level)
                    n = 4 * T // (2 * level)
                    middle = s[:, :, 0, level - 1:level].broadcast_to([P, n, level])
                    if level == 64:
                        dve.tensor_copy(to[:, :, 1, :], s[:, :, 1, :]).then_inc(dve_own, count.one(dve_own))
                    else:
                        sub(to[:, :, 1, :], s[:, :, 1, :], middle).then_inc(dve_own, count.one(dve_own))
                    sub(to[:, :, 0, :], middle, s[:, :, 0, :]).then_inc(decay_done, 1)
                    return
                s4 = gla_g[:].rearrange("p h (c t) -> p h c t", t=64)
                e4 = e[:].rearrange("p h (c t) -> p h c t", t=64)
                for c in range(2):
                    sub(e4[:, :, c, :], s4[:, :, c, 63:64].broadcast_to([P, 4, 64]), s4[:, :, c, :]).then_inc(dve_own, count.one(dve_own))
                dve.wait_ge(dve_own, count.sent[dve_own])
                add(e4[:, :, 0, :], e4[:, :, 0, :], s4[:, :, 1, 63:64].broadcast_to([P, 4, 64])).then_inc(dve_own, count.one(dve_own))
                dve.tensor_copy(e4[:, :, 2, :], s4[:, :, 2, :]).then_inc(dve_own, count.one(dve_own))
                add(e4[:, :, 3, :], s4[:, :, 3, :], s4[:, :, 2, 63:64].broadcast_to([P, 4, 64])).then_inc(decay_done, 1)

            def decayed(i):
                e = (gla_e, gla_z)[i % 2]
                dve.wait_ge(expo_done, count.next(expo_done))
                level = LEVELS[i - 1] if i <= len(LEVELS) else P
                to, ev = blocks(gla_w[i % 2], level), blocks(e, level)
                q, k = (flat(gla[:, f:f + 4, :]).rearrange("p (b h t) -> p b h t", h=2, t=level) for f in (0, 4))
                mul(to[:, :, 0, :], k[:, :, 0, :], ev[:, :, 0, :]).then_inc(dve_own, count.one(dve_own))
                mul(to[:, :, 1, :], q[:, :, 1, :], ev[:, :, 1, :]).then_inc(level_ready, count.one(level_ready))

            def keep_level(i):
                dve.wait_ge(drained_dve, count.sent[drained_dve])
                for t in range(TT):
                    dve.wait_ge(full_dve, count.next(full_dve))
                    dve.copy_predicated(gla_s[:, t, :, :], over(level_mask[:, i, :], 4),
                                                  as_tiles(D[(2 * i + t) % 4][:], P)).then_inc(drained_dve, count.one(drained_dve))

            dve.wait_ge(got_gla, count.next(got_gla, 16 * 3))
            dve.tensor_copy(flat(level_mask), level_mask_f[:]).then_inc(dve_own, count.one(dve_own))
            g0 = PCOL["mix_norm_2"] + KT
            mul(gla_wlr[:], gla_wlr[:], along(par[:, g0:g0 + KT], 16)).then_inc(lr_scaled, 1)
            restart = flat(gla_w[0])
            dve.memset(restart, 1.0).then_inc(dve_own, count.one(dve_own))
            dve.memset(gla_s[:], 0.0).then_inc(dve_own, count.one(dve_own))
            dve.wait_ge(dve_own, count.sent[dve_own])
            dve.memset(restart[:, 0::64], 0.0).then_inc(dve_own, count.one(dve_own))
            gla_evict(0)
            dve.wait_ge(full_dve, count.next(full_dve))
            mul(gla_lr[0:16, :], D[0][0:16, 0:T], rstd[0:16, :]).then_inc(lr_ready, 1)
            gla_evict(1)
            for b in range(2):
                dve.wait_ge(full_dve, count.next(full_dve))
                for f in range(2):
                    h = 2 * b + f
                    last = dve.tensor_scalar(gla_z[:, h, :], D[1 + b][:, f * T:(f + 1) * T], pcol("gla_gate_bias_2", h), None, ALU.add)
                    if f == 0:
                        last.then_inc(dve_own, count.one(dve_own))
                last.then_inc(drained_dve, count.one(drained_dve))
            dve.wait_ge(dve_own, count.sent[dve_own])
            dve.wait_ge(drained_dve, count.sent[drained_dve])
            fused(flat(gla_e), flat(gla_z), -1.0, flat(gla_z), ALU.mult, ALU.min).then_inc(logit_done, 1)
            gla_evict(2)
            dve.wait_ge(soft_done, count.next(soft_done))
            fused(flat(gla_z), flat(gla_z), 0.0, flat(gla_e), ALU.min, ALU.subtract).then_inc(dve_own, count.one(dve_own))
            dve.wait_ge(dve_own, count.sent[dve_own])
            dve.tensor_tensor_scan(sums, restart, flat(gla_z), 0.0, ALU.mult, ALU.add).then_inc(dve_own, count.one(dve_own))
            dve.wait_ge(dve_own, count.sent[dve_own])
            exponents(1)
            gla_evict(3)
            dve.wait_ge(evicted, count.sent[evicted])
            evictions = {1: 4, 2: 5, 3: 6, 5: 7, 7: 8}
            for i in range(1, len(LEVELS) + 1):
                if i > 1:
                    dve.wait_ge(level_ready, count.sent[level_ready])
                exponents(i + 1)
                decayed(i)
                keep_level(i - 1)
                if i in evictions:
                    gla_evict(evictions[i])
            decayed(len(LEVELS) + 1)
            keep_level(len(LEVELS))
            gla_evict(9)
            dve.wait_ge(full_dve, count.next(full_dve))
            dve.tensor_copy(gla_s[:, 2, :, :], as_tiles(D[0][:], P)).then_inc(gla_scores_done, 1)
            gla_evict(10)
            for pair in range(2):
                mean(pair, 2 * P, 2 * T)
                refine(mean_sq, 2 * T)
                for f in range(4):
                    o = gla_o[:, 4 * pair + f, :]
                    scale = mean_sq[:, (f // 2) * T:(f // 2 + 1) * T]
                    fused(o, o, pcol("gla_o_norm_2", f % 2), scale, ALU.mult, ALU.mult).then_inc(dve_own, count.one(dve_own))
                dve.wait_ge(dve_own, count.sent[dve_own])
                if pair == 1:
                    gla_evict(11)
                dve.wait_ge(silu_done, count.next(silu_done))
                o = gla_o[:, 4 * pair:4 * pair + 4, :]
                mul(o, o, gla[:, 16 + 4 * pair:20 + 4 * pair, :]).then_inc(mixed_ready, count.one(mixed_ready))
            dve.wait_ge(mixed_ready, count.sent[mixed_ready])
            lo_parts(B, 0, [gla_o[:, f, :] for f in range(8)])
            residual("gla_out", A, "ffn_norm_2", KT)
            conv_ffn(2, B)

        @block.gpsimd
        def _(pool):
            count = Counts(pool)

            def split_lo(c, slot):
                if isinstance(c, int) and c >= CHUNKS:
                    return
                pool.wait_ge(hi_done, c + 1)
                cols = slice(DVE_COLS, CHUNK)
                pool.tensor_tensor(w_lo[:, slot, cols], raw[:, slot, cols], w_hi[:, slot, cols].bitcast(F32), ALU.subtract).then_inc(lo_pool, 1)

            def ahead(name, j, jm):
                split_lo(j + (FIRST[name] + AHEAD), (FIRST[name] + jm + AHEAD) % U)

            def add_squares(i):
                pool.wait_ge(sq_done, count.next(sq_done))
                if i == 0:
                    return
                if i > 1:
                    pool.wait_ge(sq_added, count.sent[sq_added])
                total = pool.tensor_tensor(sq_sum[:], sq_sum[:], sq[:, i % 2, :], ALU.add)
                if i == 3:
                    total.then_inc(sq_total, 1)
                else:
                    total.then_inc(sq_added, count.one(sq_added))

            def all_squares():
                for i in range(KT // 2):
                    add_squares(i)

            def residual(name):
                for j in range(COUNT[name]):
                    ahead(name, j, j % U)
                    add_squares(j)

            def stream(name):
                count.each(COUNT[name], lambda j, jm: ahead(name, j, jm))

            pool.memset(table[N_BUCKETS:N_BUCKETS + 1, :], MASKED).then_inc(masked_row, count.one(masked_row))
            pool.wait_ge(masked_row, count.sent[masked_row])
            split_lo(0, 0)
            all_squares()
            split_lo(1, 1)

            for j in range(W_IN_Q):
                ahead("w_in", j, j % U)
                if j == 3:
                    all_squares()
            for j in range(W_IN_Q, COUNT["w_in"]):
                ahead("w_in", j, j % U)
            stream("w_ck")
            residual("w_out")
            stream("w_cq")
            stream("w_cv")
            residual("w_co")
            stream("up0")
            stream("down0")
            all_squares()
            all_squares()
            stream("hy_in")
            residual("hy_out")
            for layer in (1, 2):
                stream(f"up{layer}")
                stream(f"down{layer}")
                all_squares()
                stream(f"proj{layer}")
                stream(f"gate{layer}")
                if layer == 1:
                    all_squares()
                    stream("gla_in")
                    residual("gla_out")


def constants():
    c = np.zeros((P, N_CONST), np.float32)
    i = np.arange(P)
    c[i, C_IDENT + i] = 1.0
    c[:, C_ONES:C_ONES + P] = 1.0
    c[:, C_HALF:C_HALF + P] = (i[:, None] // 64 == i[None, :] // 64)
    low = i[i % 64 < 32]
    c[low + 32, C_ROT + low] = -1.0
    c[low, C_ROT + low + 32] = 1.0
    c[(i + 64) % P, C_SWAP + i] = 1.0
    dist = P + i[:, None] - np.arange(2 * P)[None, :]
    c[:, C_WIN:C_WIN + 2 * P] = np.where((dist >= 0) & (dist < P), 0.0, MASKED)
    exponent = -np.arange(0, 64, 2, dtype=np.float32) / np.float32(64)
    c[:, C_FREQ] = np.power(np.float32(10000.0), exponent)[i % 32]
    dist = N_DIST - P - 1 - np.arange(N_DIST)
    exact = N_BUCKETS // 2
    ratio = np.log(np.maximum(dist, exact).astype(np.float32) / np.float32(exact)) / np.float32(math.log(P / exact))
    large = np.minimum(exact + (ratio * np.float32(N_BUCKETS - exact)).astype(np.int32), N_BUCKETS - 1)
    bucket = np.where(dist < 0, N_BUCKETS, np.where(dist < exact, dist, large))
    onehot = np.zeros((N_BUCKETS + 1, N_DIST), np.float32)
    onehot[bucket, np.arange(N_DIST)] = 1.0
    s, t = i[:, None], i[None, :]
    masks = [s == t] + [(s // (2 * n) == t // (2 * n)) & (s % (2 * n) < n) & (t % (2 * n) >= n) for n in LEVELS]
    return {"const": c, "onehot": onehot, "level_mask": np.concatenate(masks, axis=1).astype(np.float32)}


def layout(inputs):
    a = {name: np.asarray(v) for name, v in inputs.items()}

    def features_first(v):
        return v.T.reshape(-1, P, v.shape[0]).transpose(1, 0, 2)

    def over_outputs(w):
        return w.reshape(KT, P, -1, 2 * P).transpose(2, 1, 0, 3).reshape(-1, P, CHUNK)

    def gate_and_up(gate, up):
        both = np.stack([gate.reshape(KT, P, FT, P), up.reshape(KT, P, FT, P)], axis=3)
        return both.transpose(2, 1, 0, 3, 4).reshape(-1, P, CHUNK)

    def over_k(w):
        return w.reshape(-1, 2, P, DM).transpose(0, 2, 1, 3).reshape(-1, P, CHUNK)

    up2, gla_w = a["ffn_w_up_2"], a["gla_w_in_2"][0]
    low_rank = 2 * DM
    weights = {
        "w_in": over_outputs(a["w_in"][0]), "w_ck": over_outputs(a["w_ck"][0]), "w_cv": over_outputs(a["w_cv"][0]),
        "w_out": over_outputs(a["w_out"][0]), "w_cq": over_outputs(a["w_cq"][0]), "w_co": over_outputs(a["w_co"][0]),
        "up0": gate_and_up(a["w_gate"][0], a["w_up"][0]), "down0": over_k(a["w_down"][0]),
        "hy_in": over_outputs(a["hy_w_in_2"][0]), "hy_out": over_outputs(a["hy_w_out_2"][0]),
        "gla_in": over_outputs(np.concatenate([gla_w[:, :low_rank], gla_w[:, low_rank + 16:]], axis=1)),
        "gla_out": over_outputs(a["gla_w_out_2"][0])}
    for i in range(2):
        weights[f"up{i + 1}"] = gate_and_up(up2[i][:, :FF], up2[i][:, FF:])
        weights[f"down{i + 1}"] = over_k(a["ffn_w_down_2"][i])
        weights[f"proj{i + 1}"] = over_k(a["ple_w_proj_2"][i])
        weights[f"gate{i + 1}"] = over_outputs(a["ple_w_gate_2"][i])
    twice = ("hy_q_norm_2", "hy_k_norm_2")
    vectors = [np.concatenate([a[name].reshape(-1)] * (2 if name in twice else 1)).reshape(-1, P) for name, _ in PARAMS]
    vectors += [a["ffn_conv_w_2"].reshape(-1, P), a["ffn_conv_b_2"].reshape(-1, P)]
    moved = {
        "weights": np.concatenate([weights[name] for name, _, _ in PHASES]),
        "par": np.concatenate(vectors).T, "x_t": features_first(a["x"][0]), "mem_t": features_first(a["mem"][0]),
        "p_t": np.stack([features_first(v[0]) for v in a["p_2"]]),
        "gla_w_lr": gla_w[:, low_rank:low_rank + 16].reshape(KT, P, 16).transpose(1, 0, 2)}
    for name in ("rel_bias_table", "diff_lambda", "hy_sinks_2", "positions_2", "gla_w_gate_up_2"):
        moved[name] = a[name]
    return {name: np.ascontiguousarray(v) for name, v in moved.items()}


def kernel(**inputs):
    import concourse.bacc as bacc
    from concourse.bass_utils import run_bass_kernel_spmd

    arrays = layout(inputs)
    arrays.update(constants())
    nc = bacc.Bacc("TRN2", target_bir_lowering=False, num_devices=1)
    io = {name: nc.dram_tensor(name, a.shape, mybir.dt.from_np(a.dtype), kind="ExternalInput").ap() for name, a in arrays.items()}
    out = nc.dram_tensor("out", (P, KT, T), F32, kind="ExternalOutput").ap()
    program(nc, io, out)
    r = run_bass_kernel_spmd(nc, [arrays], core_ids=[0])
    return r.results[0]["out"].transpose(2, 1, 0).reshape(1, T, DM)
```

```python
from contextlib import ExitStack
import math

import numpy as np
import concourse.bass as bass
from concourse import mybir

F32 = mybir.dt.float32
F32R = mybir.dt.float32r
I32 = mybir.dt.int32
U8 = mybir.dt.uint8
ALU = mybir.AluOpType
ACT = mybir.ActivationFunctionType
AX_X = mybir.AxisListType.X

P = 128
T = 256
TT = T // P
DM = 1024
KT = DM // P
FF = 2816
FT = FF // P
U = 3
CHUNK = 16 * P
DVE_COLS = 1152
AHEAD = 2
EPS = 1e-6
MASKED = -1e30
QK_SCALE = 0.125
LAMBDA_INIT = 0.8 - 0.6 * math.exp(-0.3 * 0)
N_DIST = 384
N_BUCKETS = 32
SKEW = 16
ATT_HEADS = 12
LEVELS = (64, 32, 16, 8, 4, 2, 1)

C_IDENT, C_ONES, C_HALF, C_ROT, C_SWAP, C_WIN, C_FREQ = 0, 128, 256, 384, 512, 640, 896
N_CONST = 897

PARAMS = [("mix_norm_g", 8), ("moba_out_g", 4), ("diff_subln_g", 1), ("cross_norm_g", 8), ("mem_norm_g", 8),
          ("ffn_norm_g", 8), ("final_norm_g", 8), ("mix_norm_2", 16), ("ffn_norm_2", 16), ("ple_norm_2", 16),
          ("gla_o_norm_2", 2), ("gla_gate_bias_2", 4), ("hy_conv_w_2", 12), ("hy_q_norm_2", 1), ("hy_k_norm_2", 1)]
PCOL = {}
_n = 0
for _name, _rows in PARAMS:
    PCOL[_name] = _n
    _n += _rows
N_PARAM = _n
CONV_COL = N_PARAM
N_CONV = 2 * 3 * 2 * FT
CONVB_COL = CONV_COL + N_CONV
N_PCOLS = CONVB_COL + 2 * 2 * FT

PHASES = [("w_in", 12, 0), ("w_ck", 4, 0), ("w_out", 4, 0), ("w_cq", 4, 0), ("w_cv", 4, 0), ("w_co", 4, 0),
          ("up0", FT, 0), ("down0", FT // 2, 1), ("hy_in", 9, 0), ("hy_out", 4, 0), ("up1", FT, 0),
          ("down1", FT // 2, 1), ("proj1", 1, 1), ("gate1", 4, 0), ("gla_in", 12, 0), ("gla_out", 4, 0),
          ("up2", FT, 0), ("down2", FT // 2, 1), ("proj2", 1, 1), ("gate2", 4, 0)]
W_IN_Q = 6
FIRST, COUNT, FIRST_OUT = {}, {}, {}
_c = _o = 0
for _name, _k, _over_k in PHASES:
    FIRST[_name], COUNT[_name], FIRST_OUT[_name] = _c, _k, _o
    _c += _k
    _o += 0 if _over_k else _k
CHUNKS = _c


class Counts:

    def __init__(self, engine):
        self.engine, self.taken, self.sent = engine, {}, {}
        self.per_turn = {}

    def next(self, sem, events=1):
        self.taken[sem] = self.taken.get(sem, 0) + events
        return self.taken[sem]

    def one(self, sem):
        self.sent[sem] = self.sent.get(sem, 0) + 1
        return 1

    def each(self, n, body, peel=3, ahead_of_loop=None):
        def counts():
            return [(d, s, v) for d in (self.taken, self.sent) for s, v in d.items()]

        peel = min(peel, n)
        for j in range(peel):
            before = {(id(d), s): v for d, s, v in counts()}
            body(j, j % U)
        turns = (n - peel) // U
        if turns < 2:
            turns = 0
        if turns:
            start = [(d, s, v, v - before.get((id(d), s), 0)) for d, s, v in counts() if s not in self.per_turn]
            start_turn = {s: self.taken[s] for s in self.per_turn}
            if ahead_of_loop:
                ahead_of_loop()
            with self.engine.Fori(0, turns) as turn:
                for s, v in start_turn.items():
                    self.taken[s] = turn * self.per_turn[s] + v
                for u in range(U):
                    for d, s, v, step in start:
                        if step:
                            d[s] = turn * (U * step) + (v + u * step)
                    body(turn * U + (peel + u), (peel + u) % U)
            for d, s, v, step in start:
                d[s] = v + turns * U * step
            for s, v in start_turn.items():
                self.taken[s] = turns * self.per_turn[s] + v
        for j in range(peel + turns * U, n):
            body(j, j % U)


def program(nc, io, out):
    with ExitStack() as stack:
        place = {"at": (nc.sbuf_base + 31) // 32 * 32}

        def at(name, offset, shape, dtype=F32):
            return nc.alloc_sbuf_tensor_at(name, [P] + shape, dtype, offset=offset)

        def sb(name, shape, dtype=F32, size=None):
            offset = place["at"]
            nbytes = int(np.prod(shape)) * (1 if dtype == U8 else 4) if size is None else size
            place["at"] = offset + (nbytes + 31) // 32 * 32
            return at(name, offset, shape, dtype)

        raw = sb("raw", [U, CHUNK])
        w_hi = sb("w_hi", [U, CHUNK], F32R)
        w_lo = sb("w_lo", [U, CHUNK], F32R)
        x = sb("x", [KT, T])
        a_hi, a_lo = sb("a_hi", [KT, T], F32R), sb("a_lo", [KT, T], F32R)
        b_hi, b_lo = sb("b_hi", [KT, T], F32R), sb("b_lo", [KT, T], F32R)
        A, B = (a_hi, a_lo), (b_hi, b_lo)
        sq = sb("sq", [2, 2 * T])
        sq_sum = sb("sq_sum", [2 * T])
        mean_sq = sb("mean_sq", [2 * T])
        rough = sb("rough", [2 * T])
        newton = sb("newton", [2 * T])
        rstd = sb("rstd", [T])
        rstd_mem = sb("rstd_mem", [T])
        rstd_tok = sb("rstd_tok", [TT])
        rstd_mem_tok = sb("rstd_mem_tok", [TT])
        const = sb("const", [N_CONST])
        level_mask = sb("level_mask", [len(LEVELS) + 1, P], U8)
        par = sb("par", [N_PCOLS])
        cos_t = sb("cos_t", [T])
        sin_t = sb("sin_t", [T])
        sinks = sb("sinks", [8])
        subln_g = sb("subln_g", [1])
        both_g = sb("both_g", [KT])
        neg_lam = sb("neg_lam", [1])
        lam_dot = sb("lam_dot", [2])
        lam_exp = sb("lam_exp", [2])
        row_max = sb("row_max", [2, 8])
        neg_max = sb("neg_max", [2, 8])
        row_sum = sb("row_sum", [2, 8])
        row_rec = sb("row_rec", [2, 8])
        ident = const[:, C_IDENT:C_IDENT + P]
        ones = const[:, C_ONES:C_ONES + P]
        half_ones = const[:, C_HALF:C_HALF + P]
        rot_half = const[:, C_ROT:C_ROT + P]
        swap_half = const[:, C_SWAP:C_SWAP + P]
        window = const[:, C_WIN:C_WIN + 2 * P]
        inv_freq = const[:, C_FREQ:C_FREQ + 1]

        H = place["at"]
        H_SIZE = 52 * 1024
        TR = H + H_SIZE
        assert TR + 20 * 1024 <= nc.sbuf_usable_end, (TR + 20 * 1024, nc.sbuf_usable_end)
        KB = 1024
        qkv = at("qkv", H, [20, T])
        v_tok = at("v_tok", H + 24 * KB, [TT, DM])
        scores = at("scores", H + 32 * KB, [8, 3 * P])
        probs_t = at("probs_t", H + 44 * KB, [4, 512])
        att_a = at("att_a", H, [4, T])
        mem_v = at("mem_v", H + 16 * KB, [TT, DM])
        att_b = at("att_b", H + 12 * KB, [4, T])
        bias_tab = at("bias_tab", TR, [ATT_HEADS, 2 * P])
        mem_k = at("mem_k", TR + 12 * KB, [KT, T])
        lam_in = at("lam_in", H + 10 * KB, [4, 64])
        lam_mul = at("lam_mul", H + 11 * KB, [2, 64])
        bias_rows = at("bias_rows", H + 24 * KB, [N_DIST])
        onehot = at("onehot", H + 42 * KB, [N_DIST])
        table = at("table", H + 43 * KB + 512, [ATT_HEADS])
        mem_t = at("mem_t", H + 44 * KB, [KT, T])
        q_mem = at("q_mem", H + 24 * KB, [KT, T])
        C = (at("c_hi", H + 32 * KB, [KT, T], F32R), at("c_lo", H + 44 * KB, [KT, T], F32R))
        scores_mem = at("scores_mem", H + 32 * KB, [8, T])
        hid_hi = at("hid_hi", H, [FT, T], F32R)
        gain_sq = at("gain_sq", H + 44 * KB, [2, 2 * T])
        gain_sq_sum = at("gain_sq_sum", H + 48 * KB, [2 * T])
        hid_lo = at("hid_lo", H + 22 * KB, [FT, T], F32R)
        gate_z = at("gate_z", TR, [U, T])
        up_z = at("up_z", TR + 3 * KB, [U, T])
        gate_act = at("gate_act", TR + 6 * KB, [U, T])
        hid = at("hid", TR + 9 * KB, [U, T])
        CONV_T = 2 + T
        conv_in = at("conv_in", TR, [U, 2, CONV_T])
        conv_out = at("conv_out", TR + 6208, [U, 2, T])
        conv_gelu = at("conv_gelu", TR + 6208 + 6 * KB, [U, T])
        conv_hid = at("conv_hid", TR + 6208 + 9 * KB, [U, T])
        p_in = at("p_in", H + 44 * KB, [2, T])
        p_hi = at("p_hi", H + 46 * KB, [2, T], F32R)
        p_lo = at("p_lo", H + 48 * KB, [2, T], F32R)
        ple_z = at("ple_z", TR, [2, 2, T])
        ple_sig = at("ple_sig", TR + 4 * KB, [2, 2, T])
        ple_mul = at("ple_mul", TR + 8 * KB, [2, 2, T])
        hy = at("hy", H, [18, T])
        hy_v = at("hy_v", H + 18 * KB, [TT, P])
        hy_qk = at("hy_qk", H + 39 * KB, [5, T])
        hy_cos = at("hy_cos", H + 19 * KB, [5, T])
        hy_mean = at("hy_mean", H + 24 * KB, [T])
        hy_rough = at("hy_rough", H + 25 * KB, [T])
        hy_rot = at("hy_rot", H + 46 * KB, [5, T])
        hy_kswap = at("hy_kswap", H + 51 * KB, [T])
        hy_scores = at("hy_scores", H + 19 * KB, [8, 3 * P])
        hy_probs_t = at("hy_probs_t", H + 31 * KB, [4, 512])
        hy_conv_in = at("hy_conv_in", TR, [4, CONV_T])
        hy_conv = at("hy_conv", TR + 4128, [4, T])
        hy_att = at("hy_att", TR + 4128 + 4 * KB, [4, T])
        hy_sink = at("hy_sink", TR + 4128 + 8 * KB, [2, 8])
        rope_i = at("rope_i", TR + 14 * KB, [T], I32)
        rope_a = at("rope_a", TR + 15 * KB, [T])
        rope_n = at("rope_n", TR + 16 * KB, [T])
        rope_r = at("rope_r", TR + 17 * KB, [2, T])
        gla = at("gla", H, [24, T])
        gla_v = at("gla_v", H + 24 * KB, [TT, DM])
        gla_s = at("gla_s", H + 32 * KB, [3, 4, P])
        gla_g = at("gla_g", H + 38 * KB, [4, T])
        level_mask_f = at("level_mask_f", H + 38 * KB, [(len(LEVELS) + 1) * P])
        gla_e = at("gla_e", H + 42 * KB, [4, T])
        gla_w = [at("gla_w0", H + 46 * KB, [4, T]), at("gla_w1", TR + 8 * KB, [4, T])]
        gla_lr = at("gla_lr", H + 50 * KB, [T])
        gla_o = at("gla_o", TR, [8, T])
        gla_z = at("gla_z", TR + 12 * KB, [4, T])
        gla_wlr = at("gla_wlr", TR + 16 * KB, [KT, 16])
        gla_up = at("gla_up", TR + 17 * KB, [512])
        gla_wlr_hi = at("gla_wlr_hi", TR + 16 * KB + 512, [KT, 16], F32R)
        gla_wlr_lo = at("gla_wlr_lo", TR + 19 * KB, [KT, 16], F32R)

        G = [stack.enter_context(nc.psum_tensor(f"g{i}", [P, 512], F32)) for i in range(U)]
        D = [stack.enter_context(nc.psum_tensor(f"d{i}", [P, 512], F32)) for i in range(5)]
        STAT = 4
        bias_dram = nc.dram_tensor("bias_dram", (SKEW, ATT_HEADS * N_DIST), F32, kind="Internal").ap()

        def sem(name):
            return stack.enter_context(nc.semaphore(name))

        loaded = [sem(f"loaded{i}") for i in range(U)]
        hi_done, lo_dve, lo_pool = sem("hi_done"), sem("lo_dve"), sem("lo_pool")
        first_half_loaded, first_half_hi, first_half_lo = sem("first_half_loaded"), sem("first_half_hi"), sem("first_half_lo")
        chunk_done, evicted = sem("chunk_done"), sem("evicted")
        full_dve, full_act = sem("full_dve"), sem("full_act")
        drained_dve, drained_act = sem("drained_dve"), sem("drained_act")
        x_ready, x_gated = sem("x_ready"), sem("x_gated")
        x_hi_done, x_split = sem("x_hi_done"), sem("x_split")
        sq_done, sq_added, sq_total, sq_for_pe = sem("sq_done"), sem("sq_added"), sem("sq_total"), sem("sq_for_pe")
        mean_done, rough_done = sem("mean_done"), sem("rough_done")
        max_done, exp_done, probs_done = sem("max_done"), sem("exp_done"), sem("probs_done")
        mixed_ready = sem("mixed_ready")
        lam_dots_done, lam_exp_done = sem("lam_dots_done"), sem("lam_exp_done")
        gate_done, act_done, tap_done, conv_done = sem("gate_done"), sem("act_done"), sem("tap_done"), sem("conv_done")
        hid_done, hid_hi_done, hid_split = sem("hid_done"), sem("hid_hi_done"), sem("hid_split")
        p_hi_done, p_split = sem("p_hi_done"), sem("p_split")
        angles_done, rope_done, qk_gained, qk_rotated, sink_done = (
            sem(s) for s in ("angles_done", "rope_done", "qk_gained", "qk_rotated", "sink_done"))
        lr_hi_done, lr_split, o_squared = sem("lr_hi_done"), sem("lr_split"), sem("o_squared")
        lr_ready, logit_done, soft_done, decay_done, expo_done, level_ready, gla_scores_done, silu_done = (
            sem(s) for s in ("lr_ready", "logit_done", "soft_done", "decay_done", "expo_done", "level_ready",
                             "gla_scores_done", "silu_done"))
        got_x = [sem(f"got_x{i}") for i in range(KT // 2)]
        got_const, got_par, got_conv, got_mem, got_bias, got_small, got_rope, got_p, got_gla = (sem(s) for s in (
            "got_const", "got_par", "got_conv", "got_mem", "got_bias", "got_small", "got_rope", "got_p", "got_gla"))
        bias_stored, masked_row, out_stored = sem("bias_stored"), sem("masked_row"), sem("out_stored")
        cleared = sem("cleared")
        act_own, dve_own, pool_own = sem("act_own"), sem("dve_own"), sem("pool_own")

        def pcol(name, i=0):
            if not isinstance(name, str):
                return name[:, i:i + 1]
            c = PCOL[name] + i
            return par[:, c:c + 1]

        def reused(n):
            return not isinstance(n, int) or n >= U

        def over(ap, n):
            return ap.unsqueeze(1).broadcast_to([P, n, ap.shape[-1]])

        def along(ap, n):
            return ap.unsqueeze(2).broadcast_to([P, ap.shape[-1], n])

        def flat(ap):
            return ap.rearrange("p a t -> p (a t)")

        def tile_at(ap, j):
            return flat(ap)[:, bass.ds(j * T, T)]

        def as_tiles(ap, width=T):
            return ap.rearrange("p (f t) -> p f t", t=width)

        def pair_at(ap, j):
            return as_tiles(flat(ap)[:, bass.ds(j * 2 * T, 2 * T)])

        def right_halves(ap, n):
            return ap.rearrange("p (b x t) -> p b x t", x=2, t=n)[:, :, 1, :]

        def maps_of(b, t):
            return range(b % 2 + 4 * (b // 2), 4 * (b // 2) + (4 if t else 8), 2)

        restart = flat(gla_w[0])

        def head_squares(b):
            return sq[:, b, :] if b < 2 else flat(gla_w[1])[:, (b - 2) * 2 * T:(b - 1) * 2 * T]

        block = stack.enter_context(nc.Block())

        @block.sync
        def _(sp):
            count = Counts(sp)

            def load(c, slot):
                if reused(c):
                    sp.wait_ge(lo_dve, c - (U - 1))
                    sp.wait_ge(lo_pool, c - (U - 1))
                sp.dma_start(raw[:, slot, :], io["weights"][bass.ds(c, 1)].rearrange("o p c -> p (o c)")).then_inc(loaded[slot], 16)

            def stream(first, last):
                count.each(last - first, lambda i, im: load(i + first, (im + first) % U))

            sp.dma_start(par[:, 0:N_PARAM], io["par"][:, 0:N_PARAM]).then_inc(got_par, 16)
            for i in range(KT // 2):
                sp.dma_start(x[:, 2 * i:2 * i + 2, :], io["x_t"][:, 2 * i:2 * i + 2, :]).then_inc(got_x[i], 16)
                if i < 2:
                    half = slice(i * CHUNK // 2, (i + 1) * CHUNK // 2)
                    sp.dma_start(raw[:, 0, half], io["weights"][0][:, half]).then_inc((first_half_loaded, loaded[0])[i], 16)
            sp.dma_start(const[:], io["const"]).then_inc(got_const, 16)
            load(1, 1)
            load(2, 2)
            sp.dma_start(onehot[0:N_BUCKETS + 1, :], io["onehot"]).then_inc(got_small, 16)
            sp.dma_start(table[0:N_BUCKETS, :], io["rel_bias_table"]).then_inc(got_small, 16)
            lambdas = io["diff_lambda"].rearrange("l a b -> (l a b)").partition_broadcast(P)
            sp.dma_start(lam_in[:].rearrange("p a b -> p (a b)"), lambdas).then_inc(got_small, 16)
            sp.dma_start(sinks[:], io["hy_sinks_2"].rearrange("l h -> (l h)").partition_broadcast(P)).then_inc(got_small, 16)
            sp.dma_start(mem_t[:], io["mem_t"]).then_inc(got_mem, 16)
            for c in range(3, 6):
                load(c, c % U)
            sp.wait_ge(drained_act, 1)
            copies = bias_rows[0:ATT_HEADS, :].unsqueeze(1).broadcast_to([ATT_HEADS, SKEW, N_DIST])
            sp.dma_start(bias_dram.rearrange("s (h c) -> h s c", h=ATT_HEADS), copies).then_inc(bias_stored, 16)
            load(6, 6 % U)
            sp.wait_ge(bias_stored, 16)
            width = ATT_HEADS * N_DIST
            for a in range(0, P, SKEW):
                skewed = bass.AP(bias_dram.tensor, P - 1 - a, [[width - 1, SKEW], [N_DIST, ATT_HEADS], [1, 2 * P]])
                sp.dma_start(bias_tab[a:a + SKEW], skewed).then_inc(got_bias, 16)
            stream(7, FIRST["up0"] + U)
            sp.dma_start(par[:, CONV_COL:N_PCOLS], io["par"][:, CONV_COL:N_PCOLS]).then_inc(got_conv, 16)
            sp.dma_start(rope_i[:], io["positions_2"].rearrange("b s -> (b s)").partition_broadcast(P)).then_inc(got_rope, 16)
            stream(FIRST["up0"] + U, FIRST["down1"])
            sp.dma_start(p_in[:], io["p_t"][0]).then_inc(got_p, 16)
            stream(FIRST["down1"], FIRST["gla_in"])
            sp.dma_start(gla_wlr[:], io["gla_w_lr"]).then_inc(got_gla, 16)
            sp.dma_start(gla_up[0:16, :], io["gla_w_gate_up_2"][0]).then_inc(got_gla, 16)
            sp.dma_start(level_mask_f[:], io["level_mask"]).then_inc(got_gla, 16)
            stream(FIRST["gla_in"], FIRST["down2"])
            sp.dma_start(p_in[:], io["p_t"][1]).then_inc(got_p, 16)
            stream(FIRST["down2"], CHUNKS)
            for i in range(KT // 2):
                sp.wait_ge(x_gated, KT // 2 + i + 1)
                sp.dma_start(out[:, 2 * i:2 * i + 2, :], x[:, 2 * i:2 * i + 2, :]).then_inc(out_stored, 16)
            sp.wait_ge(out_stored, 16 * (KT // 2))

        @block.tensor
        def _(pe):
            count = Counts(pe)
            due = {}
            free_at = {}

            def acquire(b):
                if b in free_at:
                    pe.wait_ge(*free_at[b])

            def fill(b, last, full, drained):
                if last is not None:
                    last.then_inc(full, 1)
                due[drained] = due.get(drained, 0) + 1
                free_at[b] = (drained, due[drained])
                return free_at[b]

            def mm(out, lhsT, rhs, start=True, stop=True):
                return pe.matmul(out, lhsT, rhs, start=start, stop=stop, skip_group_check=True)

            def turn(out, src, n=P):
                return pe.transpose(out, src, ident[0:n, 0:n])

            def chunk(name, j, jm, moving, fresh=False):
                c, n = j + FIRST[name], j + FIRST_OUT[name]
                slot, bank = (FIRST[name] + jm) % U, G[(FIRST_OUT[name] + jm) % U]
                halves = isinstance(c, int) and c == 0
                if halves:
                    pe.wait_ge(first_half_lo, 1)
                else:
                    pe.wait_ge(lo_dve, c + 1)
                    pe.wait_ge(lo_pool, c + 1)
                if reused(n):
                    pe.wait_ge(evicted, n - (U - 1))
                for k in range(KT):
                    if halves and k == KT // 2:
                        pe.wait_ge(lo_dve, 1)
                        pe.wait_ge(lo_pool, 1)
                    if fresh:
                        pe.wait_ge(x_split, count.next(x_split))
                    for f in range(2):
                        cols = slice(k * 2 * P + f * P, k * 2 * P + (f + 1) * P)
                        to = bank[:, f * T:(f + 1) * T]
                        mm(to, w_hi[:, slot, cols], moving[0][:, k, :], k == 0 and f == 0, False)
                        mm(to, w_hi[:, slot, cols], moving[1][:, k, :], False, False)
                        last = mm(to, w_lo[:, slot, cols], moving[0][:, k, :], False, k == KT - 1)
                last.then_inc(chunk_done, 1)

            def chunk_tokens(name, j, jm, x_parts):
                c, n = j + FIRST[name], j + FIRST_OUT[name]
                slot, bank = (FIRST[name] + jm) % U, G[(FIRST_OUT[name] + jm) % U]
                pe.wait_ge(lo_dve, c + 1)
                pe.wait_ge(lo_pool, c + 1)
                pe.wait_ge(evicted, n - (U - 1))
                for k in range(KT):
                    for t in range(TT):
                        to, cols = bank[:, t * 2 * P:(t + 1) * 2 * P], slice(k * 2 * P, (k + 1) * 2 * P)
                        x_hi, x_lo = (part[:, k, t * P:(t + 1) * P] for part in x_parts)
                        mm(to, x_hi, w_hi[:, slot, cols], k == 0 and t == 0, False)
                        mm(to, x_hi, w_lo[:, slot, cols], False, False)
                        last = mm(to, x_lo, w_hi[:, slot, cols], False, k == KT - 1)
                last.then_inc(chunk_done, 1)

            def turn_scale(scale, evictions):
                pe.wait_ge(evicted, evictions)
                acquire(STAT)
                for t in range(TT):
                    last = turn(D[STAT][:, t * P:(t + 1) * P], scale[:, t * P:(t + 1) * P])
                fill(STAT, last, full_dve, drained_dve)

            def chunk_k(name, j, jm, moving, k0):
                c, slot = j + FIRST[name], (FIRST[name] + jm) % U
                first = isinstance(j, int) and j == 0
                final = isinstance(j, int) and j == COUNT[name] - 1
                pe.wait_ge(lo_dve, c + 1)
                pe.wait_ge(lo_pool, c + 1)
                order = [(h, f) for f in range(KT) for h in range(2)] if final else [(h, f) for h in range(2) for f in range(KT)]
                for h, f in order:
                    if first and h == 0 and f % 2 == 0:
                        acquire(f // 2)
                    to = D[f // 2][:, (f % 2) * T:(f % 2 + 1) * T]
                    cols = slice(h * DM + f * P, h * DM + (f + 1) * P)
                    m_hi, m_lo = (tile_at(m, k0 + h) for m in moving)
                    mm(to, w_hi[:, slot, cols], m_hi, first and h == 0 and f % 2 == 0, False)
                    mm(to, w_hi[:, slot, cols], m_lo, False, False)
                    last = mm(to, w_lo[:, slot, cols], m_hi, False, final and h == 1)
                    if final and h == 1 and f in (1, 3, 5) and name[:4] == "down":
                        fill(f // 2, last, full_dve, x_ready)
                last.then_inc(chunk_done, 1)
                if final and name[:4] == "down":
                    fill(3, None, None, x_ready)

            def norm_sum(sums=sq_sum):
                pe.wait_ge(sq_total, count.next(sq_total))
                acquire(STAT)
                mm(D[STAT][:, 0:T], ones, sums[:, 0:T], True, False)
                fill(STAT, mm(D[STAT][:, 0:T], ones, sums[:, T:2 * T], False, True), full_dve, mean_done)

            def outputs(name, moving):
                def body(j, jm):
                    fresh = isinstance(j, int) and j == 0
                    chunk(name, j, jm, moving, fresh)
                    if fresh:
                        norm_sum()
                count.each(COUNT[name], body)

            for j in range(W_IN_Q):
                if j < 4:
                    chunk("w_in", j, j % U, A, fresh=j == 0)
                else:
                    chunk_tokens("w_in", j, j % U, A)
                if j == 0:
                    pe.wait_ge(got_const, 16)
                    norm_sum()
                if j == 1:
                    pe.wait_ge(got_small, count.next(got_small, 16 * 4))
                    pe.wait_ge(masked_row, count.next(masked_row))
                    by_distance = mm(D[0][0:ATT_HEADS, 0:N_DIST], table[0:N_BUCKETS + 1, :], onehot[0:N_BUCKETS + 1, :])
                    fill(0, by_distance, full_act, drained_act)
                if j == 2:
                    turn_scale(rstd, 1)
                if j == 4:
                    norm_sum()

            def score_tiles(q, key, q0, t):
                keys = (t + 1) * P
                for b in range(4 if t else 2):
                    acquire(b)
                    for i, m in enumerate(maps_of(b, t)):
                        half = slice((m % 2) * 64, (m % 2) * 64 + 64)
                        last = mm(D[b][:, i * keys:(i + 1) * keys], q[half, q0 + m // 2, t * P:(t + 1) * P], key(m)[half, 0:keys])
                    fill(b, last, full_dve, drained_dve)

            def weigh_values(heads, values, place_of, per_bank, probs, probs_t):
                turned = {}
                for step in range(heads + 1):
                    if step < heads:
                        b = step % 2
                        acquire(b)
                        for i in range(3):
                            last = turn(D[b][:, i * P:(i + 1) * P], probs[:, step, i * P:(i + 1) * P])
                        turned[step] = fill(b, last, full_act, drained_act)
                    if step >= 1:
                        h = step - 1
                        b = 2 + h // per_bank
                        to = place_of(h)
                        pe.wait_ge(*turned[h])
                        if h % per_bank == 0:
                            acquire(b)
                        mm(to, values(0, h), probs_t[:, h % 4, 0:T], True, False)
                        last = mm(to[:, P:T], values(1, h), probs_t[:, h % 4, T:3 * P], False, True)
                        if h % per_bank == per_bank - 1:
                            fill(b, last, full_act, drained_act)

            def half_place(h):
                return D[2 + h // 4][(h % 2) * 64:(h % 2) * 64 + 64, (h // 2 % 2) * T:(h // 2 % 2 + 1) * T]

            def whole_place(h):
                return D[2 + h // 2][:, (h % 2) * T:(h % 2 + 1) * T]

            chunk("w_in", W_IN_Q, W_IN_Q % U, A)
            pe.wait_ge(evicted, W_IN_Q)
            score_tiles(qkv, lambda m: qkv[:, 4 + m // 2, :], 0, 1)
            score_tiles(qkv, lambda m: qkv[:, 4 + m // 2, :], 0, 0)
            turn_scale(rstd_mem, W_IN_Q + 1)
            for j in (7, 8):
                chunk("w_in", j, j % U, A)
            pe.wait_ge(probs_done, count.next(probs_done))
            weigh_values(8, lambda t, h: v_tok[:, t, h * 64:(h + 1) * 64], half_place, 4, scores, probs_t)
            chunk("w_in", 9, 0, A)
            pe.wait_ge(sq_for_pe, count.next(sq_for_pe, 2))
            acquire(STAT)
            for f in range(4):
                last = mm(D[STAT][:, 0:T], ones, sq[:, f // 2, (f % 2) * T:(f % 2 + 1) * T], f == 0, f == 3)
            fill(STAT, last, full_dve, mean_done)
            pe.wait_ge(evicted, 10)
            score_tiles(qkv, lambda m: qkv[:, 16 + m // 2, :], 12, 1)
            score_tiles(qkv, lambda m: qkv[:, 16 + m // 2, :], 12, 0)
            chunk_tokens("w_in", 10, 1, A)
            chunk_tokens("w_in", 11, 2, A)
            chunk("w_ck", 0, 0, B, fresh=True)
            pe.wait_ge(evicted, COUNT["w_in"])
            pe.wait_ge(probs_done, count.next(probs_done, 2))
            weigh_values(4, lambda t, h: v_tok[:, t, 512 + h * P:512 + (h + 1) * P], whole_place, 2, scores, probs_t)
            chunk("w_ck", 1, 1, B)
            for b in range(2):
                pe.wait_ge(sq_for_pe, count.next(sq_for_pe))
                acquire(b)
                for f in range(2):
                    last = mm(D[b][:, f * T:(f + 1) * T], ones, sq[:, b, f * T:(f + 1) * T])
                fill(b, last, full_dve, mean_done)
            chunk("w_ck", 2, 2, B)
            chunk("w_ck", 3, 0, B)
            for j in range(COUNT["w_out"]):
                chunk("w_out", j, j % U, A, fresh=j == 0)

            outputs("w_cq", C)
            pe.wait_ge(evicted, FIRST_OUT["w_cq"] + COUNT["w_cq"])
            for b in range(4):
                acquire(b)
                for i in range(2):
                    t, h = (2 * b + i) // 4, (2 * b + i) % 4
                    for d in range(2):
                        last = mm(D[b][:, i * T:(i + 1) * T], q_mem[:, 2 * h + d, t * P:(t + 1) * P], mem_k[:, 2 * h + d, :],
                                  d == 0, d == 1)
                fill(b, last, full_dve, drained_dve)
            for j in range(COUNT["w_cv"]):
                chunk_tokens("w_cv", j, j % U, B)
            pe.wait_ge(probs_done, count.next(probs_done))
            turned = {}
            for step in range(5):
                if step < 4:
                    acquire(step % 2)
                    for s in range(2):
                        for t in range(TT):
                            last = turn(D[step % 2][:, s * T + t * P:s * T + (t + 1) * P], scores_mem[:, t * 4 + step, s * P:(s + 1) * P])
                    turned[step] = fill(step % 2, last, full_act, drained_act)
                if step >= 1:
                    h = step - 1
                    b = 2 + h % 2
                    pe.wait_ge(*turned[h])
                    pe.wait_ge(evicted, FIRST_OUT["w_cv"] + h + 1)
                    acquire(b)
                    for d in range(2):
                        to, v = D[b][:, d * T:(d + 1) * T], slice((2 * h + d) * P, (2 * h + d + 1) * P)
                        mm(to, mem_v[:, 0, v], probs_t[:, h, 0:T], True, False)
                        last = mm(to, mem_v[:, 1, v], probs_t[:, h, T:2 * T], False, True)
                    last.then_inc(full_act, 1)
                    free_at[b] = (x_split, count.taken[x_split] + 2 * (h + 1))
            for j in range(COUNT["w_co"]):
                chunk("w_co", j, j % U, A, fresh=j == 0)

            def ffn(layer, moving):
                outputs(f"up{layer}", moving)

                def body(j, jm):
                    pe.wait_ge(hid_split, count.next(hid_split, 2))
                    chunk_k(f"down{layer}", j, jm, (hid_hi, hid_lo), j * 2)
                count.each(COUNT[f"down{layer}"], body)

            ffn(0, B)

            for j in range(4):
                chunk("hy_in", j, j % U, A, fresh=j == 0)
                if j < 2:
                    norm_sum((sq_sum, gain_sq_sum)[j])
            tiles_of = (2, 2, 1)
            for i in range(3):
                pe.wait_ge(sq_for_pe, count.next(sq_for_pe))
                acquire(i)
                for f in range(tiles_of[i]):
                    last = mm(D[i][:, f * T:(f + 1) * T], half_ones, hy_rot[:, 2 * i + f, :])
                fill(i, last, full_dve, mean_done)
            for i, b in enumerate((3, STAT, 0)):
                pe.wait_ge(qk_gained, count.next(qk_gained))
                acquire(b)
                for f in range(tiles_of[i]):
                    last = mm(D[b][:, f * T:(f + 1) * T], rot_half, hy_qk[:, 2 * i + f, :])
                fill(b, last, full_dve, drained_dve)
            acquire(1)
            for t in range(TT):
                last = turn(D[1][:, t * P:(t + 1) * P], hy[:, 5, t * P:(t + 1) * P])
            hy_v_turned = fill(1, last, full_act, drained_act)
            for j in (4, 5, 6):
                chunk("hy_in", j, j % U, A)
            pe.wait_ge(qk_rotated, count.next(qk_rotated))
            acquire(STAT)
            pe.wait_ge(*fill(STAT, mm(D[STAT][:, 0:T], swap_half, hy_qk[:, 4, :]), full_act, drained_act))

            def hy_key(m):
                return hy_qk[:, 4, :] if m % 2 == m // 4 else hy_kswap[:, :]

            pe.wait_ge(qk_rotated, count.next(qk_rotated, 2))
            score_tiles(hy_qk, hy_key, 0, 1)
            score_tiles(hy_qk, hy_key, 0, 0)
            for j in (7, 8):
                chunk("hy_in", j, j % U, A)
            pe.wait_ge(probs_done, count.next(probs_done))
            pe.wait_ge(*hy_v_turned)
            weigh_values(8, lambda t, h: hy_v[:, t, (h // 4) * 64:(h // 4 + 1) * 64], half_place, 4, hy_scores, hy_probs_t)
            for j in range(COUNT["hy_out"]):
                chunk("hy_out", j, j % U, B, fresh=j == 0)

            def embedding(layer, moving):
                pe.wait_ge(p_split, count.next(p_split))
                chunk_k(f"proj{layer}", 0, 0, (p_hi, p_lo), 0)
                for b in range(4):
                    fill(b, None, None, drained_dve)
                for j in range(COUNT[f"gate{layer}"]):
                    chunk(f"gate{layer}", j, j % U, moving, fresh=j == 0)
                    if j == 0:
                        norm_sum()

            ffn(1, A)
            embedding(1, B)

            def gla_chunk(j):
                if 4 <= j < 8:
                    chunk_tokens("gla_in", j, j % U, A)
                else:
                    chunk("gla_in", j, j % U, A, fresh=j == 0)

            gla_chunk(0)
            norm_sum()
            pe.wait_ge(lr_split, count.next(lr_split))
            acquire(0)
            for k in range(KT):
                mm(D[0][0:16, 0:T], gla_wlr_hi[:, k, :], A[0][:, k, :], k == 0, False)
                mm(D[0][0:16, 0:T], gla_wlr_hi[:, k, :], A[1][:, k, :], False, False)
                last = mm(D[0][0:16, 0:T], gla_wlr_lo[:, k, :], A[0][:, k, :], False, k == KT - 1)
            fill(0, last, full_dve, lr_ready)
            gla_chunk(1)
            pe.wait_ge(lr_ready, count.next(lr_ready))
            for b in (1, 2):
                acquire(b)
                for f in range(2):
                    h = 2 * (b - 1) + f
                    last = mm(D[b][:, f * T:(f + 1) * T], gla_up[0:16, h * P:(h + 1) * P], gla_lr[0:16, :])
                fill(b, last, full_dve, drained_dve)
            gla_chunk(2)
            turn_scale(rstd, FIRST_OUT["gla_in"] + 1)
            gla_chunk(3)

            def gla_level(i):
                if i == 0:
                    pe.wait_ge(evicted, FIRST_OUT["gla_in"] + 4)
                else:
                    pe.wait_ge(level_ready, count.next(level_ready))
                for t in range(TT):
                    b = (2 * i + t) % 4
                    cols = slice(t * P, (t + 1) * P)
                    acquire(b)
                    for h in range(4):
                        if i == 0:
                            last = mm(D[b][:, h * P:(h + 1) * P], gla[:, 4 + h, cols], gla[:, h, cols])
                        else:
                            k = gla_w[i % 2][:, h, cols]
                            last = mm(D[b][:, h * P // 2:(h + 1) * P // 2], k, right_halves(k, LEVELS[i - 1]))
                    fill(b, last, full_dve, drained_dve)

            gla_chunk(4)
            gla_level(0)
            gla_chunk(5)
            for i in range(1, len(LEVELS) + 1):
                gla_level(i)
                if i % 2:
                    gla_chunk(6 + i // 2)
            pe.wait_ge(level_ready, count.next(level_ready))
            acquire(0)
            for h in range(4):
                last = mm(D[0][:, h * P:(h + 1) * P], gla_w[0][:, h, 0:P], gla_w[0][:, h, P:2 * P])
            fill(0, last, full_dve, gla_scores_done)
            pe.wait_ge(evicted, FIRST_OUT["gla_in"] + 8)
            pe.wait_ge(gla_scores_done, count.next(gla_scores_done))
            for b in range(4):
                acquire(b)
                for f in range(2):
                    v = slice((2 * b + f) * P, (2 * b + f + 1) * P)
                    to = D[b][:, f * T:(f + 1) * T]
                    mm(to[:, 0:P], gla_v[:, 0, v], gla_s[:, 0, b, :], f == 0, True)
                    mm(to[:, P:T], gla_v[:, 0, v], gla_s[:, 2, b, :], False, False)
                    last = mm(to[:, P:T], gla_v[:, 1, v], gla_s[:, 1, b, :], False, True)
                fill(b, last, full_act, drained_act)
            for pair in range(2):
                acquire(pair)
                for i in range(2):
                    pe.wait_ge(o_squared, count.next(o_squared))
                    for f in range(2):
                        last = mm(D[pair][:, i * T:(i + 1) * T], ones, head_squares(2 * pair + i)[:, f * T:(f + 1) * T],
                                  f == 0 and i == 0, f == 1)
                fill(pair, last, full_dve, mean_done)
            gla_chunk(10)
            gla_chunk(11)
            for j in range(COUNT["gla_out"]):
                chunk("gla_out", j, j % U, B, fresh=j == 0)

            ffn(2, A)
            embedding(2, B)

        @block.scalar
        def _(act):
            count = Counts(act)
            count.per_turn = {s: 16 for s in loaded}

            def fn(out, in_, func=ACT.Copy, **kw):
                return act.activation(out, in_, func, **kw)

            def split_hi(c, slot):
                if isinstance(c, int) and c >= CHUNKS:
                    return
                act.wait_ge(loaded[slot], count.next(loaded[slot], 16))
                if reused(c):
                    act.wait_ge(chunk_done, c - (U - 1))
                fn(w_hi[:, slot, :], raw[:, slot, :]).then_inc(hi_done, 1)

            def ahead(name, j, jm):
                split_hi(j + (FIRST[name] + AHEAD), (FIRST[name] + jm + AHEAD) % U)

            def out_count(name, j):
                return j + (FIRST_OUT[name] + 1)

            def loop(n, body, peel=3, function=ACT.Copy):
                count.each(n, body, peel, lambda: act.preload_act_table(function))

            def hi_parts(moving, first, src, gains=None):
                for f in range(len(src)):
                    scale = {} if gains is None else {"scale": gains[f]}
                    fn(moving[0][:, first + f, :], src[f], **scale).then_inc(x_hi_done, 1)

            def prep_pair(moving, gain, g0, src, i):
                hi_parts(moving, 2 * i, [src[:, 2 * i + f, :] for f in range(2)], [pcol(gain, g0 + 2 * i + f) for f in range(2)])
                squares(i, src)

            def squares(i, src, sums=sq_sum, ring=sq, gain=None):
                if i == 3:
                    act.wait_ge(sq_added, count.next(sq_added, 2) - 1)
                to = sums[:] if i == 0 else ring[:, i % 2, :]
                if gain is None:
                    last = fn(to, flat(src[:, 2 * i:2 * i + 2, :]), ACT.Square)
                else:
                    for f in range(2):
                        last = fn(to[:, f * T:(f + 1) * T], src[:, 2 * i + f, :], ACT.Square, scale=pcol(gain, 2 * i + f))
                last.then_inc(sq_done, 1)

            def prep(ready, moving, gain, g0=0):
                for i in range(KT // 2):
                    act.wait_ge(ready, count.next(ready))
                    prep_pair(moving, gain, g0, x, i)

            def rough_rstd(width=T, m=mean_sq, r=rough, preload=True):
                if preload:
                    act.preload_act_table(ACT.Abs_reciprocal_sqrt)
                act.wait_ge(mean_done, count.next(mean_done))
                fn(r[:, 0:width], m[:, 0:width], ACT.Abs_reciprocal_sqrt).then_inc(rough_done, 1)

            def exps(s, t, maps, cols):
                act.wait_ge(max_done, count.next(max_done))
                for m in range(maps):
                    last = fn(s[:, m, cols], s[:, m, cols], ACT.Exp, bias=neg_max[:, t, m:m + 1], accum_out=row_sum[:, t, m:m + 1])
                last.then_inc(exp_done, 1)

            def from_bank(out, in_):
                act.wait_ge(full_act, count.next(full_act))
                fn(out, in_).then_inc(drained_act, count.one(drained_act))

            def weigh_values(heads, per_bank, probs_t, att, after):
                for step in range(heads + 1):
                    if step < heads:
                        from_bank(probs_t[:, step % 4, 0:3 * P], D[step % 2][:, 0:3 * P])
                    if step >= 1 and (step - 1) % per_bank == per_bank - 1:
                        i = (step - 1) // per_bank
                        from_bank(flat(att[:, 2 * i:2 * i + 2, :]), D[2 + i][:])
                        act.wait_ge(drained_act, count.sent[drained_act])
                        after(i)

            def square_of(att):
                def after(i):
                    fn(sq[:, i, :], flat(att[:, 2 * i:2 * i + 2, :]), ACT.Square).then_inc(sq_for_pe, 1)
                return after

            def residual(name, moving, gain, g0=0):
                for j in range(COUNT[name]):
                    ahead(name, j, j % U)
                    act.wait_ge(evicted, out_count(name, j))
                    prep_pair(moving, gain, g0, x, j)

            act.wait_ge(got_par, 16)
            for i in range(KT // 2):
                act.wait_ge(got_x[i], 16)
                hi_parts(A, 2 * i, [x[:, 2 * i + f, :] for f in range(2)], [pcol("mix_norm_g", 2 * i + f) for f in range(2)])
                if i == 0:
                    act.wait_ge(first_half_loaded, 16)
                    fn(w_hi[:, 0, 0:CHUNK // 2], raw[:, 0, 0:CHUNK // 2]).then_inc(first_half_hi, 1)
                if i == 1:
                    act.wait_ge(loaded[0], count.next(loaded[0], 16))
                    fn(w_hi[:, 0, CHUNK // 2:CHUNK], raw[:, 0, CHUNK // 2:CHUNK]).then_inc(hi_done, 1)
                squares(i, x)
            split_hi(1, 1)

            for j in range(W_IN_Q):
                ahead("w_in", j, j % U)
                if j == 0:
                    rough_rstd()
                if j == 1:
                    from_bank(bias_rows[0:ATT_HEADS, :], D[0][0:ATT_HEADS, 0:N_DIST])
                    act.wait_ge(lam_dots_done, count.next(lam_dots_done))
                    fn(lam_exp[:], lam_dot[:], ACT.Exp).then_inc(lam_exp_done, 1)
                if j == 3:
                    act.wait_ge(got_mem, 16)
                    for i in range(KT // 2):
                        prep_pair(B, "mem_norm_g", 0, mem_t, i)
                if j == 4:
                    rough_rstd()


            ahead("w_in", W_IN_Q, W_IN_Q % U)
            exps(scores, 1, 8, slice(P, 3 * P))
            exps(scores, 0, 8, slice(0, P))
            ahead("w_in", 7, 1)
            weigh_values(8, 4, probs_t, att_a, square_of(att_a))
            ahead("w_in", 8, 2)
            ahead("w_in", 9, 0)
            rough_rstd()
            exps(scores, 1, 8, slice(P, 3 * P))
            ahead("w_in", 10, 1)
            exps(scores, 0, 8, slice(0, P))
            ahead("w_in", 11, 2)
            weigh_values(4, 2, probs_t, att_b, square_of(att_b))
            ahead("w_ck", 0, 0)
            act.wait_ge(chunk_done, COUNT["w_in"])
            act.wait_ge(mixed_ready, count.next(mixed_ready))
            hi_parts(A, 0, [att_a[:, f, :] for f in range(4)], [pcol("moba_out_g", f) for f in range(4)])
            ahead("w_ck", 1, 1)
            rough_rstd(2 * T)
            rough_rstd(2 * T, sq[:, 0, :], sq[:, 1, :], preload=False)
            ahead("w_ck", 2, 2)
            for b in range(2):
                act.wait_ge(mixed_ready, count.next(mixed_ready))
                hi_parts(A, 4 + 2 * b, [att_b[:, 2 * b + f, :] for f in range(2)], [subln_g[:, 0:1]] * 2)
            ahead("w_ck", 3, 0)
            residual("w_out", C, "cross_norm_g")

            for j in range(COUNT["w_cq"]):
                ahead("w_cq", j, j % U)
                if j == 0:
                    rough_rstd()
            exps(scores_mem, 0, 8, slice(0, T))
            for j in range(COUNT["w_cv"]):
                ahead("w_cv", j, j % U)
            for step in range(5):
                if step < 4:
                    from_bank(probs_t[:, step, :], D[step % 2][:])
                if step >= 1:
                    h = step - 1
                    act.wait_ge(full_act, count.next(full_act))
                    hi_parts(A, 2 * h, [D[2 + h % 2][:, d * T:(d + 1) * T] for d in range(2)])
            residual("w_co", B, "ffn_norm_g")

            def hidden_hi(j, jm, ring):
                act.wait_ge(hid_done, count.next(hid_done))
                fn(tile_at(hid_hi, j), ring[:, jm % U, :]).then_inc(hid_hi_done, 1)

            def down(layer, first=0):
                name = f"down{layer}"
                loop(COUNT[name] - first, lambda j, jm: ahead(name, j + first, jm + first))

            def gated_body(j, jm):
                ahead("up0", j, jm)
                if isinstance(j, int) and j == 0:
                    rough_rstd()
                act.wait_ge(gate_done, count.next(gate_done))
                fn(gate_act[:, jm, :], gate_z[:, jm, :], ACT.Silu).then_inc(act_done, 1)
                if not isinstance(j, int) or j >= 1:
                    hidden_hi(j - 1, jm + 2, hid)

            loop(FT, gated_body, 3, ACT.Silu)
            hidden_hi(FT - 1, (FT - 1) % U, hid)
            down(0)
            act.wait_ge(angles_done, 1)
            prep(x_ready, A, both_g)
            for i in range(KT // 2):
                squares(i, x, gain_sq_sum, gain_sq, "final_norm_g")

            def hy_ahead(j):
                ahead("hy_in", j, j % U)

            hy_ahead(0)
            rough_rstd()
            hy_ahead(1)
            rough_rstd()
            fn(sin_t[:], rope_r[:, 0, :], ACT.Sin)
            fn(cos_t[:], rope_r[:, 1, :], ACT.Sin).then_inc(rope_done, 1)
            hy_ahead(2)
            for i in range(3):
                act.wait_ge(evicted, out_count("hy_in", i))
                tiles = slice(2 * i, min(2 * i + 2, 5))
                fn(flat(hy_rot[:, tiles, :]), flat(hy[:, tiles, :]), ACT.Square).then_inc(sq_for_pe, 1)
            hy_ahead(3)
            for i, (m, rr) in enumerate(((mean_sq, rough), (sq[:, 0, :], sq[:, 1, :]), (hy_mean, hy_rough))):
                rough_rstd((2, 2, 1)[i] * T, m, rr, preload=i == 0)
            from_bank(flat(hy_v), D[1][:, 0:T])
            for j in (4, 5, 6):
                hy_ahead(j)
            from_bank(hy_kswap[:], D[STAT][:, 0:T])
            for t, cols in ((1, slice(P, 3 * P)), (0, slice(0, P))):
                act.wait_ge(max_done, count.next(max_done))
                fn(hy_sink[:, t, :], hy_sink[:, t, :], ACT.Exp).then_inc(sink_done, 1)
                for m in range(8):
                    last = fn(hy_scores[:, m, cols], hy_scores[:, m, cols], ACT.Exp, bias=neg_max[:, t, m:m + 1],
                              accum_out=row_sum[:, t, m:m + 1])
                last.then_inc(exp_done, 1)
            hy_ahead(7)
            weigh_values(8, 4, hy_probs_t, hy_att, lambda i: hi_parts(B, 2 * i, [hy_att[:, 2 * i + f, :] for f in range(2)]))
            for i in range(2):
                act.wait_ge(mixed_ready, count.next(mixed_ready))
                hi_parts(B, 4 + 2 * i, [hy_conv[:, 2 * i + f, :] for f in range(2)])
            hy_ahead(8)
            residual("hy_out", A, "ffn_norm_2")

            def conv_ffn(layer, moving, ple_moving):
                name = f"up{layer}"

                def column(base, tap, f, j):
                    return par[:, bass.ds(j + (base + ((layer - 1) * tap[1] + tap[0]) * 2 * FT + f * FT), 1)]

                def gelu(j, jm):
                    act.wait_ge(conv_done, count.next(conv_done))
                    fn(conv_gelu[:, jm % U, :], conv_out[:, jm % U, 0, :], ACT.Gelu).then_inc(act_done, 1)

                def body(j, jm):
                    early = isinstance(j, int)
                    ahead(name, j, jm)
                    if early and j == 0:
                        rough_rstd()
                    act.wait_ge(evicted, out_count(name, j))
                    for f in range(2):
                        last = fn(conv_out[:, jm, f, :], conv_in[:, jm, f, 2:2 + T], ACT.Identity,
                                  scale=column(CONV_COL, (2, 3), f, j), bias=column(CONVB_COL, (0, 1), f, j))
                    last.then_inc(tap_done, 1)
                    if not early or j >= 2:
                        hidden_hi(j - 2, jm + 1, conv_hid)
                    if not early or j >= 1:
                        gelu(j - 1, jm + 2)

                act.wait_ge(got_conv, 16)
                loop(FT, body, 4, ACT.Gelu)
                hidden_hi(FT - 2, (FT - 2) % U, conv_hid)
                ahead(f"down{layer}", 0, 0)
                gelu(FT - 1, (FT - 1) % U)
                hidden_hi(FT - 1, (FT - 1) % U, conv_hid)
                act.wait_ge(got_p, count.next(got_p, 16))
                fn(flat(p_hi), flat(p_in)).then_inc(p_hi_done, 1)
                down(layer, 1)
                prep(x_ready, ple_moving, "ple_norm_2", (layer - 1) * KT)
                ahead(f"proj{layer}", 0, 0)
                for j in range(COUNT[f"gate{layer}"]):
                    if j == 0:
                        ahead(f"gate{layer}", 0, 0)
                        rough_rstd()
                    act.wait_ge(evicted, out_count(f"gate{layer}", j))
                    fn(flat(ple_sig[:, j % 2, :, :]), flat(ple_z[:, j % 2, :, :]), ACT.Sigmoid).then_inc(act_done, 1)
                    if 0 < j < 3:
                        ahead(f"gate{layer}", j, j % U)
                    if layer == 1:
                        act.wait_ge(x_gated, count.next(x_gated))
                        prep_pair(A, "mix_norm_2", KT, x, j)
                ahead(f"gate{layer}", 3, 0)

            conv_ffn(1, A, B)

            def gla_ahead(j):
                ahead("gla_in", j, j % U)

            def decays(i):
                act.wait_ge(decay_done, count.next(decay_done))
                e = flat((gla_e, gla_z)[i % 2])
                fn(e, e, ACT.Exp, scale=1.0 / 16.0).then_inc(expo_done, 1)

            act.wait_ge(got_gla, count.next(got_gla, 16 * 3))
            fn(flat(gla_wlr_hi), flat(gla_wlr)).then_inc(lr_hi_done, 1)
            gla_ahead(0)
            rough_rstd()
            gla_ahead(1)
            gla_ahead(2)
            act.wait_ge(logit_done, count.next(logit_done))
            fn(flat(gla_e), flat(gla_e), ACT.Exp).then_inc(act_own, count.one(act_own))
            act.wait_ge(act_own, count.sent[act_own])
            fn(flat(gla_e), flat(gla_e), ACT.Ln, bias=ones[:, 0:1]).then_inc(soft_done, 1)
            decays(1)
            gla_ahead(3)

            def open_gate(i):
                act.wait_ge(evicted, out_count("gla_in", i))
                og = flat(gla[:, 2 * i:2 * i + 2, :])
                return fn(og, og, ACT.Silu)

            for i in range(1, len(LEVELS) + 1):
                decays(i + 1)
                for j in {1: (4,), 2: (5, 6), 3: (7,), 5: (8,), 7: (9,)}.get(i, ()):
                    gla_ahead(j)
            open_gate(8)
            open_gate(9).then_inc(silu_done, 1)
            for b in range(4):
                from_bank(flat(gla_o[:, 2 * b:2 * b + 2, :]), D[b][:])
                act.wait_ge(drained_act, count.sent[drained_act])
                fn(head_squares(b), flat(gla_o[:, 2 * b:2 * b + 2, :]), ACT.Square).then_inc(o_squared, 1)
            rough_rstd(2 * T)
            rough_rstd(2 * T, sq[:, 0, :], sq[:, 1, :], preload=False)
            gla_ahead(10)
            gains = [pcol("gla_o_norm_2", f) for f in range(2)]
            for h in range(4):
                if h >= 2:
                    open_gate(8 + h).then_inc(silu_done, 1)
                act.wait_ge(mixed_ready, count.next(mixed_ready))
                hi_parts(B, 2 * h, [gla_o[:, 2 * h + f, :] for f in range(2)], gains)
                if h == 1:
                    gla_ahead(11)
            residual("gla_out", A, "ffn_norm_2", KT)
            conv_ffn(2, A, B)

        @block.vector
        def _(dve):
            count = Counts(dve)

            def mul(out, a, b):
                return dve.tensor_tensor(out, a, b, ALU.mult)

            def add(out, a, b):
                return dve.tensor_tensor(out, a, b, ALU.add)

            def sub(out, a, b):
                return dve.tensor_tensor(out, a, b, ALU.subtract)

            def fused(out, a, scalar, b, op0, op1):
                return dve.scalar_tensor_tensor(out, a, scalar, b, op0, op1)

            def split_lo(c, slot, first=0):
                if isinstance(c, int) and c >= CHUNKS:
                    return
                dve.wait_ge(hi_done, c + 1)
                cols = slice(first, DVE_COLS)
                sub(w_lo[:, slot, cols], raw[:, slot, cols], w_hi[:, slot, cols].bitcast(F32)).then_inc(lo_dve, 1)

            def ahead(name, j, jm):
                split_lo(j + (FIRST[name] + AHEAD), (FIRST[name] + jm + AHEAD) % U)

            def bank_of(name, j, jm):
                dve.wait_ge(chunk_done, j + (FIRST[name] + 1))
                return as_tiles(G[(FIRST_OUT[name] + jm) % U][:])

            def lo_parts(moving, first, src, gains=None):
                for f in range(len(src)):
                    dve.wait_ge(x_hi_done, count.next(x_hi_done))
                    hi, lo = moving[0][:, first + f, :].bitcast(F32), moving[1][:, first + f, :]
                    if gains is None:
                        sub(lo, src[f], hi).then_inc(x_split, 1)
                    else:
                        fused(lo, src[f], gains[f], hi, ALU.mult, ALU.subtract).then_inc(x_split, 1)

            def prep_pair(moving, gain, g0, src, i):
                lo_parts(moving, 2 * i, [src[:, 2 * i + f, :] for f in range(2)], [pcol(gain, g0 + 2 * i + f) for f in range(2)])

            def prep(moving, gain, g0=0, src=x):
                for i in range(KT // 2):
                    prep_pair(moving, gain, g0, src, i)

            def mean(bank, features, width=T, m=mean_sq):
                dve.wait_ge(full_dve, count.next(full_dve))
                dve.tensor_scalar(m[:, 0:width], D[bank][:, 0:width], 1.0 / features, EPS, ALU.mult, ALU.add).then_inc(mean_done, count.one(mean_done))

            def refine(to, width=T, m=mean_sq, r=rough):
                dve.wait_ge(rough_done, count.next(rough_done))
                m, r, n = m[:, 0:width], r[:, 0:width], newton[:, 0:width]
                dve.wait_ge(mean_done, count.sent[mean_done])
                fused(n, m, -0.5, r, ALU.mult, ALU.mult).then_inc(dve_own, count.one(dve_own))
                dve.wait_ge(dve_own, count.sent[dve_own])
                mul(n, n, r).then_inc(dve_own, count.one(dve_own))
                dve.wait_ge(dve_own, count.sent[dve_own])
                fused(to[:, 0:width], n, 1.5, r, ALU.add, ALU.mult).then_inc(dve_own, count.one(dve_own))
                dve.wait_ge(dve_own, count.sent[dve_own])

            def token_norm(to=rstd):
                mean(STAT, DM)
                refine(to)

            def evict(name, j, jm, to, scale=rstd, split=True):
                mul(to, bank_of(name, j, jm), over(scale[:], 2)).then_inc(evicted, count.one(evicted))
                if split:
                    ahead(name, j, jm)

            def negate_max(s, t, cols, maps=8):
                dve.tensor_reduce(row_max[:, t, 0:maps], s[:, :, cols], AX_X, ALU.max).then_inc(dve_own, count.one(dve_own))
                dve.wait_ge(dve_own, count.sent[dve_own])
                dve.tensor_scalar(neg_max[:, t, 0:maps], row_max[:, t, 0:maps], -1.0, None, ALU.mult).then_inc(max_done, 1)

            def normalise(s, t, cols, width):
                return mul(s[:, :, cols], s[:, :, cols], along(row_rec[:, t, :], width))

            def residual(name, moving, gain, g0=0):
                for j in range(COUNT[name]):
                    pair = x[:, 2 * j:2 * j + 2, :]
                    add(pair, pair, bank_of(name, j, j % U)).then_inc(evicted, count.one(evicted))
                    ahead(name, j, j % U)
                    dve.wait_ge(evicted, count.sent[evicted])
                    prep_pair(moving, gain, g0, x, j)

            TILE0, TILE1 = slice(0, P), slice(P, 3 * P)

            dve.wait_ge(got_par, 16)
            for i in range(KT // 2):
                dve.wait_ge(got_x[i], 16)
                prep_pair(A, "mix_norm_g", 0, x, i)
                if i == 0:
                    dve.wait_ge(first_half_hi, 1)
                    half = slice(0, CHUNK // 2)
                    sub(w_lo[:, 0, half], raw[:, 0, half], w_hi[:, 0, half].bitcast(F32)).then_inc(first_half_lo, 1)
                if i == 1:
                    split_lo(0, 0, CHUNK // 2)
            split_lo(1, 1)

            def evict_tokens(name, j, to, scale, split=True):
                mul(to, bank_of(name, j, j % U), along(scale[:], 2 * P)).then_inc(evicted, count.one(evicted))
                if split:
                    ahead(name, j, j % U)

            def turned_scale(to):
                dve.wait_ge(full_dve, count.next(full_dve))
                dve.tensor_copy(to[:], D[STAT][:, 0:T:P]).then_inc(drained_dve, count.one(drained_dve))
                dve.wait_ge(drained_dve, count.sent[drained_dve])

            def first_chunk(j):
                if j == 0:
                    token_norm()
                if j in (4, 5):
                    evict_tokens("w_in", j, v_tok[:, :, (j - 4) * 2 * P:(j - 3) * 2 * P], rstd_tok)
                else:
                    evict("w_in", j, j % U, pair_at(qkv, j))

            for j in range(W_IN_Q):
                first_chunk(j)
                if j == 1:
                    dve.wait_ge(got_small, count.next(got_small, 16 * 4))
                    mul(lam_mul[:], lam_in[:, 0::2, :], lam_in[:, 1::2, :]).then_inc(dve_own, count.one(dve_own))
                    dve.wait_ge(dve_own, count.sent[dve_own])
                    dve.tensor_reduce(lam_dot[:], lam_mul[:], AX_X, ALU.add).then_inc(lam_dots_done, 1)
                    dve.tensor_scalar(subln_g[:], pcol("diff_subln_g"), 1.0 - LAMBDA_INIT, None, ALU.mult).then_inc(dve_own, count.one(dve_own))
                if j == 2:
                    dve.wait_ge(lam_exp_done, count.next(lam_exp_done))
                    fused(neg_lam[:], lam_exp[:, 1:2], LAMBDA_INIT, lam_exp[:, 0:1], ALU.subtract, ALU.subtract).then_inc(dve_own, count.one(dve_own))
                if j == 2:
                    turned_scale(rstd_tok)
                if j == 3:
                    dve.wait_ge(got_mem, 16)
                    dve.wait_ge(bias_stored, 16)
                if j == 4:
                    prep(B, "mem_norm_g", src=mem_t)
                    token_norm(rstd_mem)

            def score_tiles(s, bias):
                for t, cols in ((1, TILE1), (0, TILE0)):
                    for b in range(4 if t else 2):
                        maps = maps_of(b, t)
                        dve.wait_ge(full_dve, count.next(full_dve))
                        fused(s[:, maps.start:maps.stop:2, cols], as_tiles(D[b][:], (t + 1) * P), QK_SCALE,
                                        bias(maps, slice(0 if t else P, 2 * P)), ALU.mult, ALU.add).then_inc(drained_dve, count.one(drained_dve))
                    dve.wait_ge(drained_dve, count.sent[drained_dve])
                    yield t, cols

            def mem_keys(j):
                evict("w_ck", j, j % U, pair_at(mem_k, j), rstd_mem)

            def mem_values(j):
                evict_tokens("w_cv", j, mem_v[:, :, j * 2 * P:(j + 1) * 2 * P], rstd_mem_tok)

            def reciprocals(t):
                dve.wait_ge(exp_done, count.next(exp_done))
                dve.reciprocal(row_rec[:, t, :], row_sum[:, t, :]).then_inc(dve_own, count.one(dve_own))
                dve.wait_ge(dve_own, count.sent[dve_own])

            first_chunk(W_IN_Q)
            dve.wait_ge(got_bias, 16 * P // SKEW)
            for t, cols in score_tiles(scores, lambda maps, c: bias_tab[:, maps.start:maps.stop:2, c]):
                negate_max(scores, t, cols)
            turned_scale(rstd_mem_tok)
            reciprocals(1)
            normalise(scores, 1, TILE1, 2 * P).then_inc(dve_own, count.one(dve_own))
            reciprocals(0)
            normalise(scores, 0, TILE0, P).then_inc(probs_done, 1)
            for j in (7, 8, 9):
                first_chunk(j)
            mean(STAT, 4 * P)
            for t, cols in score_tiles(scores, lambda maps, c: bias_tab[:, 8 + maps.start // 2:8 + maps.stop // 2, c]):
                negate_max(scores, t, cols)
            evict_tokens("w_in", 10, v_tok[:, :, 4 * P:6 * P], rstd_tok, split=False)
            for t, cols, width in ((1, TILE1, 2 * P), (0, TILE0, P)):
                reciprocals(t)
                second = row_rec[:, t, 1::2]
                dve.tensor_scalar(second, second, neg_lam[:, 0:1], None, ALU.mult).then_inc(dve_own, count.one(dve_own))
                dve.wait_ge(dve_own, count.sent[dve_own])
                normalise(scores, t, cols, width).then_inc(dve_own, count.one(dve_own))
                dve.wait_ge(dve_own, count.sent[dve_own])
                add(scores[:, 0:4, cols], scores[:, 0::2, cols], scores[:, 1::2, cols]).then_inc(probs_done, 1)
                if t == 1:
                    ahead("w_in", 10, 1)
            evict_tokens("w_in", 11, v_tok[:, :, 6 * P:8 * P], rstd_tok)
            refine(mean_sq)
            mul(att_a[:], att_a[:], over(mean_sq[:, 0:T], 4)).then_inc(mixed_ready, count.one(mixed_ready))
            mem_keys(0)
            lo_parts(A, 0, [att_a[:, f, :] for f in range(4)], [pcol("moba_out_g", f) for f in range(4)])
            mem_keys(1)
            mean(0, P, 2 * T)
            mean(1, P, 2 * T, sq[:, 0, :])
            for b, (m, r) in enumerate(((mean_sq, rough), (sq[:, 0, :], sq[:, 1, :]))):
                refine(m, 2 * T, m, r)
                tiles = att_b[:, 2 * b:2 * b + 2, :]
                mul(tiles, tiles, as_tiles(m[:, 0:2 * T])).then_inc(mixed_ready, count.one(mixed_ready))
            mem_keys(2)
            dve.wait_ge(mixed_ready, count.sent[mixed_ready])
            lo_parts(A, 4, [att_b[:, f, :] for f in range(4)], [subln_g[:, 0:1]] * 4)
            mem_keys(3)
            residual("w_out", C, "cross_norm_g")

            for j in range(COUNT["w_cq"]):
                if j == 0:
                    token_norm()
                evict("w_cq", j, j % U, pair_at(q_mem, j))
            for b in range(4):
                dve.wait_ge(full_dve, count.next(full_dve))
                dve.tensor_scalar(scores_mem[:, 2 * b:2 * b + 2, :], as_tiles(D[b][:]), 0.0625, None, ALU.mult).then_inc(drained_dve, count.one(drained_dve))
            dve.wait_ge(drained_dve, count.sent[drained_dve])
            negate_max(scores_mem, 0, slice(0, T))
            mem_values(0)
            dve.wait_ge(exp_done, count.next(exp_done))
            dve.reciprocal(row_rec[:, 0, :], row_sum[:, 0, :]).then_inc(dve_own, count.one(dve_own))
            dve.wait_ge(dve_own, count.sent[dve_own])
            normalise(scores_mem, 0, slice(0, T), T).then_inc(probs_done, 1)
            for j in (1, 2, 3):
                mem_values(j)
            for h in range(4):
                dve.wait_ge(x_hi_done, count.taken[x_hi_done] + 2)
                lo_parts(A, 2 * h, [D[2 + h % 2][:, d * T:(d + 1) * T] for d in range(2)])
            residual("w_co", B, "ffn_norm_g")

            def hidden_lo(j, jm, ring):
                dve.wait_ge(hid_hi_done, count.next(hid_hi_done))
                dve.wait_ge(hid_done, count.sent[hid_done])
                sub(tile_at(hid_lo, j), ring[:, jm % U, :], tile_at(hid_hi, j).bitcast(F32)).then_inc(hid_split, 1)

            def down(layer, between=None, first=0):
                name = f"down{layer}"

                def body(j, jm):
                    ahead(name, j + first, jm + first)
                    if between and isinstance(j, int) and j < 2:
                        between(j)
                count.each(COUNT[name] - first - 1, body)
                for b in range(4):
                    if b < 3:
                        dve.wait_ge(full_dve, count.next(full_dve))
                    else:
                        dve.wait_ge(chunk_done, FIRST[name] + COUNT[name])
                    pair = x[:, 2 * b:2 * b + 2, :]
                    add(pair, pair, as_tiles(D[b][:])).then_inc(x_ready, count.one(x_ready))
                dve.wait_ge(x_ready, count.sent[x_ready])

            def rope_angles(i):
                two_pi, magic = 2.0 * math.pi, 1.5 * 2.0 ** 23
                c1 = 6.28125
                c2 = float(np.round((two_pi - c1) * 2.0 ** 21) * 2.0 ** -21)
                c3 = two_pi - c1 - c2
                shift, r = (0.0, 0.5 * math.pi)[i], rope_r[:, i, :]

                def step(instruction):
                    instruction.then_inc(dve_own, count.one(dve_own))
                    dve.wait_ge(dve_own, count.sent[dve_own])

                if i == 0:
                    c = [slice(PCOL[name], PCOL[name] + KT) for name in ("final_norm_g", "mix_norm_2")]
                    step(mul(both_g[:], par[:, c[0]], par[:, c[1]]))
                    dve.wait_ge(got_rope, 16)
                    step(dve.tensor_copy(rope_a[:], rope_i[:]))
                    step(mul(rope_a[:], rope_a[:], inv_freq.broadcast_to([P, T])))
                step(dve.tensor_scalar(rope_n[:], rope_a[:], shift, 1.0 / two_pi, ALU.add, ALU.mult))
                step(dve.tensor_scalar(rope_n[:], rope_n[:], magic, None, ALU.add))
                step(dve.tensor_scalar(rope_n[:], rope_n[:], magic, None, ALU.subtract))
                step(fused(r, rope_n[:], -c1, rope_a[:], ALU.mult, ALU.add))
                step(fused(r, rope_n[:], -c2, r, ALU.mult, ALU.add))
                step(fused(r, rope_n[:], -c3, r, ALU.mult, ALU.add))
                if shift:
                    step(dve.tensor_scalar(r, r, shift, None, ALU.add))
                limit = float(np.nextafter(np.float32(math.pi), np.float32(0)))
                step(dve.tensor_scalar(r, r, limit, -limit, ALU.min, ALU.max))
                if shift:
                    dve.tensor_copy(rope_n[:, 0:1], r[:, 0:1]).then_inc(angles_done, 1)

            def gated_hid(j, jm):
                dve.wait_ge(act_done, count.next(act_done))
                dve.wait_ge(evicted, j + (FIRST_OUT["up0"] + 1))
                mul(hid[:, jm % U, :], gate_act[:, jm % U, :], up_z[:, jm % U, :]).then_inc(hid_done, count.one(hid_done))

            def gated_body(j, jm):
                early = isinstance(j, int)
                if early and j == 0:
                    token_norm()
                z = bank_of("up0", j, jm)
                mul(gate_z[:, jm, :], z[:, 0, :], rstd[:]).then_inc(gate_done, 1)
                mul(up_z[:, jm, :], z[:, 1, :], rstd[:]).then_inc(evicted, count.one(evicted))
                if not early or j >= 1:
                    gated_hid(j - 1, jm + 2)
                if not early or j >= 2:
                    hidden_lo(j - 2, jm + 1, hid)
                ahead("up0", j, jm)

            count.each(FT, gated_body)
            gated_hid(FT - 1, (FT - 1) % U)
            hidden_lo(FT - 2, (FT - 2) % U, hid)
            hidden_lo(FT - 1, (FT - 1) % U, hid)
            down(0, rope_angles)
            prep(A, both_g)
            ahead("down0", FT // 2 - 1, (FT // 2 - 1) % U)

            def hy_evict(j, split=True):
                evict("hy_in", j, j % U, hy[:, 2 * j:2 * j + 2, :], scale=rstd_mem, split=split)

            dve.memset(hy_conv_in[:, :, 0:2], 0.0).then_inc(dve_own, count.one(dve_own))
            ahead("hy_in", 0, 0)
            token_norm()
            ahead("hy_in", 1, 1)
            dve.wait_ge(full_dve, count.next(full_dve))
            fused(mean_sq[:, 0:T], D[STAT][:, 0:T], 1.0 / DM, rstd[:], ALU.mult, ALU.mult).then_inc(dve_own, count.one(dve_own))
            dve.wait_ge(dve_own, count.sent[dve_own])
            mul(mean_sq[:, 0:T], mean_sq[:, 0:T], rstd[:]).then_inc(dve_own, count.one(dve_own))
            dve.wait_ge(dve_own, count.sent[dve_own])
            dve.tensor_scalar(mean_sq[:, 0:T], mean_sq[:, 0:T], EPS, None, ALU.add).then_inc(mean_done, count.one(mean_done))
            refine(rstd_mem)
            mul(rstd_mem[:], rstd_mem[:], rstd[:]).then_inc(dve_own, count.one(dve_own))
            dve.wait_ge(dve_own, count.sent[dve_own])
            tiles_of = (slice(0, 2), slice(2, 4), slice(4, 5))
            for i in range(3):
                hy_evict(i, split=i == 2)
                dve.wait_ge(evicted, count.sent[evicted])
                for f in range(tiles_of[i].start, tiles_of[i].stop):
                    gain = pcol("hy_k_norm_2" if f == 4 else "hy_q_norm_2")
                    last = dve.tensor_scalar(hy_qk[:, f, :], hy[:, f, :], gain, None, ALU.mult)
                    if f + 1 < tiles_of[i].stop:
                        last.then_inc(dve_own, count.one(dve_own))
                last.then_inc(qk_gained, count.one(qk_gained))
            hy_evict(3)
            stats = ((mean_sq, rough), (sq[:, 0, :], sq[:, 1, :]), (hy_mean, hy_rough))
            for i in range(3):
                mean(i, 64, (2, 2, 1)[i] * T, stats[i][0])
            dve.wait_ge(rope_done, 1)
            dve.wait_ge(dve_own, count.sent[dve_own])
            dve.wait_ge(qk_gained, count.sent[qk_gained])
            mul(hy_cos[:], hy_qk[:], over(cos_t[:], 5)).then_inc(dve_own, count.one(dve_own))
            for i in range(3):
                tiles = tiles_of[i]
                dve.wait_ge(full_dve, count.next(full_dve))
                n = tiles.stop - tiles.start
                mul(hy_rot[:, tiles, :], as_tiles(D[(3, STAT, 0)[i]][:, 0:n * T]), over(sin_t[:], n)).then_inc(drained_dve, count.one(drained_dve))
            dve.wait_ge(dve_own, count.sent[dve_own])
            dve.wait_ge(drained_dve, count.sent[drained_dve])
            add(hy_qk[:], hy_cos[:], hy_rot[:]).then_inc(dve_own, count.one(dve_own))
            hy_evict(4)
            for i in (2, 0, 1):
                (m, rr), tiles = stats[i], hy_qk[:, tiles_of[i], :]
                width = (2, 2, 1)[i] * T
                refine(m, width, m, rr)
                mul(tiles, tiles, as_tiles(m[:, 0:width])).then_inc(qk_rotated, count.one(qk_rotated))
            hy_evict(5)
            hy_evict(6)
            for t, cols in score_tiles(hy_scores, lambda maps, c: over(window[:, c], len(maps))):
                dve.tensor_reduce(row_max[:, t, :], hy_scores[:, :, cols], AX_X, ALU.max).then_inc(dve_own, count.one(dve_own))
                dve.wait_ge(dve_own, count.sent[dve_own])
                dve.tensor_tensor(row_max[:, t, :], row_max[:, t, :], sinks[:], ALU.max).then_inc(dve_own, count.one(dve_own))
                dve.wait_ge(dve_own, count.sent[dve_own])
                dve.tensor_scalar(neg_max[:, t, :], row_max[:, t, :], -1.0, None, ALU.mult).then_inc(dve_own, count.one(dve_own))
                sub(hy_sink[:, t, :], sinks[:], row_max[:, t, :]).then_inc(max_done, 1)
            for t, cols, width in ((1, TILE1, 2 * P), (0, TILE0, P)):
                dve.wait_ge(sink_done, count.next(sink_done))
                dve.wait_ge(exp_done, count.next(exp_done))
                add(row_sum[:, t, :], row_sum[:, t, :], hy_sink[:, t, :]).then_inc(dve_own, count.one(dve_own))
                dve.wait_ge(dve_own, count.sent[dve_own])
                dve.reciprocal(row_rec[:, t, :], row_sum[:, t, :]).then_inc(dve_own, count.one(dve_own))
                dve.wait_ge(dve_own, count.sent[dve_own])
                last = normalise(hy_scores, t, cols, width)
                if t == 1:
                    last.then_inc(dve_own, count.one(dve_own))
                else:
                    last.then_inc(probs_done, 1)
            hy_evict(7)
            hy_evict(8, split=False)
            dve.wait_ge(evicted, count.sent[evicted])
            mul(hy_conv_in[:, :, 2:2 + T], hy[:, 10:14, :], hy[:, 14:18, :]).then_inc(dve_own, count.one(dve_own))
            dve.wait_ge(dve_own, count.sent[dve_own])
            for tap in range(3):
                for f in range(4):
                    w = pcol("hy_conv_w_2", tap * 4 + f)
                    src = hy_conv_in[:, f, tap:tap + T]
                    if tap == 0:
                        dve.tensor_scalar(hy_conv[:, f, :], src, w, None, ALU.mult).then_inc(dve_own, count.one(dve_own))
                    else:
                        fused(hy_conv[:, f, :], src, w, hy_conv[:, f, :], ALU.mult, ALU.add).then_inc(dve_own, count.one(dve_own))
                if tap == 1:
                    lo_parts(B, 0, [hy_att[:, f, :] for f in range(2)])
                dve.wait_ge(dve_own, count.sent[dve_own])
            for i in range(2):
                tiles = hy_conv[:, 2 * i:2 * i + 2, :]
                mul(tiles, tiles, hy[:, 6 + 2 * i:8 + 2 * i, :]).then_inc(mixed_ready, count.one(mixed_ready))
                if i == 0:
                    lo_parts(B, 2, [hy_att[:, 2 + f, :] for f in range(2)])
            dve.wait_ge(mixed_ready, count.sent[mixed_ready])
            lo_parts(B, 4, [hy_conv[:, f, :] for f in range(4)])
            ahead("hy_in", 8, 8 % U)
            for f in range(KT):
                fused(x[:, f, :], x[:, f, :], pcol("final_norm_g", f), rstd[:], ALU.mult, ALU.mult).then_inc(dve_own, count.one(dve_own))
            dve.wait_ge(dve_own, count.sent[dve_own])
            residual("hy_out", A, "ffn_norm_2")

            def conv_ffn(layer, ple_moving):
                name = f"up{layer}"

                def tap_column(tap, f, j):
                    return par[:, bass.ds(j + (CONV_COL + ((layer - 1) * 3 + tap) * 2 * FT + f * FT), 1)]

                def taps(j, jm):
                    m = jm % U
                    dve.wait_ge(tap_done, count.next(tap_done))
                    dve.wait_ge(evicted, j + (FIRST_OUT[name] + 1))
                    for f in range(2):
                        o = conv_out[:, m, f, :]
                        fused(o, conv_in[:, m, f, 1:1 + T], tap_column(1, f, j), o, ALU.mult, ALU.add).then_inc(dve_own, count.one(dve_own))
                    dve.wait_ge(dve_own, count.sent[dve_own])
                    for f in range(2):
                        o = conv_out[:, m, f, :]
                        last = fused(o, conv_in[:, m, f, 0:T], tap_column(0, f, j), o, ALU.mult, ALU.add)
                        if f == 0:
                            last.then_inc(conv_done, 1)
                        else:
                            last.then_inc(dve_own, count.one(dve_own))

                def conv_hidden(j, jm):
                    dve.wait_ge(act_done, count.next(act_done))
                    dve.wait_ge(dve_own, count.sent[dve_own])
                    mul(conv_hid[:, jm % U, :], conv_gelu[:, jm % U, :], conv_out[:, jm % U, 1, :]).then_inc(hid_done, count.one(hid_done))

                def body(j, jm):
                    early = isinstance(j, int)
                    if early and j == 0:
                        token_norm()
                    mul(conv_in[:, jm, :, 2:2 + T], bank_of(name, j, jm), over(rstd[:], 2)).then_inc(evicted, count.one(evicted))
                    if not early or j >= 2:
                        conv_hidden(j - 2, jm + 1)
                    if not early or j >= 3:
                        hidden_lo(j - 3, jm, conv_hid)
                    if not early or j >= 1:
                        taps(j - 1, jm + 2)
                    ahead(name, j, jm)

                dve.memset(conv_in[:, :, :, 0:2], 0.0).then_inc(dve_own, count.one(dve_own))
                dve.wait_ge(got_conv, 16)
                count.each(FT, body, 4)
                m = FT % U
                conv_hidden(FT - 2, m + 1)
                hidden_lo(FT - 3, m, conv_hid)
                taps(FT - 1, m + 2)
                ahead(f"down{layer}", 0, 0)
                conv_hidden(FT - 1, m + 2)
                hidden_lo(FT - 2, m + 1, conv_hid)
                hidden_lo(FT - 1, m + 2, conv_hid)
                dve.wait_ge(p_hi_done, count.next(p_hi_done))
                sub(flat(p_lo), flat(p_in), flat(p_hi).bitcast(F32)).then_inc(p_split, 1)
                down(layer, first=1)
                ahead(f"down{layer}", FT // 2 - 1, (FT // 2 - 1) % U)
                prep(ple_moving, "ple_norm_2", (layer - 1) * KT)
                gate = f"gate{layer}"
                ahead(f"proj{layer}", 0, 0)

                def finish(j):
                    dve.wait_ge(act_done, count.next(act_done))
                    m, pair = ple_mul[:, j % 2, :, :], x[:, 2 * j:2 * j + 2, :]
                    mul(m, ple_sig[:, j % 2, :, :], as_tiles(D[j][:])).then_inc(drained_dve, count.one(drained_dve))
                    dve.wait_ge(drained_dve, count.sent[drained_dve])
                    add(pair, pair, m).then_inc(x_gated, count.one(x_gated))

                for j in range(COUNT[gate]):
                    if j == 0:
                        ahead(gate, 0, 0)
                        token_norm()
                    evict(gate, j, j % U, ple_z[:, j % 2, :, :], split=False)
                    finish(j)
                    if 0 < j < 3:
                        ahead(gate, j, j % U)
                    if layer == 1:
                        dve.wait_ge(x_gated, count.sent[x_gated])
                        prep_pair(A, "mix_norm_2", KT, x, j)
                ahead(gate, 3, 0)

            conv_ffn(1, B)

            def gla_evict(j, split=True):
                if j == 0:
                    token_norm()
                if j < 2:
                    fused(gla[:, 2 * j:2 * j + 2, :], bank_of("gla_in", j, j % U), float(P) ** -0.5, over(rstd[:], 2),
                                    ALU.mult, ALU.mult).then_inc(evicted, count.one(evicted))
                    ahead("gla_in", j, j % U)
                elif 4 <= j < 8:
                    evict_tokens("gla_in", j, gla_v[:, :, (j - 4) * 2 * P:(j - 3) * 2 * P], rstd_tok)
                else:
                    evict("gla_in", j, j % U, gla[:, 2 * j:2 * j + 2, :], split=split)

            sums = flat(gla_g)

            def blocks(ap, level):
                return flat(ap).rearrange("p (b h t) -> p b h t", h=2, t=level)

            def exponents(i):
                e = (gla_e, gla_z)[i % 2]
                if i <= len(LEVELS):
                    level = LEVELS[i - 1]
                    s, to = blocks(gla_g, level), blocks(e, level)
                    n = 4 * T // (2 * level)
                    middle = s[:, :, 0, level - 1:level].broadcast_to([P, n, level])
                    if level == 64:
                        dve.tensor_copy(to[:, :, 1, :], s[:, :, 1, :]).then_inc(dve_own, count.one(dve_own))
                    else:
                        sub(to[:, :, 1, :], s[:, :, 1, :], middle).then_inc(dve_own, count.one(dve_own))
                    sub(to[:, :, 0, :], middle, s[:, :, 0, :]).then_inc(decay_done, 1)
                    return
                s4 = gla_g[:].rearrange("p h (c t) -> p h c t", t=64)
                e4 = e[:].rearrange("p h (c t) -> p h c t", t=64)
                for c in range(2):
                    sub(e4[:, :, c, :], s4[:, :, c, 63:64].broadcast_to([P, 4, 64]), s4[:, :, c, :]).then_inc(dve_own, count.one(dve_own))
                dve.wait_ge(dve_own, count.sent[dve_own])
                add(e4[:, :, 0, :], e4[:, :, 0, :], s4[:, :, 1, 63:64].broadcast_to([P, 4, 64])).then_inc(dve_own, count.one(dve_own))
                dve.tensor_copy(e4[:, :, 2, :], s4[:, :, 2, :]).then_inc(dve_own, count.one(dve_own))
                add(e4[:, :, 3, :], s4[:, :, 3, :], s4[:, :, 2, 63:64].broadcast_to([P, 4, 64])).then_inc(decay_done, 1)

            def decayed(i):
                e = (gla_e, gla_z)[i % 2]
                dve.wait_ge(expo_done, count.next(expo_done))
                level = LEVELS[i - 1] if i <= len(LEVELS) else P
                to, ev = blocks(gla_w[i % 2], level), blocks(e, level)
                q, k = (flat(gla[:, f:f + 4, :]).rearrange("p (b h t) -> p b h t", h=2, t=level) for f in (0, 4))
                mul(to[:, :, 0, :], k[:, :, 0, :], ev[:, :, 0, :]).then_inc(dve_own, count.one(dve_own))
                mul(to[:, :, 1, :], q[:, :, 1, :], ev[:, :, 1, :]).then_inc(level_ready, count.one(level_ready))

            def keep_level(i):
                dve.wait_ge(drained_dve, count.sent[drained_dve])
                for t in range(TT):
                    dve.wait_ge(full_dve, count.next(full_dve))
                    to, keep, found = gla_s[:, t, :, :], over(level_mask[:, i, :], 4), as_tiles(D[(2 * i + t) % 4][:], P)
                    if i > 0:
                        n = LEVELS[i - 1]
                        to = to.rearrange("p h (b x t) -> p h b x t", x=2, t=n)[:, :, :, 1, :]
                        keep = right_halves(level_mask[:, i, :], n).unsqueeze(1).broadcast_to([P, 4, P // (2 * n), n])
                        found = D[(2 * i + t) % 4][:, 0:2 * P].rearrange("p (h b t) -> p h b t", h=4, t=n)
                    dve.copy_predicated(to, keep, found).then_inc(drained_dve, count.one(drained_dve))

            dve.wait_ge(lr_hi_done, count.next(lr_hi_done))
            sub(flat(gla_wlr_lo), flat(gla_wlr), flat(gla_wlr_hi).bitcast(F32)).then_inc(lr_split, 1)
            gla_evict(0)
            dve.wait_ge(full_dve, count.next(full_dve))
            mul(gla_lr[0:16, :], D[0][0:16, 0:T], rstd[0:16, :]).then_inc(lr_ready, 1)
            gla_evict(1)
            dve.tensor_copy(flat(level_mask), level_mask_f[:]).then_inc(dve_own, count.one(dve_own))
            for b in range(2):
                dve.wait_ge(full_dve, count.next(full_dve))
                for f in range(2):
                    h = 2 * b + f
                    last = dve.tensor_scalar(gla_z[:, h, :], D[1 + b][:, f * T:(f + 1) * T], pcol("gla_gate_bias_2", h), None, ALU.add)
                    if f == 0:
                        last.then_inc(dve_own, count.one(dve_own))
                last.then_inc(drained_dve, count.one(drained_dve))
            dve.wait_ge(dve_own, count.sent[dve_own])
            dve.wait_ge(drained_dve, count.sent[drained_dve])
            fused(flat(gla_e), flat(gla_z), -1.0, flat(gla_z), ALU.mult, ALU.min).then_inc(logit_done, 1)
            gla_evict(2)
            dve.wait_ge(soft_done, count.next(soft_done))
            fused(flat(gla_z), flat(gla_z), 0.0, flat(gla_e), ALU.min, ALU.subtract).then_inc(dve_own, count.one(dve_own))
            dve.wait_ge(dve_own, count.sent[dve_own])
            dve.wait_ge(cleared, 1)
            dve.tensor_tensor_scan(sums, restart, flat(gla_z), 0.0, ALU.mult, ALU.add).then_inc(dve_own, count.one(dve_own))
            dve.wait_ge(dve_own, count.sent[dve_own])
            exponents(1)
            turned_scale(rstd_tok)
            gla_evict(3, split=False)
            dve.wait_ge(evicted, count.sent[evicted])
            evictions = {1: 4, 2: 5, 3: 6, 5: 7, 7: 8}
            for i in range(1, len(LEVELS) + 1):
                if i > 1:
                    dve.wait_ge(level_ready, count.sent[level_ready])
                exponents(i + 1)
                decayed(i)
                if i == 1:
                    ahead("gla_in", 3, 0)
                keep_level(i - 1)
                if i in evictions:
                    gla_evict(evictions[i])
            decayed(len(LEVELS) + 1)
            keep_level(len(LEVELS))
            gla_evict(9, split=False)
            dve.wait_ge(full_dve, count.next(full_dve))
            dve.tensor_copy(gla_s[:, 2, :, :], as_tiles(D[0][:], P)).then_inc(gla_scores_done, 1)
            ahead("gla_in", 9, 9 % U)
            def gate_head(h):
                if h != 1:
                    dve.wait_ge(silu_done, count.next(silu_done))
                dve.wait_ge(o_squared, count.next(o_squared))
                gate = gla[:, 16 + 2 * h:18 + 2 * h, :]
                mul(gate, gate, gla_o[:, 2 * h:2 * h + 2, :]).then_inc(dve_own, count.one(dve_own))
                dve.wait_ge(dve_own, count.sent[dve_own])

            def scale_head(h):
                scale = (mean_sq[:], sq[:, 0, :])[h // 2][:, (h % 2) * T:(h % 2 + 1) * T]
                mul(gla_o[:, 2 * h:2 * h + 2, :], gla[:, 16 + 2 * h:18 + 2 * h, :], over(scale, 2)).then_inc(mixed_ready, count.one(mixed_ready))

            def split_head(h):
                lo_parts(B, 2 * h, [gla_o[:, 2 * h + f, :] for f in range(2)], [pcol("gla_o_norm_2", f) for f in range(2)])

            gate_head(0)
            gate_head(1)
            mean(0, 2 * P, 2 * T)
            mean(1, 2 * P, 2 * T, sq[:, 0, :])
            refine(mean_sq, 2 * T)
            scale_head(0)
            scale_head(1)
            dve.wait_ge(mixed_ready, count.sent[mixed_ready])
            refine(sq[:, 0, :], 2 * T, sq[:, 0, :], sq[:, 1, :])
            gla_evict(10, split=False)
            split_head(0)
            split_head(1)
            ahead("gla_in", 10, 10 % U)
            gate_head(2)
            scale_head(2)
            gla_evict(11, split=False)
            dve.wait_ge(mixed_ready, count.sent[mixed_ready])
            split_head(2)
            gate_head(3)
            scale_head(3)
            dve.wait_ge(mixed_ready, count.sent[mixed_ready])
            split_head(3)
            ahead("gla_in", 11, 11 % U)
            residual("gla_out", A, "ffn_norm_2", KT)
            conv_ffn(2, B)

        @block.gpsimd
        def _(pool):
            count = Counts(pool)

            def split_lo(c, slot):
                if isinstance(c, int) and c >= CHUNKS:
                    return
                pool.wait_ge(hi_done, c + 1)
                cols = slice(DVE_COLS, CHUNK)
                pool.tensor_tensor(w_lo[:, slot, cols], raw[:, slot, cols], w_hi[:, slot, cols].bitcast(F32), ALU.subtract).then_inc(lo_pool, 1)

            def ahead(name, j, jm):
                split_lo(j + (FIRST[name] + AHEAD), (FIRST[name] + jm + AHEAD) % U)

            def add_squares(i, sums=sq_sum, ring=sq):
                pool.wait_ge(sq_done, count.next(sq_done))
                if i == 0:
                    return
                if i > 1:
                    pool.wait_ge(sq_added, count.sent[sq_added])
                total = pool.tensor_tensor(sums[:], sums[:], ring[:, i % 2, :], ALU.add)
                if i == 3:
                    total.then_inc(sq_total, 1)
                else:
                    total.then_inc(sq_added, count.one(sq_added))

            def all_squares(sums=sq_sum, ring=sq):
                for i in range(KT // 2):
                    add_squares(i, sums, ring)

            def residual(name):
                for j in range(COUNT[name]):
                    ahead(name, j, j % U)
                    add_squares(j)

            def stream(name):
                count.each(COUNT[name], lambda j, jm: ahead(name, j, jm))

            pool.memset(table[N_BUCKETS:N_BUCKETS + 1, :], MASKED).then_inc(masked_row, count.one(masked_row))
            pool.wait_ge(masked_row, count.sent[masked_row])
            split_lo(0, 0)
            all_squares()
            split_lo(1, 1)

            for j in range(W_IN_Q):
                ahead("w_in", j, j % U)
                if j == 3:
                    all_squares()
            for j in range(W_IN_Q, COUNT["w_in"]):
                ahead("w_in", j, j % U)
            stream("w_ck")
            residual("w_out")
            stream("w_cq")
            stream("w_cv")
            residual("w_co")
            stream("up0")
            stream("down0")
            all_squares()
            all_squares(gain_sq_sum, gain_sq)
            stream("hy_in")
            residual("hy_out")
            for layer in (1, 2):
                stream(f"up{layer}")
                stream(f"down{layer}")
                all_squares()
                stream(f"proj{layer}")
                for j in range(COUNT[f"gate{layer}"]):
                    if layer == 1 and j >= 1:
                        add_squares(j - 1)
                    if layer == 1 and j == 3:
                        add_squares(3)
                    ahead(f"gate{layer}", j, j % U)
                if layer == 1:
                    pool.memset(gla_s[:], 0.0)
                    pool.memset(restart, 1.0).then_inc(pool_own, 1)
                    pool.wait_ge(pool_own, 1)
                    pool.memset(restart[:, 0::64], 0.0).then_inc(cleared, 1)
                    stream("gla_in")
                    residual("gla_out")


def constants():
    c = np.zeros((P, N_CONST), np.float32)
    i = np.arange(P)
    c[i, C_IDENT + i] = 1.0
    c[:, C_ONES:C_ONES + P] = 1.0
    c[:, C_HALF:C_HALF + P] = (i[:, None] // 64 == i[None, :] // 64)
    low = i[i % 64 < 32]
    c[low + 32, C_ROT + low] = -1.0
    c[low, C_ROT + low + 32] = 1.0
    c[(i + 64) % P, C_SWAP + i] = 1.0
    dist = P + i[:, None] - np.arange(2 * P)[None, :]
    c[:, C_WIN:C_WIN + 2 * P] = np.where((dist >= 0) & (dist < P), 0.0, MASKED)
    exponent = -np.arange(0, 64, 2, dtype=np.float32) / np.float32(64)
    c[:, C_FREQ] = np.power(np.float32(10000.0), exponent)[i % 32]
    dist = N_DIST - P - 1 - np.arange(N_DIST)
    exact = N_BUCKETS // 2
    ratio = np.log(np.maximum(dist, exact).astype(np.float32) / np.float32(exact)) / np.float32(math.log(P / exact))
    large = np.minimum(exact + (ratio * np.float32(N_BUCKETS - exact)).astype(np.int32), N_BUCKETS - 1)
    bucket = np.where(dist < 0, N_BUCKETS, np.where(dist < exact, dist, large))
    onehot = np.zeros((N_BUCKETS + 1, N_DIST), np.float32)
    onehot[bucket, np.arange(N_DIST)] = 1.0
    s, t = i[:, None], i[None, :]
    masks = [s == t] + [(s // (2 * n) == t // (2 * n)) & (s % (2 * n) < n) & (t % (2 * n) >= n) for n in LEVELS]
    return {"const": c, "onehot": onehot, "level_mask": np.concatenate(masks, axis=1).astype(np.float32)}


def layout(inputs):
    a = {name: np.asarray(v) for name, v in inputs.items()}

    def features_first(v):
        return v.T.reshape(-1, P, v.shape[0]).transpose(1, 0, 2)

    def over_outputs(w):
        return w.reshape(KT, P, -1, 2 * P).transpose(2, 1, 0, 3).reshape(-1, P, CHUNK)

    def gate_and_up(gate, up):
        both = np.stack([gate.reshape(KT, P, FT, P), up.reshape(KT, P, FT, P)], axis=3)
        return both.transpose(2, 1, 0, 3, 4).reshape(-1, P, CHUNK)

    def over_k(w):
        return w.reshape(-1, 2, P, DM).transpose(0, 2, 1, 3).reshape(-1, P, CHUNK)

    up2, gla_w = a["ffn_w_up_2"], a["gla_w_in_2"][0]
    low_rank = 2 * DM
    weights = {
        "w_in": over_outputs(a["w_in"][0]), "w_ck": over_outputs(a["w_ck"][0]), "w_cv": over_outputs(a["w_cv"][0]),
        "w_out": over_outputs(a["w_out"][0]), "w_cq": over_outputs(a["w_cq"][0]), "w_co": over_outputs(a["w_co"][0]),
        "up0": gate_and_up(a["w_gate"][0], a["w_up"][0]), "down0": over_k(a["w_down"][0]),
        "hy_in": over_outputs(a["hy_w_in_2"][0]), "hy_out": over_outputs(a["hy_w_out_2"][0]),
        "gla_in": over_outputs(np.concatenate([gla_w[:, :low_rank], gla_w[:, low_rank + 16:]], axis=1)),
        "gla_out": over_outputs(a["gla_w_out_2"][0])}
    for i in range(2):
        weights[f"up{i + 1}"] = gate_and_up(up2[i][:, :FF], up2[i][:, FF:])
        weights[f"down{i + 1}"] = over_k(a["ffn_w_down_2"][i])
        weights[f"proj{i + 1}"] = over_k(a["ple_w_proj_2"][i])
        weights[f"gate{i + 1}"] = over_outputs(a["ple_w_gate_2"][i])
    twice = ("hy_q_norm_2", "hy_k_norm_2")
    vectors = [np.concatenate([a[name].reshape(-1)] * (2 if name in twice else 1)).reshape(-1, P) for name, _ in PARAMS]
    vectors += [a["ffn_conv_w_2"].reshape(-1, P), a["ffn_conv_b_2"].reshape(-1, P)]
    moved = {
        "weights": np.concatenate([weights[name] for name, _, _ in PHASES]),
        "par": np.concatenate(vectors).T, "x_t": features_first(a["x"][0]), "mem_t": features_first(a["mem"][0]),
        "p_t": np.stack([features_first(v[0]) for v in a["p_2"]]),
        "gla_w_lr": gla_w[:, low_rank:low_rank + 16].reshape(KT, P, 16).transpose(1, 0, 2)}
    for name in ("rel_bias_table", "diff_lambda", "hy_sinks_2", "positions_2", "gla_w_gate_up_2"):
        moved[name] = a[name]
    return {name: np.ascontiguousarray(v) for name, v in moved.items()}


def kernel(**inputs):
    import concourse.bacc as bacc
    from concourse.bass_utils import run_bass_kernel_spmd

    arrays = layout(inputs)
    arrays.update(constants())
    nc = bacc.Bacc("TRN2", target_bir_lowering=False, num_devices=1)
    io = {name: nc.dram_tensor(name, a.shape, mybir.dt.from_np(a.dtype), kind="ExternalInput").ap() for name, a in arrays.items()}
    out = nc.dram_tensor("out", (P, KT, T), F32, kind="ExternalOutput").ap()
    program(nc, io, out)
    r = run_bass_kernel_spmd(nc, [arrays], core_ids=[0])
    return r.results[0]["out"].transpose(2, 1, 0).reshape(1, T, DM)
```
